# Optimizing a Trainium2 kernel written in Bass

```python
import jax, jax.numpy as jnp
from jax import lax
import numpy as np

D_MODEL = 1024
BATCH = 1
SEQ = 256
DEPTH = 2

CHUNK = 64
N_MIXERS = 2
GLA_HEADS = 4
GLA_DK = D_MODEL // 2
GLA_DV = D_MODEL
GLA_DK_HEAD = GLA_DK // GLA_HEADS
GLA_DV_HEAD = GLA_DV // GLA_HEADS
GLA_GATE_RANK = 16
GLA_GATE_TAU = 16.0
GLA_IN_WIDTH = 2 * GLA_DK + 2 * GLA_DV + GLA_GATE_RANK
ATT_HEADS = 16
ATT_HEAD_DIM = D_MODEL // ATT_HEADS
LEFT_CHUNKS = 8
BAND = (LEFT_CHUNKS + 1) * CHUNK
MAX_REL = 128
N_REL = 2 * MAX_REL + 1
D_FF = 4 * D_MODEL
DEEPNORM_ALPHA = (2.0 * DEPTH) ** 0.25
DEEPNORM_BETA = (8.0 * DEPTH) ** -0.25
LN_EPS = 1e-5
RMS_EPS = 1e-6
NEG_INF = -1e30
N_GLA_LAYERS = (DEPTH + 1) // 2
N_ATT_LAYERS = DEPTH // 2


def layer_norm(x, g, b):
    xf = x.astype(jnp.float32)
    mu = jnp.mean(xf, -1, keepdims=True)
    var = jnp.mean(jnp.square(xf - mu), -1, keepdims=True)
    return ((xf - mu) * lax.rsqrt(var + LN_EPS)).astype(x.dtype) * g + b

def gla_mixer(u, w_in, w_gk2, b_gk, g_norm, w_out):
    B_, S_, _ = u.shape
    nC = S_ // CHUNK
    proj = u @ w_in
    q, k, v, g, gk_lr = jnp.split(
        proj, [GLA_DK, 2 * GLA_DK, 2 * GLA_DK + GLA_DV, 2 * GLA_DK + 2 * GLA_DV], axis=-1)
    log_a = jax.nn.log_sigmoid((gk_lr @ w_gk2 + b_gk).astype(jnp.float32)) / GLA_GATE_TAU

    def to_chunks(t, hd):
        return t.reshape(B_, nC, CHUNK, GLA_HEADS, hd).transpose(0, 3, 1, 2, 4)

    qc = to_chunks(q.astype(jnp.float32), GLA_DK_HEAD) * (GLA_DK_HEAD ** -0.5)
    kc = to_chunks(k.astype(jnp.float32), GLA_DK_HEAD)
    vc = to_chunks(v.astype(jnp.float32), GLA_DV_HEAD)
    cum = jnp.cumsum(to_chunks(log_a, GLA_DK_HEAD), axis=3)
    e_pos = jnp.exp(cum)
    e_neg = jnp.exp(-cum)
    q_fwd = qc * e_pos
    a_fwd = jnp.einsum('bhntd,bhnsd->bhnts', q_fwd, kc * e_neg)
    a_bwd = jnp.einsum('bhntd,bhnsd->bhnts', qc * e_neg, kc * e_pos)
    lower = jnp.tril(jnp.ones((CHUNK, CHUNK), dtype=bool))
    o_intra = jnp.einsum('bhnts,bhnsv->bhntv', jnp.where(lower, a_fwd, a_bwd), vc)
    k_to_end = kc * jnp.exp(cum[:, :, :, -1:, :] - cum)
    chunk_decay = jnp.exp(cum[:, :, :, -1, :])

    def step(state, inp):
        qs, ke, vv, dec = inp
        o = jnp.einsum('bhtk,bhkv->bhtv', qs, state)
        state = state * dec[..., None] + jnp.einsum('bhtk,bhtv->bhkv', ke, vv)
        return state, o

    s0 = jnp.zeros((B_, GLA_HEADS, GLA_DK_HEAD, GLA_DV_HEAD), jnp.float32)
    _, o_inter = lax.scan(step, s0, (jnp.moveaxis(q_fwd, 2, 0), jnp.moveaxis(k_to_end, 2, 0),
                                     jnp.moveaxis(vc, 2, 0), jnp.moveaxis(chunk_decay, 2, 0)))
    o = o_intra + jnp.moveaxis(o_inter, 0, 2)
    o = o * lax.rsqrt(jnp.mean(jnp.square(o), -1, keepdims=True) + RMS_EPS)
    o = o * g_norm.astype(jnp.float32)[None, :, None, None, :]
    o = o.transpose(0, 2, 3, 1, 4).reshape(B_, S_, GLA_DV).astype(u.dtype)
    return (o * jax.nn.silu(g)) @ w_out

def chunk_attention(u, w_in, b_in, rel_bias, w_out):
    B_, S_, _ = u.shape
    nC = S_ // CHUNK
    q, k, v = jnp.split(u @ w_in + b_in, 3, axis=-1)

    def heads(t):
        return t.reshape(B_, S_, ATT_HEADS, ATT_HEAD_DIM).transpose(0, 2, 1, 3)

    pad = LEFT_CHUNKS * CHUNK
    qc = (heads(q) * (ATT_HEAD_DIM ** -0.5)).reshape(B_, ATT_HEADS, nC, CHUNK, ATT_HEAD_DIM)
    kp = jnp.pad(heads(k), ((0, 0), (0, 0), (pad, 0), (0, 0)))
    vp = jnp.pad(heads(v), ((0, 0), (0, 0), (pad, 0), (0, 0)))
    key_valid = jnp.arange(S_ + pad) >= pad
    rel = jnp.clip(pad + jnp.arange(CHUNK)[:, None] - jnp.arange(BAND)[None, :], -MAX_REL, MAX_REL) + MAX_REL
    bias = rel_bias.astype(jnp.float32)[:, rel]

    def one_chunk(inp):
        qi, start = inp
        kb = lax.dynamic_slice_in_dim(kp, start, BAND, axis=2)
        vb = lax.dynamic_slice_in_dim(vp, start, BAND, axis=2)
        mb = lax.dynamic_slice_in_dim(key_valid, start, BAND)
        s = jnp.einsum('bhtd,bhjd->bhtj', qi, kb).astype(jnp.float32) + bias
        p = jax.nn.softmax(jnp.where(mb, s, NEG_INF), axis=-1).astype(vb.dtype)
        return jnp.einsum('bhtj,bhjd->bhtd', p, vb)

    o = lax.map(one_chunk, (jnp.moveaxis(qc, 2, 0), jnp.arange(nC) * CHUNK))
    o = o.transpose(1, 0, 3, 2, 4).reshape(B_, S_, D_MODEL)
    return o @ w_out

def squared_relu_mlp(u, w1, w2):
    return jnp.square(jax.nn.relu(u @ w1)) @ w2

def first_inputs(seed: int = 0) -> dict:
    key = jax.random.key(seed)
    ks = jax.random.split(key, 16)
    nrm = lambda k, shape, s: jax.random.normal(k, shape, jnp.float32) * s
    D = D_MODEL
    return {
        "x": nrm(ks[0], (BATCH, SEQ, D), 1.0),
        "c": nrm(ks[1], (BATCH, D), 1.0),
        "w_ada": nrm(ks[2], (DEPTH, D, 6 * D), 0.1 * D ** -0.5),
        "b_ada": nrm(ks[3], (DEPTH, 6 * D), 0.02),
        "ln_g": 1.0 + nrm(ks[4], (DEPTH, 2, D), 0.02),
        "ln_b": nrm(ks[5], (DEPTH, 2, D), 0.02),
        "gla_w_in": nrm(ks[6], (N_GLA_LAYERS, D, GLA_IN_WIDTH), D ** -0.5),
        "gla_w_gk2": nrm(ks[7], (N_GLA_LAYERS, GLA_GATE_RANK, GLA_DK), GLA_GATE_RANK ** -0.5),
        "gla_b_gk": nrm(ks[8], (N_GLA_LAYERS, GLA_DK), 0.1),
        "gla_g_norm": 1.0 + nrm(ks[9], (N_GLA_LAYERS, GLA_HEADS, GLA_DV_HEAD), 0.02),
        "gla_w_out": nrm(ks[10], (N_GLA_LAYERS, GLA_DV, D), DEEPNORM_BETA * GLA_DV ** -0.5),
        "att_w_in": nrm(ks[11], (N_ATT_LAYERS, D, 3 * D), D ** -0.5),
        "att_b_in": nrm(ks[12], (N_ATT_LAYERS, 3 * D), 0.02),
        "att_rel_bias": nrm(ks[13], (N_ATT_LAYERS, ATT_HEADS, N_REL), 0.2),
        "att_w_out": nrm(ks[14], (N_ATT_LAYERS, D, D), DEEPNORM_BETA * D ** -0.5),
        "ff_w1": nrm(jax.random.fold_in(ks[15], 0), (DEPTH, D, D_FF), D ** -0.5),
        "ff_w2": nrm(jax.random.fold_in(ks[15], 1), (DEPTH, D_FF, D), DEEPNORM_BETA * D_FF ** -0.5),
    }

def first_block(x, c, w_ada, b_ada, ln_g, ln_b, gla_w_in, gla_w_gk2, gla_b_gk, gla_g_norm, gla_w_out,
              att_w_in, att_b_in, att_rel_bias, att_w_out, ff_w1, ff_w2):
    c_act = jax.nn.silu(c)
    for i in range(DEPTH):
        mods = jnp.split(c_act @ w_ada[i] + b_ada[i], 6, axis=-1)
        sh1, sc1, g1, sh2, sc2, g2 = [m[:, None, :] for m in mods]
        u = x * (1.0 + sc1) + sh1
        j = i // N_MIXERS
        if i % N_MIXERS == 0:
            y = gla_mixer(u, gla_w_in[j], gla_w_gk2[j], gla_b_gk[j], gla_g_norm[j], gla_w_out[j])
        else:
            y = chunk_attention(u, att_w_in[j], att_b_in[j], att_rel_bias[j], att_w_out[j])
        x = layer_norm(DEEPNORM_ALPHA * x + (1.0 + g1) * y, ln_g[i, 0], ln_b[i, 0])
        u = x * (1.0 + sc2) + sh2
        y = squared_relu_mlp(u, ff_w1[i], ff_w2[i])
        x = layer_norm(DEEPNORM_ALPHA * x + (1.0 + g2) * y, ln_g[i, 1], ln_b[i, 1])
    return x


DEPTH_2 = 1

POOL_WIDTH = D_MODEL // 2
POOL_GROUPS = 4
POOL_GROUP_DIM = POOL_WIDTH // POOL_GROUPS
POOL_WINDOWS = (2, 4, 8, 16)
N_HEADS = 8
HEAD_DIM = 64
ATTN_WIDTH = N_HEADS * HEAD_DIM
ROT_DIM = HEAD_DIM // 4
ROPE_THETA = 500000.0
IDX_HEADS = 8
IDX_DIM = 64
TOPK_MAX = 256
Q_BLOCK = 128
N_BRANCH = 2
D_FF_2 = 2816
CONV_WIDTH = 3
EPS = 1e-6
IN_SPLITS = (POOL_WIDTH, ATTN_WIDTH, ATTN_WIDTH, ATTN_WIDTH,
             IDX_HEADS * IDX_DIM, IDX_DIM, IDX_HEADS, N_BRANCH * D_MODEL)
D_IN = POOL_WIDTH + 3 * ATTN_WIDTH + IDX_HEADS * IDX_DIM + IDX_DIM + IDX_HEADS + N_BRANCH * D_MODEL


def rmsnorm(x, g):
    xf = x.astype(jnp.float32)
    y = xf * lax.rsqrt(jnp.mean(xf * xf, axis=-1, keepdims=True) + EPS)
    return (y * g.astype(jnp.float32)).astype(x.dtype)

def rope_partial(x, pos):
    half = ROT_DIM // 2
    inv_freq = 1.0 / (ROPE_THETA ** (jnp.arange(half, dtype=jnp.float32) * 2.0 / ROT_DIM))
    ang = pos[:, None] * inv_freq[None, :]
    cos = jnp.cos(ang)[None, :, None, :]
    sin = jnp.sin(ang)[None, :, None, :]
    xr = x[..., :ROT_DIM].astype(jnp.float32)
    x1, x2 = xr[..., :half], xr[..., half:]
    rot = jnp.concatenate([x1 * cos - x2 * sin, x2 * cos + x1 * sin], axis=-1)
    return jnp.concatenate([rot.astype(x.dtype), x[..., ROT_DIM:]], axis=-1)

def multiscale_pool(u):
    B, S, _ = u.shape
    ug = u.astype(jnp.float32).reshape(B, S, POOL_GROUPS, POOL_GROUP_DIM)
    c0 = jnp.concatenate([jnp.zeros((B, 1, POOL_GROUPS, POOL_GROUP_DIM), jnp.float32),
                          jnp.cumsum(ug, axis=1)], axis=1)
    t = jnp.arange(S)
    outs = []
    for g, w in enumerate(POOL_WINDOWS):
        lo = jnp.maximum(t + 1 - w, 0)
        cg = c0[:, :, g]
        sums = cg[:, 1:] - cg[:, lo]
        cnt = jnp.minimum(t + 1, w).astype(jnp.float32)[None, :, None]
        outs.append(sums / cnt - ug[:, :, g])
    return jnp.stack(outs, axis=2).astype(u.dtype)

def indexed_sparse_attention(q, k, v, iq, ik, iw):
    B, S, H, Dh = q.shape
    k_top = min(TOPK_MAX, S // 4)
    nblk = S // Q_BLOCK
    kpos = jnp.arange(S)

    def to_blocks(a):
        return a.reshape((B, nblk, Q_BLOCK) + a.shape[2:]).swapaxes(0, 1)

    t_blocks = kpos.reshape(nblk, Q_BLOCK)

    def block_fn(args):
        qb, iqb, iwb, tb = args
        s = jnp.einsum('bqhd,bkd->bhqk', iqb, ik).astype(jnp.float32) * (IDX_DIM ** -0.5)
        w = iwb.astype(jnp.float32) * (IDX_HEADS ** -0.5)
        score = jnp.einsum('bqh,bhqk->bqk', w, jax.nn.relu(s))
        causal = kpos[None, :] <= tb[:, None]
        score = jnp.where(causal[None], score, -jnp.inf)
        _, idx = lax.top_k(score, k_top)
        valid = idx <= tb[None, :, None]
        kg = jax.vmap(lambda kb, ib: kb[ib])(k, idx)
        vg = jax.vmap(lambda vb, ib: vb[ib])(v, idx)
        sc = jnp.einsum('bqhd,bqkhd->bhqk', qb, kg).astype(jnp.float32) * (Dh ** -0.5)
        sc = jnp.where(valid[:, None], sc, -jnp.inf)
        p = jax.nn.softmax(sc, axis=-1)
        return jnp.einsum('bhqk,bqkhd->bqhd', p.astype(vg.dtype), vg)

    out = lax.map(block_fn, (to_blocks(q), to_blocks(iq), to_blocks(iw), t_blocks))
    return out.swapaxes(0, 1).reshape(B, S, H * Dh)

def hybrid_mixer(xn, w_in, pool_w, pool_scale, w_pool_proj, w_attn_proj, w_out):
    B, S, _ = xn.shape
    proj = xn @ w_in
    cuts = [int(c) for c in np.cumsum(IN_SPLITS)[:-1]]
    u_pool, q, k, v, iq, ik, iw, gates = jnp.split(proj, cuts, axis=-1)
    pos = jnp.arange(S, dtype=jnp.float32)

    pooled = multiscale_pool(u_pool)
    mixed = jnp.einsum('bsgc,gcd->bsgd', pooled, pool_w).reshape(B, S, POOL_WIDTH) * pool_scale
    y_pool = mixed @ w_pool_proj

    q = rope_partial(q.reshape(B, S, N_HEADS, HEAD_DIM), pos)
    k = rope_partial(k.reshape(B, S, N_HEADS, HEAD_DIM), pos)
    v = v.reshape(B, S, N_HEADS, HEAD_DIM)
    iq = rope_partial(iq.reshape(B, S, IDX_HEADS, IDX_DIM), pos)
    ik = rope_partial(ik.reshape(B, S, 1, IDX_DIM), pos)[:, :, 0]
    o = indexed_sparse_attention(q, k, v, iq, ik, iw)
    y_attn = o @ w_attn_proj

    g = jax.nn.sigmoid(gates.astype(jnp.float32)).reshape(B, S, N_BRANCH, D_MODEL)
    merged = (g[:, :, 0] * y_pool.astype(jnp.float32) + g[:, :, 1] * y_attn.astype(jnp.float32)).astype(xn.dtype)
    return merged @ w_out

def conv_ffn(xn, w_up, conv_w, conv_b, w_down):
    h = xn @ w_up
    C = h.shape[-1]
    h = lax.conv_general_dilated(h, conv_w[:, None, :].astype(h.dtype), window_strides=(1,),
                                 padding=[(CONV_WIDTH - 1, 0)],
                                 dimension_numbers=('NWC', 'WIO', 'NWC'),
                                 feature_group_count=C) + conv_b
    a, b = jnp.split(h, 2, axis=-1)
    return (jax.nn.silu(a) * b) @ w_down

def second_inputs(seed: int = 0) -> dict:
    key = jax.random.key(seed)
    ks = jax.random.split(key, 16)
    f32 = jnp.float32
    nrm = lambda k, shape, fan: jax.random.normal(k, shape, f32) * (fan ** -0.5)
    L = DEPTH_2
    return {
        "x": jax.random.normal(ks[0], (BATCH, SEQ, D_MODEL), f32),
        "norm_mix_g": 1.0 + 0.05 * jax.random.normal(ks[1], (L, D_MODEL), f32),
        "w_in": nrm(ks[2], (L, D_MODEL, D_IN), D_MODEL),
        "pool_w": nrm(ks[3], (L, POOL_GROUPS, POOL_GROUP_DIM, POOL_GROUP_DIM), POOL_GROUP_DIM),
        "pool_scale": 1.0 + 0.1 * jax.random.normal(ks[4], (L, POOL_WIDTH), f32),
        "w_pool_proj": nrm(ks[5], (L, POOL_WIDTH, D_MODEL), POOL_WIDTH),
        "w_attn_proj": nrm(ks[6], (L, ATTN_WIDTH, D_MODEL), ATTN_WIDTH),
        "w_out": nrm(ks[7], (L, D_MODEL, D_MODEL), D_MODEL),
        "norm_ffn_g": 1.0 + 0.05 * jax.random.normal(ks[8], (L, D_MODEL), f32),
        "w_up": nrm(ks[9], (L, D_MODEL, 2 * D_FF_2), D_MODEL),
        "conv_w": nrm(ks[10], (L, CONV_WIDTH, 2 * D_FF_2), CONV_WIDTH),
        "conv_b": 0.02 * jax.random.normal(ks[11], (L, 2 * D_FF_2), f32),
        "w_down": nrm(ks[12], (L, D_FF_2, D_MODEL), D_FF_2),
        "norm_final_g": 1.0 + 0.05 * jax.random.normal(ks[13], (D_MODEL,), f32),
    }

def second_block(x, norm_mix_g, w_in, pool_w, pool_scale, w_pool_proj, w_attn_proj, w_out,
              norm_ffn_g, w_up, conv_w, conv_b, w_down, norm_final_g):
    h = x
    for l in range(DEPTH_2):
        h = h + hybrid_mixer(rmsnorm(h, norm_mix_g[l]), w_in[l], pool_w[l], pool_scale[l],
                             w_pool_proj[l], w_attn_proj[l], w_out[l])
        h = h + conv_ffn(rmsnorm(h, norm_ffn_g[l]), w_up[l], conv_w[l], conv_b[l], w_down[l])
    return rmsnorm(h, norm_final_g)


def setup_inputs(seed=0):
    out = dict(first_inputs(seed))
    for name, value in second_inputs(seed + 1).items():
        if name != "x":
            out[name + "_2"] = value
    return out


def reference(
    x, c, w_ada, b_ada, ln_g, ln_b, gla_w_in, gla_w_gk2, gla_b_gk, gla_g_norm, gla_w_out,
    att_w_in, att_b_in, att_rel_bias, att_w_out, ff_w1, ff_w2, norm_mix_g_2, w_in_2, pool_w_2,
    pool_scale_2, w_pool_proj_2, w_attn_proj_2, w_out_2, norm_ffn_g_2, w_up_2, conv_w_2,
    conv_b_2, w_down_2, norm_final_g_2,
):
    x = first_block(
        x, c, w_ada, b_ada, ln_g, ln_b, gla_w_in, gla_w_gk2, gla_b_gk, gla_g_norm, gla_w_out,
        att_w_in, att_b_in, att_rel_bias, att_w_out, ff_w1, ff_w2,
    )
    return second_block(
        x, norm_mix_g_2, w_in_2, pool_w_2, pool_scale_2, w_pool_proj_2, w_attn_proj_2, w_out_2,
        norm_ffn_g_2, w_up_2, conv_w_2, conv_b_2, w_down_2, norm_final_g_2,
    )


_drawn_inputs = setup_inputs


def setup_inputs(seed=0):
    import zlib

    import numpy as np

    out = dict(_drawn_inputs(seed))
    spreads = {}
    factors = {'gla_b_gk': 4.377,
     'gla_g_norm': 6.865,
     'att_b_in': 4.776,
     'att_rel_bias': 4.151,
     'conv_b_2': 4.264}
    for name, (base, spread) in spreads.items():
        noise = np.random.default_rng([zlib.crc32(name.encode()), seed]).standard_normal(out[name].shape)
        drawn = base * np.exp(spread * noise) if base else spread * noise
        out[name] = __import__('jax').numpy.asarray(drawn.astype(out[name].dtype))
    for name, factor in factors.items():
        out[name] = (out[name] * factor).astype(out[name].dtype)
    return out
```

```python
from contextlib import ExitStack

import numpy as np
import concourse.bass as bass
from concourse import mybir

F32 = mybir.dt.float32
F32R = mybir.dt.float32r
I32 = mybir.dt.int32
ACT = mybir.ActivationFunctionType
ALU = mybir.AluOpType
AX = mybir.AxisListType

P = 128
D = 1024
KT = D // P
S = 256
ST = S // P
DEPTH = 2
CHUNK = 64
NCH = S // CHUNK
GLA_H, GLA_DK, GLA_DV, GLA_RANK = 4, 128, 256, 16
ATT_H, HD = 16, 64
MAX_REL = 128
D_FF = 4096
ALPHA = (2.0 * DEPTH) ** 0.25
LN_EPS, RMS_EPS = 1e-5, 1e-6
NEG = -1e30
TAKEN = -3e38
POOL_WINDOWS = (2, 4, 8, 16)
ATT2_H = 8
IDX_H = 8
ROT = 16
ROPE_THETA = 500000.0
TOPK = min(256, S // 4)
D_FF2 = 2816
FT2 = D_FF2 // P

CW = 2048
N_RAW, N_SPLIT, N_ADA_RING = 4, 2, 3
ADA_COLS = 6 * D
ADA_CHUNKS = KT * ADA_COLS // CW


def chunk_sizes():
    full, out = CW, []
    out += [KT * P] + [full] * 16
    out += [full] * (2 * (D_FF // 256))
    out += [full] * 16
    out += [full] * (2 * (D_FF // 256))
    out += [KT * (2 * HD + IDX_H)] + [full] * (10 + 8)
    out += [full] * 8
    out += [full] + [full, D] * (FT2 - 1) + [D]
    return out


SIZES = chunk_sizes()

VEC_PARTS = [("c", KT), ("b_ada", DEPTH * 48), ("ln_g", 4 * KT), ("ln_b", 4 * KT), ("b_gk", 4),
             ("g_norm", 8), ("att_b", 24), ("pool_scale", 4), ("norm_mix", 8), ("norm_ffn", 8),
             ("conv_b", 2 * FT2), ("conv_w", 3 * 2 * FT2), ("norm_final", 8)]
VEC = {}
_at = 0
for _name, _n in VEC_PARTS:
    VEC[_name] = _at
    _at += _n
N_VEC = _at


class Tok:

    def __init__(self, sem, base, loop=None, step=None):
        self.sem, self.base, self.loop, self.step = sem, base, loop, step

    def value(self, loop, i):
        if self.loop is None:
            return self.base
        step = self.step if self.step is not None else self.loop.per.get(self.sem, 0)
        if self.loop is loop:
            return self.base + step * i
        return self.base + step * (self.loop.n - 1)


class Lag:

    def __init__(self, tok=None, back=1):
        self.tok, self.back = tok, back

    def bind(self, tok):
        self.tok = tok

    @property
    def sem(self):
        return self.tok.sem

    def value(self, loop, i):
        step = self.tok.step if self.tok.step is not None else self.tok.loop.per[self.tok.sem]
        return self.tok.base - step * self.back + step * i


class Loop:
    def __init__(self, n):
        self.n, self.per, self.base, self.i = n, {}, {}, None


class Queues:

    def __init__(self, nc, sem):
        self.nc, self.sem = nc, sem
        self.items = {k: [] for k in ("pe", "act", "dve", "pool", "sp")}
        self.done = {k: sem(f"{k}_done") for k in self.items}
        self.count = {}
        self.loop = None
        self.uses = 4

    def token(self, s, by):
        if self.loop is not None:
            self.loop.base.setdefault(s, self.count.get(s, 0))
            self.loop.per[s] = self.loop.per.get(s, 0) + by
        self.count[s] = self.count.get(s, 0) + by
        return Tok(s, self.count[s], self.loop)

    def add(self, engine, make, waits, inc=None, by=1):
        flat = []

        def spread(ws):
            for w in ws:
                if isinstance(w, (list, tuple)):
                    spread(w)
                elif w is not None:
                    flat.append(w)

        spread(waits)
        s = self.done[engine] if inc is True else inc
        tok = self.token(s, by) if s is not None else None
        self.items[engine].append((make, flat, s, by, self.loop))
        return tok

    def pe(self, make, *waits, inc=None):
        return self.add("pe", make, waits, inc)

    def act(self, make, *waits, inc=True):
        return self.add("act", make, waits, inc)

    def dve(self, make, *waits, inc=True):
        return self.add("dve", make, waits, inc)

    def pool(self, make, *waits, inc=True):
        return self.add("pool", make, waits, inc)

    def repeat(self, n, body):
        loop = Loop(n)
        marks = {k: len(v) for k, v in self.items.items()}
        self.loop = loop
        body(loop)
        self.loop = None
        for s, per in loop.per.items():
            self.count[s] += per * (n - 1)
        for k, v in self.items.items():
            inside = v[marks[k]:]
            if inside:
                v[marks[k]:] = [(loop, inside)]

    def emit(self, name, e):
        seen = {}

        def wait(w, loop):
            inside = loop is not None and w.loop is loop if isinstance(w, Tok) else True
            if inside:
                e.wait_ge(w.sem, w.value(loop, loop.i))
                return
            v = w.value(None, None)
            if seen.get(id(w.sem), 0) < v:
                e.wait_ge(w.sem, v)
                if loop is None:
                    seen[id(w.sem)] = v

        def one(item):
            make, waits, s, by, loop = item
            for w in waits:
                wait(w, loop)
            ins = make(e)
            if s is not None:
                ins.then_inc(s, by)

        for item in self.items[name]:
            if isinstance(item[0], Loop):
                loop, inside = item
                with e.Fori(0, loop.n) as i:
                    loop.i = i
                    for x in inside:
                        one(x)
                loop.i = None
            else:
                one(item)


def build(nc, weights, ada, vecs, x_in, w_gk2, rel_bias, pool_w, rope, pool_count, out):
    with ExitStack() as ctx:
        def sb(name, shape, dt=F32):
            return ctx.enter_context(nc.sbuf_tensor(name, shape, dt))

        def sem(name):
            return ctx.enter_context(nc.semaphore(name))

        weight_raw = [sb(f"weight_raw{i}", [P, CW]) for i in range(N_RAW)]
        weight_hi = [sb(f"weight_hi{i}", [P, CW], F32R) for i in range(N_SPLIT)]
        weight_lo = [sb(f"weight_lo{i}", [P, CW], F32R) for i in range(N_SPLIT)]
        ada_raw = [sb(f"ada_raw{i}", [P, CW]) for i in range(N_ADA_RING)]
        raw_full = [sem(f"raw_full{i}") for i in range(N_RAW)]
        hi_full = [sem(f"hi_full{i}") for i in range(N_SPLIT)]
        lo_full = [sem(f"lo_full{i}") for i in range(N_SPLIT)]
        chunk_done = sem("chunk_done")
        ada_full = [sem(f"ada_full{i}") for i in range(N_ADA_RING)]
        ada_used = sem("ada_used")
        bank_free = [sem(f"bank_free{i}") for i in range(2)]
        vec_in, x_arrived, w2_in = sem("vec_in"), sem("x_arrived"), sem("w2_in")
        tables_in = [sem(f"tables_in{i}") for i in range(3)]
        stored = sem("stored")
        bias_full = [sem(f"bias_full{i}") for i in range(4)]

        ada_acc = sb("ada_acc", [P, ADA_COLS])
        res = sb("res", [P, KT, S])
        dev = sb("dev", [P, KT, S])
        act_hi = sb("act_hi", [P, KT, S], F32R)
        act_lo = sb("act_lo", [P, KT, S], F32R)
        vec = sb("vec", [P, N_VEC])
        mods = [sb(f"mods{i}", [P, 48]) for i in range(DEPTH)]
        norm_scale = sb("norm_scale", [P, 2, KT])
        gate1 = sb("gate1", [P, KT])
        c_act = sb("c_act", [P, KT])
        ident = sb("ident", [P, P])
        ones_d = sb("ones_d", [P, P])
        eps = sb("eps", [P, 2])
        rstd = sb("rstd", [P, S])
        ones_col = sb("ones_col", [P, 2])
        square = sb("square", [P, KT, S])
        alpha_ln = sb("alpha_ln", [P, 2, KT])
        arena_at = nc.sbuf_base
        arena_end = nc.sbuf_usable_end

        class Arena:

            def __init__(self, tag):
                self.tag, self.at = tag, arena_at

            def __call__(self, name, shape, dt=F32):
                n = 4 * int(np.prod(shape[1:]))
                t = nc.alloc_sbuf_tensor_at(f"{self.tag}_{name}", shape, dt, offset=self.at)
                self.at += (n + 31) // 32 * 32
                assert self.at <= arena_end, (self.tag, name, self.at, arena_end)
                return t

        ps = ctx.enter_context(nc.psum_tensor("ps", [P, 8, 512], F32))
        work = [ps[:, b, :] for b in range(2)]
        y_acc = ps[:, 2:6, :].rearrange("p a (b n) -> p (a b) n", b=2)
        mean_ps = ps[:, 6, 0:S]
        var_ps = ps[:, 7, 0:S]

        q = Queues(nc, sem)
        pe, act, dve, pool = q.pe, q.act, q.dve, q.pool

        def v_of(name, n=0):
            return vec[:, VEC[name] + n:VEC[name] + n + 1]

        stream = {"j": 0, "bank": 0}

        def at_chunk(s, j, slots, unit):
            step = 4 // slots * unit if q.loop else None
            return Tok(s, (j // slots + 1) * unit, q.loop, step)

        def split(j, size):
            r, h = j % N_RAW, j % N_SPLIT
            free = Tok(chunk_done, j - N_SPLIT + 1, q.loop, 4 if q.loop else None) if j >= N_SPLIT else None
            landed = at_chunk(raw_full[r], j, N_RAW, 16)
            q.add("act", lambda e: e.activation(weight_hi[h][:, 0:size], weight_raw[r][:, 0:size], ACT.Copy),
                  [landed, free], hi_full[h])
            q.add("dve", lambda e: e.tensor_tensor(weight_lo[h][:, 0:size], weight_raw[r][:, 0:size],
                                                   weight_hi[h][:, 0:size].bitcast(F32), ALU.subtract),
                  [at_chunk(hi_full[h], j, N_SPLIT, 1), free], lo_full[h])

        def next_chunk():
            j = stream["j"]
            stream["j"] += 1
            split(j, SIZES[j])
            return j, weight_hi[j % N_SPLIT], weight_lo[j % N_SPLIT]

        def skip(n):
            stream["j"] += n

        def chunk_products(j, groups, waits=(), steps=None):
            hi_in = at_chunk(hi_full[j % N_SPLIT], j, N_SPLIT, 1)
            lo_in = at_chunk(lo_full[j % N_SPLIT], j, N_SPLIT, 1)
            first = True
            last = len(groups) - 1
            for n, (o, a, b, start, lo, extra) in enumerate(groups):
                w = list(extra)
                if first:
                    w += [hi_in, *waits]
                if lo == 2:
                    w.append(lo_in)
                first = False
                pe(lambda e, o=o, a=a, b=b, start=start: e.matmul(o, a, b, start=start, stop=False,
                                                                  skip_group_check=True),
                   *w, inc=chunk_done if n == last else None)
            return Tok(chunk_done, j + 1, q.loop, 4 if q.loop else None)

        def products(hi, lo, wide, nk, outs, m_hi, m_lo, k0=0, ready=None, fresh=True, token_major=False):
            wh, wl = (w[:, 0:nk * wide].rearrange("p (k n) -> p k n", k=nk) for w in (hi, lo))
            first, second = [], []
            seen_banks = set()
            for n, (o, bank) in enumerate(outs):
                for k in range(nk):
                    start = fresh and k == 0 and (bank not in seen_banks)
                    if token_major:
                        t = slice(n * P, (n + 1) * P)
                        a, al, b, bl = m_hi[:, k0 + k, t], m_lo[:, k0 + k, t], wh[:, k, :], wl[:, k, :]
                        tri = [(a, b), (al, b), (a, bl)]
                    else:
                        c = slice(n * P, (n + 1) * P)
                        a, al, b, bl = wh[:, k, c], wl[:, k, c], m_hi[:, k0 + k, :], m_lo[:, k0 + k, :]
                        tri = [(a, b), (a, bl), (al, b)]
                    extra = ready[k] if ready is not None and n == 0 else ()
                    first.append((o, tri[0][0], tri[0][1], start, 0, extra))
                    first.append((o, tri[1][0], tri[1][1], False, 0, ()))
                    second.append((o, tri[2][0], tri[2][1], False, 2 if not second else 1, ()))
                    seen_banks.add(bank)
            return first + second

        def project(evac, act_k=KT, ready=None, wide=256, token_major=False, cols=None, m=None, nk=KT):
            j, hi, lo = next_chunk()
            w = stream["bank"]
            stream["bank"] += 1
            b = w % 2
            free = None
            if w >= 2:
                free = Tok(bank_free[b], w // 2, q.loop, 2 if q.loop else None)
                if q.loop and q.uses == 2:
                    free.step = 1
            hi_m, lo_m = m if m else (act_hi, act_lo)
            width = cols if token_major and cols else S
            n_out = ST if token_major else wide // P
            outs = [(work[b][:, n * S:n * S + width], b) for n in range(n_out)]
            done = chunk_products(j, products(hi, lo, wide, nk, outs, hi_m, lo_m, ready=ready,
                                              token_major=token_major), waits=[free])
            evac(work[b].rearrange("p (n t) -> p n t", n=2), done, bank_free[b])
            return done

        def accumulate(outs, m, nk=KT, wide=256, waits=(), ready=None):
            j, hi, lo = next_chunk()
            return chunk_products(j, products(hi, lo, wide, nk, outs, *m, ready=ready), waits=waits)

        def y_tiles(first, n):
            return [(y_acc[:, first + i, :], 2 + (first + i) // 2) for i in range(n)]

        ada_state = {"n": 0}

        def ada_chunk(extra=()):
            n = ada_state["n"]
            ada_state["n"] += 1
            r = n % N_ADA_RING
            k = n % KT
            g = n // KT % (ADA_COLS // CW)
            a = ada_acc[:, g * CW:(g + 1) * CW]
            before = ada_state.get("tok")
            landed = Tok(ada_full[r], (n // N_ADA_RING + 1) * 16)
            if k == 0:
                t = q.add("dve", lambda e: e.tensor_scalar(a, ada_raw[r][:, :], c_act[:, 0:1], None, ALU.mult),
                          [landed, ada_state["c"], *extra], ada_used)
            else:
                t = q.add("dve", lambda e: e.scalar_tensor_tensor(out=a, in0=ada_raw[r][:, :], scalar=c_act[:, k:k + 1],
                                                                  in1=a, op0=ALU.mult, op1=ALU.add),
                          [landed, before], ada_used)
            ada_state["tok"] = t
            return t

        def mods_of(layer, g, *waits):
            first = 16 * g
            m_ps = ps[:, 7, 0:16]
            t = None
            for n in range(16):
                t = pe(lambda e, n=n: e.matmul(m_ps[:, n:n + 1], ada_acc[:, (first + n) * P:(first + n + 1) * P],
                                               ones_col[:, 0:1], start=True, stop=True, skip_group_check=True),
                       *((ada_state["tok"], ada_state.get("mods"), consts, waits) if n == 0 else ()),
                       inc=True if n == 15 else None)
            b = VEC["b_ada"] + 48 * layer + first
            ada_state["mods"] = dve(lambda e: e.tensor_tensor(mods[layer][:, first:first + 16], m_ps,
                                                              vec[:, b:b + 16], ALU.add), t)
            ada_state["summed"] = t
            return ada_state["mods"]

        def mod(layer, which, n=None):
            if n is None:
                return mods[layer][:, which * KT:(which + 1) * KT]
            return mods[layer][:, which * KT + n:which * KT + n + 1]

        def queue_ada_loads():
            for n in range(N_ADA_RING):
                q.add("pool", lambda e, n=n: e.dma_start(ada_raw[n][:, :], ada[n]), [], ada_full[n], 16)
            total = DEPTH * ADA_CHUNKS

            def body(loop):
                for u in range(N_ADA_RING):
                    n = N_ADA_RING + u
                    q.add("pool", lambda e, u=u: e.dma_start(
                        ada_raw[u][:, :], ada[bass.ds(loop.i * N_ADA_RING + N_ADA_RING + u, 1), :, :].squeeze(0)),
                        [Tok(ada_used, n - N_ADA_RING + 1, q.loop, N_ADA_RING)], ada_full[u], 16)

            q.repeat(total // N_ADA_RING - 1, body)

        t_vec = q.add("sp", lambda e: e.dma_start(vec[:, :], vecs), [], vec_in, 16)
        t_load = [t_vec, q.add("sp", lambda e: e.dma_start(res[:, :, :], x_in), [], x_arrived, 16)]
        consts = [pool(lambda e: e.memset(ones_col[:, :], 1.0)),
                  pool(lambda e: e.memset(ones_d[:, :], 1.0 / D)),
                  pool(lambda e: e.memset(eps[:, 0:1], LN_EPS)),
                  pool(lambda e: e.memset(eps[:, 1:2], RMS_EPS))]
        t = pool(lambda e: e.memset(ident[:, :], 0.0))
        consts.append(pool(lambda e: e.affine_select(out=ident[:, :], in_=ident[:, :], compare_op=ALU.not_equal,
                                                     fill=1.0, base=0, pattern=[[-1, P]], channel_multiplier=1), t))
        consts = consts[-1]

        ar = Arena("gla")
        g_q = ar("q", [P, GLA_H, S])
        g_k = ar("k", [P, GLA_H, S])
        g_v = ar("v", [P, ST, D])
        g_sg = ar("sg", [P, KT, S])
        g_la = ar("la", [P, GLA_H * S])
        g_e = ar("e", [P, GLA_H * S])
        g_en = ar("en", [P, GLA_H * S])
        g_scan = g_sg[:, 0:GLA_H, :].rearrange("p h t -> p (h t)")
        g_qn = ar("qn", [P, GLA_H, S])
        g_kn = g_en[:, :].rearrange("p (h t) -> p h t", h=GLA_H)
        g_kp = g_e[:, :].rearrange("p (h t) -> p h t", h=GLA_H)
        g_dec = ar("dec", [P, GLA_H * NCH])
        g_gk = ar("gk", [P, S])
        g_w2 = ar("w2", [GLA_RANK, GLA_H * P])
        g_fwd = ar("fwd", [P, ST * P])
        g_bwd = ar("bwd", [P, ST * P])
        a_at = [ar(f"a{i}", [P, ST, P]) for i in range(2)]
        g_ket = ar("ket", [P, ST, P])
        g_st = ar("st", [P, 3, GLA_DV])
        t_w2 = q.add("sp", lambda e: e.dma_start(g_w2[:, :], w_gk2), [], w2_in, 16)

        pool(lambda e: e.memset(g_scan, 1.0))
        t = pool(lambda e: e.memset(g_fwd[:, :], 1.0))
        pool(lambda e: e.memset(g_bwd[:, :], 1.0))
        for i in range(2):
            t = pool(lambda e, i=i: e.memset(a_at[i][:, :, :], 0.0))
        scan_v = g_scan.rearrange("p (c t) -> p c t", t=CHUNK)
        fwd_v, bwd_v = (m[:, :].rearrange("p (a t) -> p a t", a=ST) for m in (g_fwd, g_bwd))
        pool(lambda e: e.memset(scan_v[:, :, 0:1], 0.0), t)
        pool(lambda e: e.affine_select(out=fwd_v, in_=fwd_v, compare_op=ALU.is_ge, fill=0.0, base=0,
                                       pattern=[[0, ST], [1, P]], channel_multiplier=-1))
        t = pool(lambda e: e.affine_select(out=bwd_v, in_=bwd_v, compare_op=ALU.is_gt, fill=0.0, base=0,
                                           pattern=[[0, ST], [-1, P]], channel_multiplier=1))
        pool(lambda e: e.memset(fwd_v[0:CHUNK, :, CHUNK:P], 0.0), t)
        gla_consts = pool(lambda e: e.memset(bwd_v[CHUNK:P, :, 0:CHUNK], 0.0), t)
        queue_ada_loads()

        def queue_weight_loads():
            j = 0
            while j < len(SIZES):
                run = 1
                pat = SIZES[j:j + 4]
                while SIZES[j + 4 * run:j + 4 * run + 4] == pat and j >= 4:
                    run += 1
                if run >= 2:
                    j0 = j

                    def body(loop):
                        for u in range(4):
                            jj = j0 + u
                            size = SIZES[jj]
                            freed = Tok(lo_full[jj % 2], (jj - 4) // 2 + 1, q.loop, 2)
                            q.add("sp", lambda e, jj=jj, size=size: e.dma_start(
                                weight_raw[jj % 4][:, 0:size],
                                weights[bass.ds(loop.i * 4 + jj, 1), :, 0:size].squeeze(0)),
                                [freed], raw_full[jj % 4], 16)

                    q.repeat(run, body)
                    j += 4 * run
                else:
                    size = SIZES[j]
                    freed = Tok(lo_full[j % 2], (j - 4) // 2 + 1) if j >= 4 else None
                    q.add("sp", lambda e, j=j, size=size: e.dma_start(weight_raw[j % 4][:, 0:size],
                                                                      weights[j, :, 0:size]),
                          [freed], raw_full[j % 4], 16)
                    j += 1

        queue_weight_loads()

        def split_activation(src, n, hi, lo, *waits, free=()):
            h = act(lambda e: e.activation(hi, src, ACT.Copy), *waits, *free)
            return [h, dve(lambda e: e.tensor_tensor(lo, src, hi.bitcast(F32), ALU.subtract), h, *waits, *free)]

        def modulate(k, src, a, b, tmp, ready, free):
            h = act(lambda e: e.activation(act_hi[:, k, :], src, ACT.Identity, bias=b, scale=a), ready, *free)
            t = dve(lambda e: e.tensor_scalar(tmp, src, a, b, ALU.mult, ALU.add), ready, *free)
            lo = dve(lambda e: e.tensor_tensor(act_lo[:, k, :], tmp, act_hi[:, k, :].bitcast(F32), ALU.subtract),
                     h, t)
            return [h, lo]

        def norm(eps_col, z_toks, centre, layer_vec, x_of, u_of, free):
            t = None
            if centre:
                for k in range(KT):
                    t = pe(lambda e, k=k: e.matmul(mean_ps, ones_d[:, :], dev[:, k, :], start=(k == 0),
                                                   stop=(k == KT - 1), skip_group_check=True),
                           z_toks[k], *(free if k == 0 else ()), inc=True if k == KT - 1 else None)
                mean_t = t
                cent = []
                for h in range(4):
                    d = dev[:, 2 * h:2 * h + 2, :]
                    cent.append(dve(lambda e, d=d: e.tensor_tensor(
                        d, d, mean_ps.unsqueeze(1).broadcast_to([P, 2, S]), ALU.subtract), mean_t))
            else:
                cent = [z_toks[2 * h:2 * h + 2] for h in range(4)]
            sq_t = []
            for h in range(4):
                sq_t.append(act(lambda e, h=h: e.activation(square[:, 2 * h:2 * h + 2, :], dev[:, 2 * h:2 * h + 2, :],
                                                            ACT.Square), cent[h], *free))
            for k in range(KT):
                t = pe(lambda e, k=k: e.matmul(var_ps, ones_d[:, :], square[:, k, :], start=(k == 0),
                                               stop=(k == KT - 1), skip_group_check=True), sq_t[k // 2],
                       *(free if k == 0 else ()), inc=True if k == KT - 1 else None)
            a = act(lambda e: e.activation(rstd[:, :], var_ps, ACT.Ln, bias=eps[:, eps_col:eps_col + 1]), t, *free)
            r = act(lambda e: e.activation(rstd[:, :], rstd[:, :], ACT.Exp, scale=-0.5), a)
            ready, used = [], []
            for k in range(KT):
                nt = dve(lambda e, k=k: e.tensor_tensor(dev[:, k, :], dev[:, k, :], rstd[:, :], ALU.mult), r,
                         sq_t[k // 2], cent[k // 2])
                ready.append(u_of(k, nt))
                used.append(nt)
            xs = [x_of(k, used[k]) for k in range(KT)]
            return ready, xs

        def residual(y_done, gate, x_toks, scale_x, free_dev):
            out_t = []
            for k in range(KT):
                if gate is None:
                    out_t.append(dve(lambda e, k=k: e.tensor_tensor(dev[:, k, :], y_acc[:, k, :], res[:, k, :], ALU.add),
                                     y_done, x_toks[k], *free_dev))
                else:
                    out_t.append(dve(lambda e, k=k: e.scalar_tensor_tensor(
                        out=dev[:, k, :], in0=y_acc[:, k, :], scalar=gate[:, k:k + 1], in1=res[:, k, :],
                        op0=ALU.mult, op1=ALU.add), y_done, x_toks[k], *free_dev))
            return out_t

        state = {}

        def layer_norm_stage(idx, y_done, gate_t, sc, sh, next_vec_t):
            z = residual([y_done, gate_t], gate1, state["x"], ALPHA, state["dev_free"])
            g0, b0 = VEC["ln_g"] + KT * idx, VEC["ln_b"] + KT * idx
            lg, lb = vec[:, g0:g0 + KT], vec[:, b0:b0 + KT]
            w = state["norm_scale_free"]
            if sc is not None:
                t = dve(lambda e: e.scalar_tensor_tensor(out=norm_scale[:, 0, :], in0=sc, scalar=1.0, in1=lg,
                                                         op0=ALU.add, op1=ALU.mult), next_vec_t, *w)
                t1 = dve(lambda e: e.scalar_tensor_tensor(out=norm_scale[:, 1, :], in0=sc, scalar=1.0, in1=lb,
                                                          op0=ALU.add, op1=ALU.mult), next_vec_t, *w)
                t2 = dve(lambda e: e.tensor_tensor(norm_scale[:, 1, :], norm_scale[:, 1, :], sh, ALU.add), t1)
                t3 = dve(lambda e: e.tensor_scalar(alpha_ln[:, 0, :], lg, ALPHA, None, ALU.mult), *w)
                t4 = dve(lambda e: e.tensor_scalar(alpha_ln[:, 1, :], lb, ALPHA, None, ALU.mult), *w)
                vt = [t, t2, t3, t4]

                def u_of(k, nt):
                    return modulate(k, dev[:, k, :], norm_scale[:, 0, k:k + 1], norm_scale[:, 1, k:k + 1],
                                    square[:, k, :], [nt, *vt], [])

                def x_of(k, nt):
                    return act(lambda e: e.activation(res[:, k, :], dev[:, k, :], ACT.Identity,
                                                      bias=alpha_ln[:, 1, k:k + 1], scale=alpha_ln[:, 0, k:k + 1]),
                               nt, z[k], *vt)
                ready, xs = norm(0, z, True, None, x_of, u_of, state["ps_free"])
            else:
                def x_only(k, nt):
                    return act(lambda e: e.activation(res[:, k, :], dev[:, k, :], ACT.Identity,
                                                      bias=vec[:, b0 + k:b0 + k + 1], scale=vec[:, g0 + k:g0 + k + 1]),
                               nt, z[k])
                ready, xs = norm(0, z, True, None, x_only, lambda k, nt: None, state["ps_free"])
            state["x"] = xs
            state["z"] = z
            state["dev_free"] = xs + [x for r in ready if r for x in r]
            state["norm_scale_free"] = state["dev_free"]
            state["ps_free"] = state["dev_free"]
            return ready

        def rms_stage(vname, z, next_u=True):
            def u_of(k, nt):
                if not next_u:
                    return None
                h = act(lambda e: e.activation(act_hi[:, k, :], dev[:, k, :], ACT.Copy, scale=v_of(vname, k)), nt)
                t = dve(lambda e: e.tensor_scalar(square[:, k, :], dev[:, k, :], v_of(vname, k), None, ALU.mult), nt)
                return [h, dve(lambda e: e.tensor_tensor(act_lo[:, k, :], square[:, k, :],
                                                         act_hi[:, k, :].bitcast(F32), ALU.subtract), h, t)]

            def x_of(k, nt):
                if next_u:
                    return None
                return act(lambda e: e.activation(res[:, k, :], dev[:, k, :], ACT.Copy, scale=v_of(vname, k)), nt)
            ready, xs = norm(1, z, False, None, x_of, u_of, state["ps_free"])
            if next_u:
                state["dev_free"] = [x for r in ready for x in r]
                state["ps_free"] = state["dev_free"]
            return ready, xs

        e_c = act(lambda e: e.activation(c_act[:, :], vec[:, VEC["c"]:VEC["c"] + KT], ACT.Exp, scale=-1.0), t_load)
        t = dve(lambda e: e.tensor_scalar(c_act[:, :], c_act[:, :], 1.0, None, ALU.add), e_c)
        t = dve(lambda e: e.reciprocal(c_act[:, :], c_act[:, :]), t)
        ada_state["c"] = dve(lambda e: e.tensor_tensor(c_act[:, :], c_act[:, :], vec[:, VEC["c"]:VEC["c"] + KT],
                                                       ALU.mult), t)
        for _ in range(KT):
            ada_chunk()
        mt = mods_of(0, 0)
        t = dve(lambda e: e.tensor_scalar(norm_scale[:, 0, :], mod(0, 1), 1.0, None, ALU.add), mt)
        ready = [modulate(k, res[:, k, :], norm_scale[:, 0, k:k + 1], mod(0, 0, k), square[:, k, :], [t, t_load], [])
                 for k in range(KT)]
        state["x"] = [act(lambda e, k=k: e.activation(res[:, k, :], res[:, k, :], ACT.Copy, scale=ALPHA), *ready[k])
                      for k in range(KT)]
        state["dev_free"], state["ps_free"] = [], []
        state["norm_scale_free"] = [x for r in ready for x in r]

        box = {}

        def evac_gk(b, done, s):
            box["gk"] = q.add("act", lambda e: e.activation(g_gk[:, :], b[:, 0, :], ACT.Copy), [done], s)

        project(evac_gk, wide=P, ready=ready)
        gate_ps = ps[:, 2:4, :].rearrange("p a (b n) -> p (a b) n", b=2)
        for h in range(GLA_H):
            t = pe(lambda e, h=h: e.matmul(gate_ps[:, h, :], g_w2[:, h * P:(h + 1) * P], g_gk[0:GLA_RANK, :],
                                           start=True, stop=True, skip_group_check=True),
                   box["gk"], t_w2, inc=True if h == GLA_H - 1 else None)
        la = g_la[:, :]
        zt = [dve(lambda e, h=h: e.tensor_scalar(g_la[:, h * S:(h + 1) * S], gate_ps[:, h, :], v_of("b_gk", h), None,
                                                 ALU.add), t) for h in range(GLA_H)]
        gate_read = zt[-1]
        a = act(lambda e: e.activation(g_e[:, :], la, ACT.Abs), zt)
        a = act(lambda e: e.activation(g_e[:, :], g_e[:, :], ACT.Exp, scale=-1.0), a)
        a = act(lambda e: e.activation(g_e[:, :], g_e[:, :], ACT.Ln, bias=1.0), a)
        t = dve(lambda e: e.scalar_tensor_tensor(out=g_en[:, :], in0=la, scalar=0.0, in1=g_e[:, :], op0=ALU.min,
                                                 op1=ALU.subtract), a)
        cum = dve(lambda e: e.tensor_tensor_scan(out=la, data0=g_scan, data1=g_en[:, :], initial=0.0,
                                                 op0=ALU.mult, op1=ALU.add), t, gla_consts, zt, a)
        TAU = 1.0 / 16.0
        e_pos = act(lambda e: e.activation(g_e[:, :], la, ACT.Exp, scale=TAU), cum, t)
        e_neg = act(lambda e: e.activation(g_en[:, :], la, ACT.Exp, scale=-TAU), cum)
        cum4 = la.rearrange("p (c t) -> p c t", t=CHUNK)
        end_t = dve(lambda e: e.tensor_tensor(g_qn[:, :, :].rearrange("p h (c t) -> p (h c) t", t=CHUNK),
                                              cum4[:, :, CHUNK - 1:CHUNK].broadcast_to([P, GLA_H * NCH, CHUNK]), cum4,
                                              ALU.subtract), cum)
        e_end = act(lambda e: e.activation(la, g_qn[:, :, :].rearrange("p h t -> p (h t)"), ACT.Exp, scale=TAU),
                    end_t, e_pos, e_neg)
        e3 = lambda m: m[:, :].rearrange("p (h t) -> p h t", h=GLA_H)
        dec_t = act(lambda e: e.activation(g_dec[:, :], g_e[:, CHUNK - 1::CHUNK], ACT.Copy), e_pos)

        def evac_to(dst, eng, scale=1.0, key=None):
            def evac(b, done, s):
                box.setdefault(key, []).append(
                    q.add("act", lambda e: e.activation(dst, b, ACT.Copy, scale=scale), [done], s) if eng == "act"
                    else q.add("dve", lambda e: e.tensor_scalar(dst, b, scale, None, ALU.mult), [done], s))
            return evac

        for n in range(2):
            project(evac_to(g_q[:, 2 * n:2 * n + 2, :], "act", GLA_DK ** -0.5, "q"))
            ada_chunk()
        for n in range(2):
            project(evac_to(g_k[:, 2 * n:2 * n + 2, :], "act", 1.0, "k"))
            ada_chunk()
        mul = lambda o, a, b: (lambda e: e.tensor_tensor(o, a, b, ALU.mult))
        qn_t = dve(mul(g_qn[:, :, :], g_q[:, :, :], e3(g_en)), box["q"], e_neg, e_end)
        qf_t = dve(mul(g_q[:, :, :], g_q[:, :, :], e3(g_e)), e_pos, qn_t)
        kn_t = dve(mul(g_kn, g_k[:, :, :], e3(g_en)), box["k"], e_neg, qn_t)
        kp_t = dve(mul(g_kp, g_k[:, :, :], e3(g_e)), e_pos, qf_t, dec_t)
        ke_t = dve(mul(g_k[:, :, :], g_k[:, :, :], e3(g_la)), e_end, kn_t, kp_t)
        for n in range(4):
            def evac_v(b, done, s, n=n):
                box.setdefault("v", []).append(
                    q.add("act", lambda e: e.activation(g_v[:, :, n * 256:(n + 1) * 256], b, ACT.Copy), [done], s))
            project(evac_v, token_major=True, cols=256)
            ada_chunk()

        a_ps = ps[:, 2, :].rearrange("p (a t) -> p a t", a=4)
        ket_ps = ps[:, 3, 0:2 * P].rearrange("p (a t) -> p a t", a=2)
        u_ps = ps[:, 4:6, :].rearrange("p a (b n) -> p (a b) n", b=2)
        o_ps = ps[:, 6, :].rearrange("p (v t) -> p v t", v=2)
        ms_ps = ps[:, 7, 0:S]
        U_AT = (0, 2, 1)
        gh = {}

        def gla_scores(h):
            prev = gh.get(h - 1)
            for t in range(ST):
                c = slice(t * P, (t + 1) * P)
                pe(lambda e, t=t, c=c: e.matmul(a_ps[:, t, :], g_kn[:, h, c], g_q[:, h, c], start=True, stop=True,
                                                skip_group_check=True), kn_t, qf_t, gate_read, prev and prev["a"])
                pe(lambda e, t=t, c=c: e.matmul(a_ps[:, 2 + t, :], g_kp[:, h, c], g_qn[:, h, c], start=True,
                                                stop=True, skip_group_check=True), kp_t, qn_t)
            for t in range(ST):
                c = slice(t * P, (t + 1) * P)
                sc = pe(lambda e, t=t, c=c: e.matmul(ket_ps[:, t, :], g_k[:, h, c], ident[:, :], is_transpose=True,
                                                     start=True, stop=True, skip_group_check=True)
                        , ke_t, consts, prev and prev["ket"], inc=True if t else None)
            A = a_at[h % 2]
            w = gh[h - 2]["o_mm"] if h >= 2 else None
            t = dve(lambda e: e.copy_predicated(A[:, :, :], fwd_v.bitcast(I32), a_ps[:, 0:2, :]), sc, gla_consts, w)
            a2 = dve(lambda e: e.copy_predicated(A[:, :, :], bwd_v.bitcast(I32), a_ps[:, 2:4, :]), t)
            ket = act(lambda e: e.activation(g_ket[:, :, :], ket_ps, ACT.Copy), sc, prev and prev["u"])
            for c in range(NCH - 1):
                p0 = CHUNK * (c % 2)
                u = pe(lambda e, c=c, p0=p0: e.matmul(u_ps[:, U_AT[c], :], g_ket[p0:p0 + CHUNK, c // 2, :],
                                                      g_v[p0:p0 + CHUNK, c // 2, h * GLA_DV:(h + 1) * GLA_DV],
                                                      start=True, stop=True, skip_group_check=True),
                       ket, box["v"], prev and prev["st"], inc=True if c == NCH - 2 else None)
            st = act(lambda e: e.activation(g_st[:, 0, :], u_ps[:, 0, :], ACT.Copy), u, prev and prev["o_mm"])
            for c in (1, 2):
                st = dve(lambda e, c=c: e.scalar_tensor_tensor(
                    out=g_st[:, c, :], in0=g_st[:, c - 1, :], scalar=g_dec[:, h * NCH + c:h * NCH + c + 1],
                    in1=u_ps[:, U_AT[c], :], op0=ALU.mult, op1=ALU.add), st, dec_t, u, prev and prev["o_mm"])
            gh[h] = {"a": a2, "ket": ket, "u": u, "st": st}

        def gla_out(h):
            prev = gh.get(h - 1)
            first = True
            for v in range(2):
                for t in range(ST):
                    vs = slice(h * GLA_DV + v * P, h * GLA_DV + (v + 1) * P)
                    pe(lambda e, v=v, t=t, vs=vs, first=first: e.matmul(
                        o_ps[:, v, t * P:(t + 1) * P], g_v[:, t, vs], a_at[h % 2][:, t, :], start=first, stop=False,
                        skip_group_check=True), gh[h]["a"], prev and prev["og"])
                    first = False
            for v in range(2):
                for c in range(1, NCH):
                    o_mm = pe(lambda e, v=v, c=c: e.matmul(
                        o_ps[:, v, c * CHUNK:(c + 1) * CHUNK], g_st[:, c - 1, v * P:(v + 1) * P],
                        g_q[:, h, c * CHUNK:(c + 1) * CHUNK], start=False, stop=False, skip_group_check=True),
                        gh[h]["st"], inc=True if (v, c) == (1, NCH - 1) else None)
            sq = act(lambda e: e.activation(square[:, 0:2, :], o_ps, ACT.Square), o_mm, prev and prev["ms"],
                     [x for r in ready for x in r])
            for v in range(2):
                ms = pe(lambda e, v=v: e.matmul(ms_ps, ones_d[:, :], square[:, v, :], start=(v == 0), stop=(v == 1),
                                                skip_group_check=True), sq, prev and prev["r1"], ada_state["mods"],
                        inc=True if v else None)
            r = act(lambda e: e.activation(rstd[:, :], ms_ps, ACT.Ln, bias=eps[:, 1:2], scale=float(D // GLA_DV)),
                    ms, prev and prev["og"])
            r2 = act(lambda e: e.activation(rstd[:, :], rstd[:, :], ACT.Exp, scale=-0.5), r)
            og = dve(lambda e: e.tensor_tensor(dev[:, 2 * h:2 * h + 2, :], o_ps,
                                               rstd[:, :].unsqueeze(1).broadcast_to([P, 2, S]), ALU.mult), r2)
            gh[h].update(o_mm=o_mm, ms=ms, r1=r, og=og)

        def evac_g(n):
            def evac(b, done, s):
                sg = g_sg[:, 2 * n:2 * n + 2, :]
                t = act(lambda e: e.activation(sg, b, ACT.Exp, scale=-1.0), done)
                t = dve(lambda e: e.tensor_scalar(sg, sg, 1.0, None, ALU.add), t)
                t = dve(lambda e: e.reciprocal(sg, sg), t)
                box.setdefault("sg", []).append(
                    q.add("dve", lambda e: e.tensor_tensor(sg, sg, b, ALU.mult), [t, done], s))
            return evac

        for h in range(GLA_H):
            gla_scores(h)
            project(evac_g(h))
            ada_chunk()
            gla_out(h)
        in_done = Tok(chunk_done, stream["j"])
        mods_of(0, 1, gh[GLA_H - 1]["r1"])
        out_ready = []
        for k in range(KT):
            h = k // 2
            t = dve(lambda e, k=k: e.scalar_tensor_tensor(out=dev[:, k, :], in0=dev[:, k, :], scalar=v_of("g_norm", k),
                                                          in1=g_sg[:, k, :], op0=ALU.mult, op1=ALU.mult),
                    gh[h]["og"], box["sg"])
            out_ready.append(split_activation(dev[:, k, :], k, act_hi[:, k, :], act_lo[:, k, :], t, free=[in_done]))
        y_free = [gh[GLA_H - 1]["st"], gh[GLA_H - 1]["a"], gh[GLA_H - 1]["ket"]]

        def out_projection(ready, ada_n=0, m=None, nk=KT, wide=256, waits=()):
            tiles = wide // P
            for n in range(KT // tiles):
                done = accumulate(y_tiles(n * tiles, tiles), m or (act_hi, act_lo), nk=nk, wide=wide,
                                  waits=waits if n == 0 else (), ready=ready if n == 0 else None)
                if ada_n:
                    ada_chunk()
            return done

        y_done = out_projection(out_ready, ada_n=1, waits=y_free)
        mt = mods_of(0, 2)
        state["dev_free"] = [x for r in out_ready for x in r]
        state["ps_free"] = [gh[GLA_H - 1]["og"], gh[GLA_H - 1]["r1"], ada_state["mods"], *state["dev_free"]]


        def everything():
            return [Tok(q.done[k], q.count[q.done[k]]) for k in ("act", "dve", "pe", "pool")
                    if q.count.get(q.done[k])] + [Tok(chunk_done, stream["j"])]

        def up_down(tag, ready, y_read, n_blocks, n_tiles, evac_up, buffers, in_loop=None, after_first=None):
            hid_hi, hid_lo = buffers
            buf = {("y", 0): None, ("y", 1): None, ("split", 0): None, ("split", 1): None}
            base_j = stream["j"]

            def up(i, block, ready=None):
                p = i % 2

                def evac(b, done, s):
                    buf[("split", p)] = evac_up(block, p, b, done, s, buf[("y", p)], buf[("split", p)])

                project(evac, ready=ready)

            def down(i, fresh=False):
                p = i % 2
                j, hi, lo = next_chunk()
                buf[("y", p)] = chunk_products(
                    j, products(hi, lo, D, n_tiles, y_tiles(0, KT), hid_hi[p], hid_lo[p], fresh=fresh),
                    waits=[buf[("split", p)], y_read if fresh else None])
                return buf[("y", p)]

            up(0, 0, ready)
            if after_first:
                after_first()
            up(1, 1)
            down(0, fresh=True)
            n_loop = (n_blocks - 2) // 2

            def body(loop):
                lags = {}
                for key in buf:
                    lags[key] = Lag()
                    buf[key] = [lags[key], buf[key]]
                up(0, lambda: loop.i * 2 + 2)
                down(1)
                up(1, lambda: loop.i * 2 + 3)
                down(0)
                if in_loop:
                    in_loop(loop)
                for key, lag in lags.items():
                    lag.bind(buf[key][-1] if isinstance(buf[key], list) else buf[key])

            q.uses = 2
            q.repeat(n_loop, body)
            q.uses = 4
            skip(4 * (n_loop - 1))
            stream["bank"] += 2 * (n_loop - 1)
            done = down(1)
            assert stream["j"] == base_j + 2 * n_blocks and n_blocks % 2 == 0
            return done

        def mlp(tag, ready, y_read, in_loop=None, after_first=None):
            ar = Arena(tag)
            relu_buf = [ar(f"relu{i}", [P, 2, S]) for i in range(2)]
            sq_buf = [ar(f"sq{i}", [P, 2, S]) for i in range(2)]
            hid_hi = [ar(f"hi{i}", [P, 2, S], F32R) for i in range(2)]
            hid_lo = [ar(f"lo{i}", [P, 2, S], F32R) for i in range(2)]
            free = state["arena_free"]

            def evac_up(block, p, b, done, s, y_tok, split_tok):
                r = q.add("dve", lambda e: e.tensor_scalar(relu_buf[p][:, :, :], b, 0.0, None, ALU.max),
                          [done, split_tok, free], s)
                h = act(lambda e: e.activation(hid_hi[p][:, :, :], relu_buf[p][:, :, :], ACT.Square), r, y_tok)
                t = dve(lambda e: e.tensor_tensor(sq_buf[p][:, :, :], relu_buf[p][:, :, :], relu_buf[p][:, :, :],
                                                  ALU.mult), r)
                lo = dve(lambda e: e.tensor_tensor(hid_lo[p][:, :, :], sq_buf[p][:, :, :],
                                                   hid_hi[p][:, :, :].bitcast(F32), ALU.subtract), h, t, y_tok)
                return lo

            done = up_down(tag, ready, y_read, D_FF // 256, 2, evac_up, (hid_hi, hid_lo), in_loop, after_first)
            state["arena_free"] = everything()
            return done

        def ada_step(k, k_col, g, extra):
            n = ada_state["n"]
            a = ada_acc[:, g * CW:(g + 1) * CW]
            landed = Tok(ada_full[n % N_ADA_RING], (n // N_ADA_RING + 1) * 16, q.loop, 16 if q.loop else None)
            ada_state["n"] += 1
            r = n % N_ADA_RING
            if k == 0:
                return q.add("dve", lambda e: e.tensor_scalar(a, ada_raw[r][:, :], c_act[:, 0:1], None, ALU.mult),
                             [landed, extra], ada_used)
            return q.add("dve", lambda e: e.scalar_tensor_tensor(out=a, in0=ada_raw[r][:, :], scalar=k_col(), in1=a,
                                                                 op0=ALU.mult, op1=ALU.add), [landed, extra], ada_used)

        def gate_plus_one(layer, which):
            return dve(lambda e: e.tensor_scalar(gate1[:, :], mod(layer, which), 1.0, None, ALU.add),
                       ada_state["mods"], state.get("z"))

        state["arena_free"] = everything()
        gt = gate_plus_one(0, 2)
        ready = layer_norm_stage(0, y_done, gt, mod(0, 4), mod(0, 3), ada_state["mods"])
        n_groups = ADA_COLS // CW

        def ada_first():
            ada_state["g"] = [ada_step(0, None, g, ada_state["summed"]) for g in range(n_groups)]

        def ada_loop(loop):
            for g in range(n_groups):
                lag = Lag()
                t = ada_step(1, lambda: c_act[:, bass.ds(loop.i + 1, 1)], g, [lag, ada_state["g"][g]])
                lag.bind(t)
                ada_state["tok"] = t

        y_done = mlp("mlp0", ready, state["z"], ada_loop, ada_first)
        ada_state["n"] = DEPTH * ADA_CHUNKS
        gt = gate_plus_one(0, 5)
        for g in range(n_groups):
            mods_of(1, g)
        state["ps_free"] = [state["ps_free"], ada_state["mods"]]
        ready = layer_norm_stage(1, y_done, gt, mod(1, 1), mod(1, 0), ada_state["mods"])

        def attention(tag, qs, ks, vs, n_heads, bias_of, out_tile, s_sb, pt_sb, stats, free):
            h_of = {}
            s_ps = [ps[:, 2 + i, 0:3 * P] for i in range(2)]
            pt_ps = [ps[:, 4 + i, 0:3 * P].rearrange("p (a n) -> p a n", a=3) for i in range(2)]
            o_ps = [ps[:, 6 + i, 0:S] for i in range(2)]
            n_pt = len(pt_sb)

            def part(h):
                p0 = HD * (h % 2)
                return slice(p0, p0 + HD), h // 2

            def scores(h, q_tok):
                rows, n = part(h)
                sp, s = s_ps[h % 2], s_sb[h % 2]
                old = h_of.get(h - 2, {})
                pe(lambda e: e.matmul(sp[:, 0:P], qs[rows, n, 0:P], ks[rows, n, 0:P], start=True, stop=True,
                                      skip_group_check=True), q_tok, old.get("biased"), free)
                mm = pe(lambda e: e.matmul(sp[:, P:3 * P], qs[rows, n, P:S], ks[rows, n, :], start=True, stop=True,
                                           skip_group_check=True), inc=True)
                b0, b1, b_tok = bias_of(h)
                t0 = dve(lambda e: e.scalar_tensor_tensor(out=s[:, 0:P], in0=sp[:, 0:P], scalar=HD ** -0.5, in1=b0,
                                                          op0=ALU.mult, op1=ALU.add), mm, b_tok, old.get("turned"), free)
                t1 = dve(lambda e: e.scalar_tensor_tensor(out=s[:, P:3 * P], in0=sp[:, P:3 * P], scalar=HD ** -0.5,
                                                          in1=b1, op0=ALU.mult, op1=ALU.add), mm, b_tok)
                st = stats[h % 2]
                m0 = dve(lambda e: e.tensor_reduce(st[:, 0:1], s[:, 0:P], AX.X, ALU.max, negate=True), t0,
                         old.get("scaled"))
                m1 = dve(lambda e: e.tensor_reduce(st[:, 1:2], s[:, P:3 * P], AX.X, ALU.max, negate=True), t1)
                e0 = act(lambda e: e.activation(s[:, 0:P], s[:, 0:P], ACT.Exp, bias=st[:, 0:1],
                                                accum_out=st[:, 2:3]), m0)
                e1 = act(lambda e: e.activation(s[:, P:3 * P], s[:, P:3 * P], ACT.Exp, bias=st[:, 1:2],
                                                accum_out=st[:, 3:4]), m1)
                r = dve(lambda e: e.reciprocal(st[:, 4:6], st[:, 2:4]), e0, e1)
                p0 = dve(lambda e: e.tensor_scalar(s[:, 0:P], s[:, 0:P], st[:, 4:5], None, ALU.mult), r)
                p1 = dve(lambda e: e.tensor_scalar(s[:, P:3 * P], s[:, P:3 * P], st[:, 5:6], None, ALU.mult), r)
                h_of[h] = {"biased": [t0, t1], "scaled": [p0, p1]}

            def turn(h):
                s, pp = s_sb[h % 2], pt_ps[h % 2]
                old = h_of.get(h - 2, {})
                for a in range(3):
                    t = pe(lambda e, a=a: e.matmul(pp[:, a, :], s[:, a * P:(a + 1) * P], ident[:, :], is_transpose=True,
                                                   start=True, stop=True, skip_group_check=True),
                           h_of[h]["scaled"], old.get("pt"), free, inc=True if a == 2 else None)
                h_of[h]["turned"] = t
                h_of[h]["pt"] = act(lambda e: e.activation(pt_sb[h % n_pt], pp, ACT.Copy), t,
                                    h_of.get(h - n_pt, {}).get("pv"), free)

            def values(h, v_tok):
                rows, n = part(h)
                o, pt = o_ps[n % 2][rows, :], pt_sb[h % n_pt]
                vh = slice(h * HD, (h + 1) * HD)
                old = h_of.get(("out", n - 2))
                pe(lambda e: e.matmul(o[:, 0:P], vs[:, 0, vh], pt[:, 0, :], start=True, stop=False,
                                      skip_group_check=True), v_tok, h_of[h]["pt"], old, free)
                pe(lambda e: e.matmul(o[:, P:S], vs[:, 0, vh], pt[:, 1, :], start=False, stop=False,
                                      skip_group_check=True))
                h_of[h]["pv"] = t = pe(lambda e: e.matmul(o[:, P:S], vs[:, 1, vh], pt[:, 2, :], start=False, stop=True,
                                                          skip_group_check=True), inc=True)
                if h % 2:
                    h_of[("out", n)] = out_tile(n, o_ps[n % 2], [t, h_of[h - 1]["pv"]])
                    return h_of[("out", n)]

            return scores, turn, values

        ar = Arena("att")
        at_q, at_k = ar("q", [P, KT, S]), ar("k", [P, KT, S])
        at_v = ar("v", [P, ST, D])
        at_s = [ar(f"s{i}", [P, 3 * P]) for i in range(2)]
        N_PT = 8
        at_pt = [ar(f"pt{i}", [P, 3, P]) for i in range(N_PT)]
        N_BIAS = 4
        at_bias = [ar(f"bias{i}", [P, S]) for i in range(N_BIAS)]
        at_st = [ar(f"st{i}", [P, 8]) for i in range(2)]
        arena_free = state["arena_free"]
        masked = []
        box = {}

        def load_bias(h, free):
            r = h % N_BIAS
            t = q.add("pool", lambda e: e.dma_start(at_bias[r][:, :], rel_bias[h]), free, bias_full[r], 16)
            masked.append(pool(lambda e: e.memset(at_bias[r][0:CHUNK, S - CHUNK:S], NEG), t))

        for h in range(N_BIAS):
            load_bias(h, [arena_free])

        def evac_bias(dst, first):
            def evac(b, done, s):
                t = act(lambda e: e.activation(dst[:, first % KT, :], b[:, 0, :], ACT.Identity,
                                               bias=v_of("att_b", first)), done, arena_free)
                t2 = q.add("act", lambda e: e.activation(dst[:, first % KT + 1, :], b[:, 1, :], ACT.Identity,
                                                         bias=v_of("att_b", first + 1)), [done, arena_free], s)
                box.setdefault("qk", []).extend([t, t2])
            return evac

        for n in range(8):
            project(evac_bias(at_q if n < 4 else at_k, 2 * n), ready=ready if n == 0 else None)

        def out_tile1(n, o, toks):
            in_done = Tok(chunk_done, box["in_done"])
            h = act(lambda e: e.activation(act_hi[:, n, :], o, ACT.Identity, bias=v_of("att_b", 16 + n)), toks, in_done)
            t = dve(lambda e: e.tensor_scalar(square[:, n, :], o, v_of("att_b", 16 + n), None, ALU.add), toks, h,
                    state["dev_free"])
            return [h, dve(lambda e: e.tensor_tensor(act_lo[:, n, :], square[:, n, :],
                                                     act_hi[:, n, :].bitcast(F32), ALU.subtract), h, t, in_done), t]

        def bias1(h):
            b = at_bias[h % N_BIAS]
            return b[:, P:S], b[:, :], masked[h]

        scores, turn, values = attention("att", at_q, at_k, at_v, ATT_H, bias1, out_tile1, at_s,
                                         [x[:, :, :] for x in at_pt], at_st, [arena_free, state["ps_free"]])

        def scores1(h):
            scores(h, box["qk"])
            if h + N_BIAS < ATT_H:
                load_bias(h + N_BIAS, [Tok(q.done["dve"], q.count[q.done["dve"]])])

        for n in range(4):
            scores1(2 * n)
            scores1(2 * n + 1)

            def evac_v1(b, done, s, n=n):
                box.setdefault("v", []).append(q.add("act", lambda e: e.activation(
                    at_v[:, :, n * 256:(n + 1) * 256], b, ACT.Copy), [done, arena_free], s))
            project(evac_v1, token_major=True, cols=256)
            turn(2 * n)
            turn(2 * n + 1)
        box["in_done"] = stream["j"]
        att_ready = []
        scores1(8)
        for h in range(8, ATT_H):
            if h + 1 < ATT_H:
                scores1(h + 1)
            t = values(h - 8, box["v"])
            att_ready += [t] if t else []
            turn(h)
        for h in range(8, ATT_H):
            t = values(h, box["v"])
            att_ready += [t] if t else []
        fr = everything()
        y_done = out_projection(att_ready, waits=[fr])
        state["arena_free"] = fr
        gt = gate_plus_one(1, 2)
        state["dev_free"] = [state["dev_free"], att_ready]
        state["ps_free"] = [state["ps_free"], fr]
        ready = layer_norm_stage(2, y_done, gt, mod(1, 4), mod(1, 3), ada_state["mods"])
        y_done = mlp("mlp1", ready, state["z"])
        gt = gate_plus_one(1, 5)
        layer_norm_stage(3, y_done, gt, None, None, None)

        z = [dve(lambda e, k=k: e.tensor_copy(dev[:, k, :], res[:, k, :]), state["x"][k]) for k in range(KT)]
        state["ps_free"] = [state["ps_free"], state["x"]]
        ready, _ = rms_stage("norm_mix", z)

        ar = Arena("mix")
        arena_free = state["arena_free"]
        m_tab = ar("rope", [P, 2 * S + P])
        m_cnt = ar("cnt", [P, 4, 16])
        m_pw = ar("pw", [P, 4, P])
        iq_at = ar.at
        m_iq = ar("iq", [P, 4, S])
        up_at = ar.at
        m_up = ar("up", [P, 4, S])
        m_ik = ar("ik", [P, S])
        m_iw = ar("iw", [P, ST, IDX_H])
        m_q, m_k = ar("q", [P, 4, S]), ar("k", [P, 4, S])
        m_v = ar("v", [P, ST, 512])
        m_mix_hi, m_mix_lo = ar("mix_hi", [P, 4, S], F32R), ar("mix_lo", [P, 4, S], F32R)
        m_score, m_mask = ar("score", [P, 3 * P]), ar("mask", [P, 3 * P])
        m_top = ar("top", [P, 2, 8])
        m_s = [ar(f"s{i}", [P, 3 * P]) for i in range(2)]
        m_st = [ar(f"st{i}", [P, 8]) for i in range(2)]
        m_ptb = ar("ptb", [P, 6 * 3 * P])
        m_pt = [m_ptb[:, i * 3 * P:(i + 1) * 3 * P].rearrange("p (a n) -> p a n", a=3) for i in range(6)]
        rope_tmp = [m_ptb[:, i * 512:(i + 1) * 512].rearrange("p (a n) -> p a n", a=2) for i in range(2)]
        relu_tmp = [m_ptb[:, 1024 + i * 384:1024 + (i + 1) * 384] for i in range(2)]
        m_o_hi = nc.alloc_sbuf_tensor_at("mix_o_hi", [P, 4, S], F32R, offset=iq_at)
        m_o_lo = nc.alloc_sbuf_tensor_at("mix_o_lo", [P, 4, S], F32R, offset=up_at)
        t_tab = [q.add("pool", lambda e, a=a, b=b: e.dma_start(a, b), [arena_free], s, 16)
                 for a, b, s in ((m_tab[:, :], rope, tables_in[0]), (m_cnt[:, :, :], pool_count, tables_in[1]),
                                 (m_pw[:, :, :], pool_w, tables_in[2]))]
        cos_t, sin_t, rot_t = m_tab[:, 0:S], m_tab[:, S:2 * S], m_tab[:, 2 * S:2 * S + P]
        m_ps_free = state["ps_free"]
        box = {}

        j, hi, lo = next_chunk()
        wide = 2 * HD + IDX_H
        wh, wl = (w[:, 0:KT * wide].rearrange("p (k n) -> p k n", k=KT) for w in (hi, lo))
        w = stream["bank"]
        stream["bank"] += 1
        b = w % 2
        groups = []
        for k in range(KT):
            groups.append((work[b][:, 0:S], wh[:, k, 0:P], act_hi[:, k, :], k == 0, 0, ready[k]))
            groups.append((work[b][:, 0:S], wh[:, k, 0:P], act_lo[:, k, :], False, 0, ()))
        for t in range(ST):
            c = slice(t * P, (t + 1) * P)
            o = work[b][:, S + 8 * t:S + 8 * t + 8]
            for k in range(KT):
                groups.append((o, act_hi[:, k, c], wh[:, k, P:P + 8], False, 0, ()))
                groups.append((o, act_lo[:, k, c], wh[:, k, P:P + 8], False, 0, ()))
        for k in range(KT):
            groups.append((work[b][:, 0:S], wl[:, k, 0:P], act_hi[:, k, :], False, 2 if k == 0 else 1, ()))
        for t in range(ST):
            for k in range(KT):
                groups.append((work[b][:, S + 8 * t:S + 8 * t + 8], act_hi[:, k, t * P:(t + 1) * P],
                               wl[:, k, P:P + 8], False, 1, ()))
        done = chunk_products(j, groups, waits=[Tok(bank_free[b], w // 2)])
        ik_t = act(lambda e: e.activation(m_ik[:, :], work[b][:, 0:S], ACT.Copy), done, arena_free)
        iw_t = q.add("act", lambda e: e.activation(m_iw[:, :, :], work[b][:, S:S + 16].rearrange("p (t h) -> p t h", t=2),
                                                   ACT.Copy, scale=IDX_H ** -0.5), [done, arena_free], bank_free[b])

        rope_state = {"free": [m_ps_free, arena_free]}

        def rope_tiles(x, n, tok):
            rp = ps[:, 7, 0:n * S].rearrange("p (a t) -> p a t", a=n)
            mm = pe(lambda e: e.matmul(rp, rot_t, x, start=True, stop=True, skip_group_check=True), tok, t_tab,
                    rope_state["free"], inc=True)
            a, b = rope_tmp[0][:, 0:n, :], rope_tmp[1][:, 0:n, :]
            cb, sbb = (v.unsqueeze(1).broadcast_to([P, n, S]) for v in (cos_t, sin_t))
            t1 = dve(lambda e: e.tensor_tensor(a, x, cb, ALU.mult), tok, t_tab, rope_state["free"])
            t2 = dve(lambda e: e.tensor_tensor(b, rp, sbb, ALU.mult), mm)
            t3 = dve(lambda e: e.tensor_tensor(x, a, b, ALU.add), t1, t2)
            rope_state["free"] = [t3]
            return t3

        def evac_plain(dst, first, key, n=2):
            def evac(b, done, s):
                box.setdefault(key, []).append(q.add("act", lambda e: e.activation(
                    dst[:, first:first + n, :], b[:, 0:n, :], ACT.Copy), [done, arena_free], s))
            return evac

        background = []

        def drip(n):
            for _ in range(min(n, len(background))):
                background.pop(0)()

        project(evac_plain(m_iq, 0, "iq"))
        ik_t = rope_tiles(m_ik[:, :].unsqueeze(1), 1, ik_t)
        project(evac_plain(m_iq, 2, "iq"))
        iq_t = [rope_tiles(m_iq[:, 0:2, :], 2, box["iq"][0])]
        project(evac_plain(m_q, 0, "q"))
        iq_t.append(rope_tiles(m_iq[:, 2:4, :], 2, box["iq"][1]))

        idx = {}

        def index_scores(h):
            rows = slice(HD * (h % 2), HD * (h % 2) + HD)
            sp = ps[:, 2 + h % 2, 0:3 * P]
            rel = relu_tmp[h % 2]
            n = h // 2
            old = idx.get(h - 2, {})
            pe(lambda e: e.matmul(sp[:, 0:P], m_iq[rows, n, 0:P], m_ik[rows, 0:P], start=True, stop=True,
                                  skip_group_check=True), iq_t[n // 2], ik_t, old.get("relu"), m_ps_free)
            mm = pe(lambda e: e.matmul(sp[:, P:3 * P], m_iq[rows, n, P:S], m_ik[rows, :], start=True, stop=True,
                                       skip_group_check=True), inc=True)
            r = act(lambda e: e.activation(rel, sp, ACT.Relu, scale=HD ** -0.5), mm, old.get("sum"), arena_free)
            t = []
            for a, cols in ((0, slice(0, P)), (1, slice(P, 3 * P))):
                w = m_iw[:, a, h:h + 1]
                if h == 0:
                    t.append(dve(lambda e, w=w, cols=cols: e.tensor_scalar(m_score[:, cols], rel[:, cols], w, None,
                                                                           ALU.mult), r, iw_t, arena_free))
                else:
                    t.append(dve(lambda e, w=w, cols=cols: e.scalar_tensor_tensor(
                        out=m_score[:, cols], in0=rel[:, cols], scalar=w, in1=m_score[:, cols], op0=ALU.mult,
                        op1=ALU.add), r, idx[h - 1]["sum"]))
            idx[h] = {"relu": r, "sum": t, "mm": mm}

        for h in range(4):
            index_scores(h)
        project(evac_plain(m_q, 2, "q"))
        for h in range(4, IDX_H):
            index_scores(h)

        causal = []
        for a, cols, n in ((0, slice(0, P), P), (1, slice(P, 3 * P), S)):
            causal.append(pool(lambda e, cols=cols, n=n, a=a: e.affine_select(
                out=m_score[:, cols], in_=m_score[:, cols], compare_op=ALU.is_ge, fill=NEG, base=a * P,
                pattern=[[-1, n]], channel_multiplier=1), idx[IDX_H - 1]["sum"][a]))
        top_state = {"t": list(causal)}

        def top_max(a, cols):
            def f():
                top_state["t"][a] = dve(lambda e: e.max(m_top[:, a, :], m_score[:, cols]), top_state["t"][a])
            return f

        def top_mark(a, cols):
            def f():
                top_state["t"][a] = dve(lambda e: e.match_replace(m_score[:, cols], m_top[:, a, :], m_score[:, cols],
                                                                  TAKEN), top_state["t"][a])
            return f

        halves = ((0, slice(0, P)), (1, slice(P, 3 * P)))
        for _ in range(TOPK // 8):
            background += [top_max(*x) for x in halves] + [top_mark(*x) for x in halves]
        project(evac_plain(m_k, 0, "k"))
        q_t = [rope_tiles(m_q[:, 0:2, :], 2, box["q"][0])]
        drip(6)
        project(evac_plain(m_k, 2, "k"))
        q_t.append(rope_tiles(m_q[:, 2:4, :], 2, box["q"][1]))
        drip(5)
        for n in range(2):
            def evac_v2(b, done, s, n=n):
                box.setdefault("v", []).append(q.add("act", lambda e: e.activation(
                    m_v[:, :, n * 256:(n + 1) * 256], b, ACT.Copy), [done, arena_free], s))
            project(evac_v2, token_major=True, cols=256)
            q_t.append(rope_tiles(m_k[:, 2 * n:2 * n + 2, :], 2, box["k"][n]))
            drip(6)
        for n in range(2):
            project(evac_plain(m_up, 2 * n, "up"))
            drip(6)
        drip(99)
        t = dve(lambda e: e.tensor_scalar(m_mask[:, :], m_score[:, :], TAKEN / 2, NEG, ALU.is_gt, ALU.mult),
                top_state["t"], arena_free)
        mask_t = [pool(lambda e, cols=cols, n=n, a=a: e.affine_select(
            out=m_mask[:, cols], in_=m_mask[:, cols], compare_op=ALU.is_ge, fill=NEG, base=a * P,
            pattern=[[-1, n]], channel_multiplier=1), t) for a, cols, n in ((0, slice(0, P), P), (1, slice(P, 3 * P), S))]

        gates_t = []
        gate_free = state["dev_free"]

        def evac_gate(n):
            def evac(b, done, s):
                g = (dev if n < 4 else square)[:, (2 * n) % KT:(2 * n) % KT + 2, :]
                t = q.add("act", lambda e: e.activation(g, b, ACT.Exp, scale=-1.0), [done, gate_free], s)
                t = dve(lambda e: e.tensor_scalar(g, g, 1.0, None, ALU.add), t)
                gates_t.append(dve(lambda e: e.reciprocal(g, g), t))
            return evac

        def out_tile2(n, o, toks):
            h = act(lambda e: e.activation(m_o_hi[:, n, :], o, ACT.Copy), toks, iq_done, up_done)
            return [h, dve(lambda e: e.tensor_tensor(m_o_lo[:, n, :], o, m_o_hi[:, n, :].bitcast(F32), ALU.subtract),
                           h)]

        scores, turn, values = attention(
            "att2", m_q, m_k, m_v, ATT2_H, lambda h: (m_mask[:, 0:P], m_mask[:, P:3 * P], mask_t), out_tile2, m_s,
            m_pt, m_st, [rope_state["free"], idx[IDX_H - 1]["sum"], idx[IDX_H - 2]["relu"], idx[IDX_H - 1]["relu"]])
        iq_done = [idx[IDX_H - 1]["mm"]]

        def pool_group(g, first_tok):
            u = m_up[:, g, :]
            a, t = u, first_tok
            bufs = [rstd[:, :], pool_tmp[:, :]]
            for i in range(g + 1):
                sh = 1 << i
                o = bufs[i % 2]
                t1 = dve(lambda e, o=o, a=a, sh=sh: e.tensor_tensor(o[:, sh:S], a[:, sh:S], a[:, 0:S - sh], ALU.add), t)
                t2 = dve(lambda e, o=o, a=a, sh=sh: e.tensor_copy(o[:, 0:sh], a[:, 0:sh]), t)
                a, t = o, [t1, t2]
            o = bufs[(g + 1) % 2]
            t1 = dve(lambda e: e.tensor_tensor(o[:, 0:16], a[:, 0:16], m_cnt[:, g, :], ALU.mult), t, t_tab)
            t2 = dve(lambda e: e.tensor_tensor(u[:, 0:16], o[:, 0:16], u[:, 0:16], ALU.subtract), t1)
            t3 = dve(lambda e: e.scalar_tensor_tensor(out=u[:, 16:S], in0=a[:, 16:S], scalar=1.0 / POOL_WINDOWS[g],
                                                      in1=u[:, 16:S], op0=ALU.mult, op1=ALU.subtract), t)
            return [t2, t3]

        pool_tmp = ar("pool_tmp", [P, S])
        pooled, prev_t = [], [box["up"], arena_free]
        for g in range(4):
            prev_t = pool_group(g, prev_t)
            pooled.append(prev_t)
        mix_ready, pool_mm = [], []
        for half in range(2):
            mp = ps[:, 6 + half, :].rearrange("p (a t) -> p a t", a=2)
            for i in range(2):
                g = 2 * half + i
                t = pe(lambda e, g=g, i=i, mp=mp: e.matmul(mp[:, i, :], m_pw[:, g, :], m_up[:, g, :], start=True,
                                                           stop=True, skip_group_check=True),
                       pooled[g], t_tab, rope_state["free"], m_ps_free, inc=True if i else None)
            pool_mm.append(t)
            rounded = [act(lambda e, g=g, i=i, mp=mp: e.activation(m_mix_hi[:, g, :], mp[:, i, :], ACT.Copy,
                                                                scale=v_of("pool_scale", g)), t, arena_free)
                       for i, g in enumerate((2 * half, 2 * half + 1))]
            for i in range(2):
                g = 2 * half + i
                h = rounded[i]
                t1 = dve(lambda e, g=g, i=i, mp=mp: e.tensor_scalar(rstd[:, :], mp[:, i, :], v_of("pool_scale", g), None,
                                                                    ALU.mult), rounded, prev_t)
                prev_t = dve(lambda e, g=g: e.tensor_tensor(m_mix_lo[:, g, :], rstd[:, :],
                                                            m_mix_hi[:, g, :].bitcast(F32), ALU.subtract), h, t1, arena_free)
                mix_ready.append([h, prev_t])
        up_done = [pool_mm, [x for r in mix_ready for x in r]]

        att2_ready = []
        for n in range(8):
            if n == 0:
                scores(0, q_t)
            if n + 1 < ATT2_H:
                scores(n + 1, q_t)
            project(evac_gate(n))
            turn(n)
            if n:
                t = values(n - 1, [box["v"], up_done])
                att2_ready += [t] if t else []
        att2_ready.append(values(7, box["v"]))
        y_free = everything()

        def accumulate_all(m, ready, waits):
            for n in range(2):
                done = accumulate(y_tiles(4 * n, 4), m, nk=4, wide=512, waits=waits if n == 0 else (),
                                  ready=ready if n == 0 else None)
            return done

        y1 = accumulate_all((m_mix_hi, m_mix_lo), mix_ready, [y_free])
        prod = [dve(lambda e, h=h: e.tensor_tensor(dev[:, 4 * h:4 * h + 4, :], dev[:, 4 * h:4 * h + 4, :],
                                                   y_acc[:, 4 * h:4 * h + 4, :], ALU.mult), y1, gates_t)
                for h in range(2)]
        y2 = accumulate_all((m_o_hi, m_o_lo), att2_ready, [prod])
        in_done = Tok(chunk_done, stream["j"] - 4)
        merged_ready, prod2 = [], []
        for h in range(4):
            c = slice(2 * h, 2 * h + 2)
            t = dve(lambda e, c=c: e.tensor_tensor(square[:, c, :], square[:, c, :], y_acc[:, c, :], ALU.mult), y2,
                    gates_t)
            prod2.append(t)
            t = dve(lambda e, c=c: e.tensor_tensor(dev[:, c, :], dev[:, c, :], square[:, c, :], ALU.add), t, prod)
            r = split_activation(dev[:, c, :], 0, act_hi[:, c, :], act_lo[:, c, :], t, free=[in_done])
            merged_ready += [r, r]
        y_done = out_projection(merged_ready, waits=[prod2])
        state["arena_free"] = everything()

        z = residual([y_done], None, [[] for _ in range(KT)], 1.0, [x for r in merged_ready for x in r])
        keep = [act(lambda e, k=k: e.activation(res[:, k, :], dev[:, k, :], ACT.Copy), z[k]) for k in range(KT)]
        state["ps_free"] = [state["ps_free"], state["arena_free"]]
        ready, _ = rms_stage("norm_ffn", [[z[k], keep[k]] for k in range(KT)])

        ar = Arena("conv")
        cv = [ar(f"cv{i}", [P, 2, S]) for i in range(2)]
        sig = [ar(f"sig{i}", [P, S]) for i in range(2)]
        hid_hi = [ar(f"hi{i}", [P, 1, S], F32R) for i in range(2)]
        hid_lo = [ar(f"lo{i}", [P, 1, S], F32R) for i in range(2)]
        arena_free = state["arena_free"]

        def evac_conv(block, p, b, done, s, y_tok, split_tok):
            def col(name, half, tap=0):
                first = VEC[name] + 2 * FT2 * tap + FT2 * half
                if isinstance(block, int):
                    return vec[:, first + block:first + block + 1]
                return vec[:, bass.ds(block() + first, 1)]

            t = [act(lambda e, x=x: e.activation(cv[p][:, x, :], b[:, x, :], ACT.Identity, bias=col("conv_b", x),
                                                 scale=col("conv_w", x, 2)), done, split_tok, arena_free)
                 for x in range(2)]
            t1 = [dve(lambda e, x=x: e.scalar_tensor_tensor(
                out=cv[p][:, x, 1:S], in0=b[:, x, 0:S - 1], scalar=col("conv_w", x, 1), in1=cv[p][:, x, 1:S],
                op0=ALU.mult, op1=ALU.add), t) for x in range(2)]
            a = dve(lambda e: e.scalar_tensor_tensor(
                out=cv[p][:, 0, 2:S], in0=b[:, 0, 0:S - 2], scalar=col("conv_w", 0, 0), in1=cv[p][:, 0, 2:S],
                op0=ALU.mult, op1=ALU.add), t1[0])
            bb = q.add("dve", lambda e: e.scalar_tensor_tensor(
                out=cv[p][:, 1, 2:S], in0=b[:, 1, 0:S - 2], scalar=col("conv_w", 1, 0), in1=cv[p][:, 1, 2:S],
                op0=ALU.mult, op1=ALU.add), [t1[1]], s)
            ex = act(lambda e: e.activation(sig[p][:, :], cv[p][:, 0, :], ACT.Exp, scale=-1.0), a, split_tok)
            t = dve(lambda e: e.tensor_scalar(sig[p][:, :], sig[p][:, :], 1.0, None, ALU.add), ex)
            t = dve(lambda e: e.reciprocal(sig[p][:, :], sig[p][:, :]), t)
            t = dve(lambda e: e.tensor_tensor(cv[p][:, 0, :], cv[p][:, 0, :], sig[p][:, :], ALU.mult), t, a)
            t = dve(lambda e: e.tensor_tensor(cv[p][:, 0, :], cv[p][:, 0, :], cv[p][:, 1, :], ALU.mult), t, bb)
            h = act(lambda e: e.activation(hid_hi[p][:, 0, :], cv[p][:, 0, :], ACT.Copy), t, y_tok)
            return dve(lambda e: e.tensor_tensor(hid_lo[p][:, 0, :], cv[p][:, 0, :], hid_hi[p][:, 0, :].bitcast(F32),
                                                 ALU.subtract), h, t, y_tok)

        y_done = up_down("conv", ready, z, FT2, 1, evac_conv, (hid_hi, hid_lo))

        z = residual([y_done], None, [[k] for k in keep], 1.0, state["dev_free"])
        _, xs = rms_stage("norm_final", z, next_u=False)
        for h in range(4):
            t = q.add("sp", lambda e, h=h: e.dma_start(out[:, 2 * h:2 * h + 2, :], res[:, 2 * h:2 * h + 2, :]),
                      [xs[2 * h], xs[2 * h + 1]], stored, 16)
        assert stream["j"] == len(SIZES), (stream["j"], len(SIZES))
        q.items["sp"].append((lambda e: None, [t], None, 0, None))

        block = ctx.enter_context(nc.Block())

        @block.sync
        def _(e):
            q.emit("sp", e)

        @block.tensor
        def _(e):
            q.emit("pe", e)

        @block.scalar
        def _(e):
            q.emit("act", e)

        @block.vector
        def _(e):
            q.emit("dve", e)

        @block.gpsimd
        def _(e):
            q.emit("pool", e)


def _tiles(w, c0, n, k0=0, nk=KT):
    return w[k0 * P:(k0 + nk) * P, c0:c0 + n].reshape(nk, P, n).transpose(1, 0, 2).reshape(P, nk * n)


def _weights(a):
    parts = []
    w = a["gla_w_in"][0]
    qk, v0 = 2 * GLA_H * GLA_DK, 2 * GLA_H * GLA_DK + D
    gk = np.concatenate([w[:, v0 + D:], np.zeros((D, P - GLA_RANK), np.float32)], 1)
    parts.append(_tiles(gk, 0, P))
    parts += [_tiles(w, c, 256) for c in range(0, qk + 2 * D, 256)]
    parts += [_tiles(a["gla_w_out"][0], c, 256) for c in range(0, D, 256)]

    def mlp(w1, w2):
        n = D_FF // 256
        up = [_tiles(w1, 256 * i, 256) for i in range(n)]
        down = [_tiles(w2, 0, D, 2 * i, 2) for i in range(n)]
        out = [up[0]]
        for i in range(1, n):
            out += [up[i], down[i - 1]]
        return out + [down[-1]]

    parts += mlp(a["ff_w1"][0], a["ff_w2"][0])
    parts += [_tiles(a["att_w_in"][0], c, 256) for c in range(0, 3 * D, 256)]
    parts += [_tiles(a["att_w_out"][0], c, 256) for c in range(0, D, 256)]
    parts += mlp(a["ff_w1"][1], a["ff_w2"][1])
    w = a["w_in_2"][0]
    o_pool, o_q, o_k, o_v, o_iq, o_ik, o_iw, o_g = 0, 512, 1024, 1536, 2048, 2560, 2624, 2632
    ik = w[:, o_ik:o_ik + HD]
    parts.append(_tiles(np.concatenate([ik, ik, w[:, o_iw:o_iw + IDX_H]], 1), 0, 2 * HD + IDX_H))
    for o in (o_iq, o_q, o_k, o_v, o_pool):
        parts += [_tiles(w, o + c, 256) for c in (0, 256)]
    parts += [_tiles(w, o_g + c, 256) for c in range(0, 2 * D, 256)]
    for name in ("w_pool_proj_2", "w_attn_proj_2"):
        parts += [_tiles(a[name][0], c, 512, 0, 4) for c in (0, 512)]
    parts += [_tiles(a["w_out_2"][0], c, 256) for c in range(0, D, 256)]
    w = a["w_up_2"][0]
    up = [_tiles(np.concatenate([w[:, f * P:(f + 1) * P], w[:, D_FF2 + f * P:D_FF2 + (f + 1) * P]], 1), 0, 256)
          for f in range(FT2)]
    down = [_tiles(a["w_down_2"][0], 0, D, f, 1) for f in range(FT2)]
    parts.append(up[0])
    for f in range(1, FT2):
        parts += [up[f], down[f - 1]]
    parts.append(down[-1])
    out = np.zeros((len(parts), P, CW), np.float32)
    for j, x in enumerate(parts):
        assert x.shape[1] == SIZES[j], (j, x.shape, SIZES[j])
        out[j, :, :x.shape[1]] = x
    return out


def _ada(w):
    t = w.reshape(DEPTH, KT, P, ADA_COLS // CW, CW)
    return np.ascontiguousarray(np.concatenate(
        [t[0].transpose(2, 0, 1, 3).reshape(ADA_CHUNKS, P, CW), t[1].transpose(0, 2, 1, 3).reshape(ADA_CHUNKS, P, CW)]))


def _cols(v):
    return np.ascontiguousarray(v).reshape(-1, P).T


def _rope_tables():
    half = ROT // 2
    inv = np.float32(1.0) / (np.float32(ROPE_THETA) ** (np.arange(half, dtype=np.float32) * np.float32(2.0)
                                                         / np.float32(ROT)))
    ang = (np.arange(S, dtype=np.float32)[:, None] * inv.astype(np.float32)[None, :]).astype(np.float32)
    cos, sin = np.cos(ang.astype(np.float64)).T, np.sin(ang.astype(np.float64)).T
    t = np.zeros((P, 2 * S + P), np.float32)
    t[:, 0:S] = 1.0
    for h in range(2):
        for x in range(2):
            r = slice(HD * h + half * x, HD * h + half * (x + 1))
            t[r, 0:S] = cos
            t[r, S:2 * S] = sin
        for i in range(half):
            t[HD * h + half + i, 2 * S + HD * h + i] = -1.0
            t[HD * h + i, 2 * S + HD * h + half + i] = 1.0
    return t


def kernel(**inputs):
    import concourse.bacc as bacc
    from concourse.bass_utils import run_bass_kernel_spmd

    a = {k: np.asarray(v) for k, v in inputs.items()}
    vec = np.concatenate([
        _cols(a["c"][0]), _cols(a["b_ada"]), _cols(a["ln_g"]), _cols(a["ln_b"]), _cols(a["gla_b_gk"][0]),
        _cols(a["gla_g_norm"][0]), _cols(a["att_b_in"][0]), _cols(a["pool_scale_2"][0]), _cols(a["norm_mix_g_2"][0]),
        _cols(a["norm_ffn_g_2"][0]), _cols(a["conv_b_2"][0]), _cols(a["conv_w_2"][0]), _cols(a["norm_final_g_2"])], 1)
    key, query = np.arange(S)[None, :], P + np.arange(P)[:, None]
    rel = np.clip(query - key, -MAX_REL, MAX_REL) + MAX_REL
    count = np.zeros((P, 4, 16), np.float32)
    for g, w in enumerate(POOL_WINDOWS):
        count[:, g, :] = 1.0 / np.minimum(np.arange(16) + 1, w)
    arrays = {
        "weights": _weights(a), "ada": _ada(a["w_ada"]), "vecs": np.ascontiguousarray(vec),
        "x_in": np.ascontiguousarray(a["x"][0].T.reshape(KT, P, S).transpose(1, 0, 2)),
        "w_gk2": np.ascontiguousarray(a["gla_w_gk2"][0]),
        "rel_bias": np.ascontiguousarray(a["att_rel_bias"][0][:, rel]),
        "pool_w": np.ascontiguousarray(a["pool_w_2"][0].transpose(1, 0, 2)), "rope": _rope_tables(),
        "pool_count": count,
    }
    nc = bacc.Bacc("TRN2", target_bir_lowering=False, num_devices=1)
    args = [nc.dram_tensor(k, v.shape, mybir.dt.from_np(v.dtype), kind="ExternalInput").ap() for k, v in arrays.items()]
    out = nc.dram_tensor("out", (P, KT, S), F32, kind="ExternalOutput").ap()
    build(nc, *args, out)
    r = run_bass_kernel_spmd(nc, [arrays], core_ids=[0])
    return r.results[0]["out"].transpose(1, 0, 2).reshape(D, S).T.reshape(1, S, D)
```

```python
from contextlib import ExitStack

import numpy as np
import concourse.bass as bass
from concourse import mybir

F32 = mybir.dt.float32
F32R = mybir.dt.float32r
I32 = mybir.dt.int32
ACT = mybir.ActivationFunctionType
ALU = mybir.AluOpType
AX = mybir.AxisListType

P = 128
D = 1024
KT = D // P
S = 256
ST = S // P
DEPTH = 2
CHUNK = 64
NCH = S // CHUNK
GLA_H, GLA_DK, GLA_DV, GLA_RANK = 4, 128, 256, 16
ATT_H, HD = 16, 64
MAX_REL = 128
D_FF = 4096
ALPHA = (2.0 * DEPTH) ** 0.25
LN_EPS, RMS_EPS = 1e-5, 1e-6
NEG = -1e30
TAKEN = -3e38
POOL_WINDOWS = (2, 4, 8, 16)
ATT2_H = 8
IDX_H = 8
ROT = 16
ROPE_THETA = 500000.0
TOPK = min(256, S // 4)
D_FF2 = 2816
FT2 = D_FF2 // P

CW = 2048
N_RAW, N_SPLIT, N_ADA_RING = 4, 2, 3
ADA_COLS = 6 * D
ADA_CHUNKS = KT * ADA_COLS // CW


def chunk_sizes():
    full, out = CW, []
    out += [KT * P] + [full] * 16
    out += [full] * (2 * (D_FF // 256))
    out += [full] * 16
    out += [full] * (2 * (D_FF // 256))
    out += [KT * (2 * HD + IDX_H)] + [full] * (10 + 8)
    out += [full] * 8
    out += [full] + [full, D] * (FT2 - 1) + [D]
    return out


SIZES = chunk_sizes()

VEC_PARTS = [("c", KT), ("b_ada", DEPTH * 48), ("ln_g", 4 * KT), ("ln_b", 4 * KT), ("b_gk", 4),
             ("g_norm", 8), ("att_b", 24), ("pool_scale", 4), ("norm_mix", 8), ("norm_ffn", 8),
             ("conv_b", 2 * FT2), ("conv_w", 3 * 2 * FT2), ("norm_final", 8)]
VEC = {}
_at = 0
for _name, _n in VEC_PARTS:
    VEC[_name] = _at
    _at += _n
N_VEC = _at


class Tok:

    def __init__(self, sem, base, loop=None, step=None):
        self.sem, self.base, self.loop, self.step = sem, base, loop, step

    def value(self, loop, i):
        if self.loop is None:
            return self.base
        step = self.step if self.step is not None else self.loop.per.get(self.sem, 0)
        if self.loop is loop:
            return self.base + step * i
        return self.base + step * (self.loop.n - 1)


class Lag:

    def __init__(self, tok=None, back=1):
        self.tok, self.back = tok, back

    def bind(self, tok):
        self.tok = tok

    @property
    def sem(self):
        return self.tok.sem

    def value(self, loop, i):
        step = self.tok.step if self.tok.step is not None else self.tok.loop.per[self.tok.sem]
        return self.tok.base - step * self.back + step * i


class Loop:
    def __init__(self, n):
        self.n, self.per, self.base, self.i = n, {}, {}, None


class Queues:

    def __init__(self, nc, sem):
        self.nc, self.sem = nc, sem
        self.items = {k: [] for k in ("pe", "act", "dve", "pool", "sp")}
        self.done = {k: sem(f"{k}_done") for k in self.items}
        self.count = {}
        self.loop = None
        self.uses = 4

    def token(self, s, by):
        if self.loop is not None:
            self.loop.base.setdefault(s, self.count.get(s, 0))
            self.loop.per[s] = self.loop.per.get(s, 0) + by
        self.count[s] = self.count.get(s, 0) + by
        return Tok(s, self.count[s], self.loop)

    def add(self, engine, make, waits, inc=None, by=1):
        flat = []

        def spread(ws):
            for w in ws:
                if isinstance(w, (list, tuple)):
                    spread(w)
                elif w is not None:
                    flat.append(w)

        spread(waits)
        s = self.done[engine] if inc is True else inc
        tok = self.token(s, by) if s is not None else None
        self.items[engine].append((make, flat, s, by, self.loop))
        return tok

    def pe(self, make, *waits, inc=None):
        return self.add("pe", make, waits, inc)

    def act(self, make, *waits, inc=True):
        return self.add("act", make, waits, inc)

    def dve(self, make, *waits, inc=True):
        return self.add("dve", make, waits, inc)

    def pool(self, make, *waits, inc=True):
        return self.add("pool", make, waits, inc)

    def repeat(self, n, body):
        loop = Loop(n)
        marks = {k: len(v) for k, v in self.items.items()}
        self.loop = loop
        body(loop)
        self.loop = None
        for s, per in loop.per.items():
            self.count[s] += per * (n - 1)
        for k, v in self.items.items():
            inside = v[marks[k]:]
            if inside:
                v[marks[k]:] = [(loop, inside)]

    def emit(self, name, e):
        seen = {}

        def wait(w, loop):
            inside = loop is not None and w.loop is loop if isinstance(w, Tok) else True
            if inside:
                e.wait_ge(w.sem, w.value(loop, loop.i))
                return
            v = w.value(None, None)
            if seen.get(id(w.sem), 0) < v:
                e.wait_ge(w.sem, v)
                if loop is None:
                    seen[id(w.sem)] = v

        def one(item):
            make, waits, s, by, loop = item
            for w in waits:
                wait(w, loop)
            ins = make(e)
            if s is not None:
                ins.then_inc(s, by)

        for item in self.items[name]:
            if isinstance(item[0], Loop):
                loop, inside = item
                with e.Fori(0, loop.n) as i:
                    loop.i = i
                    for x in inside:
                        one(x)
                loop.i = None
            else:
                one(item)


def build(nc, weights, ada, vecs, x_in, w_gk2, rel_bias, pool_w, rope, pool_count, out):
    with ExitStack() as ctx:
        def sb(name, shape, dt=F32):
            return ctx.enter_context(nc.sbuf_tensor(name, shape, dt))

        def sem(name):
            return ctx.enter_context(nc.semaphore(name))

        weight_raw = [sb(f"weight_raw{i}", [P, CW]) for i in range(N_RAW)]
        weight_hi = [sb(f"weight_hi{i}", [P, CW], F32R) for i in range(N_SPLIT)]
        weight_lo = [sb(f"weight_lo{i}", [P, CW], F32R) for i in range(N_SPLIT)]
        ada_raw = [sb(f"ada_raw{i}", [P, CW]) for i in range(N_ADA_RING)]
        raw_full = [sem(f"raw_full{i}") for i in range(N_RAW)]
        hi_full = [sem(f"hi_full{i}") for i in range(N_SPLIT)]
        lo_full = [sem(f"lo_full{i}") for i in range(N_SPLIT)]
        chunk_done = sem("chunk_done")
        ada_full = [sem(f"ada_full{i}") for i in range(N_ADA_RING)]
        ada_used = sem("ada_used")
        bank_free = [sem(f"bank_free{i}") for i in range(2)]
        vec_in, x_arrived, w2_in = sem("vec_in"), sem("x_arrived"), sem("w2_in")
        tables_in = [sem(f"tables_in{i}") for i in range(3)]
        stored = sem("stored")
        bias_full = [sem(f"bias_full{i}") for i in range(4)]

        ada_acc = sb("ada_acc", [P, ADA_COLS])
        res = sb("res", [P, KT, S])
        dev = sb("dev", [P, KT, S])
        act_hi = sb("act_hi", [P, KT, S], F32R)
        act_lo = sb("act_lo", [P, KT, S], F32R)
        vec = sb("vec", [P, N_VEC])
        mods = [sb(f"mods{i}", [P, 48]) for i in range(DEPTH)]
        norm_scale = sb("norm_scale", [P, 2, KT])
        gate1 = sb("gate1", [P, KT])
        c_act = sb("c_act", [P, KT])
        ident = sb("ident", [P, P])
        ones_d = sb("ones_d", [P, P])
        minus_half = sb("minus_half", [P, ST])
        root = sb("root", [P, 2 * ST])
        rstd = sb("rstd", [P, S])
        diag = rstd[:, :].rearrange("p (t n) -> p t n", t=ST)
        ones_sq = sb("ones_sq", [P, P])
        square = sb("square", [P, KT, S])
        alpha_ln = sb("alpha_ln", [P, 2, KT])
        arena_at = nc.sbuf_base
        arena_end = nc.sbuf_usable_end

        class Arena:

            def __init__(self, tag):
                self.tag, self.at = tag, arena_at

            def __call__(self, name, shape, dt=F32):
                n = 4 * int(np.prod(shape[1:]))
                t = nc.alloc_sbuf_tensor_at(f"{self.tag}_{name}", shape, dt, offset=self.at)
                self.at += (n + 31) // 32 * 32
                assert self.at <= arena_end, (self.tag, name, self.at, arena_end)
                return t

        ps = ctx.enter_context(nc.psum_tensor("ps", [P, 8, 512], F32))
        work = [ps[:, b, :] for b in range(2)]
        y_acc = ps[:, 2:6, :].rearrange("p a (b n) -> p (a b) n", b=2)
        mean_ps = ps[:, 6, 0:S]
        rstd_ps = ps[:, 7, S:2 * S]

        q = Queues(nc, sem)
        pe, act, dve, pool = q.pe, q.act, q.dve, q.pool

        def v_of(name, n=0):
            return vec[:, VEC[name] + n:VEC[name] + n + 1]

        stream = {"j": 0, "bank": 0}

        def at_chunk(s, j, slots, unit):
            step = 4 // slots * unit if q.loop else None
            return Tok(s, (j // slots + 1) * unit, q.loop, step)

        def split(j):
            size = SIZES[j]
            r, h = j % N_RAW, j % N_SPLIT
            free = Tok(chunk_done, j - N_SPLIT + 1, q.loop, 4 if q.loop else None) if j >= N_SPLIT else None
            landed = at_chunk(raw_full[r], j, N_RAW, 16)
            q.add("act", lambda e: e.activation(weight_hi[h][:, 0:size], weight_raw[r][:, 0:size], ACT.Copy),
                  [landed, free], hi_full[h])
            q.add("dve", lambda e: e.tensor_tensor(weight_lo[h][:, 0:size], weight_raw[r][:, 0:size],
                                                   weight_hi[h][:, 0:size].bitcast(F32), ALU.subtract),
                  [at_chunk(hi_full[h], j, N_SPLIT, 1), free], lo_full[h])

        def next_chunk():
            j = stream["j"]
            stream["j"] += 1
            return j, weight_hi[j % N_SPLIT], weight_lo[j % N_SPLIT]

        def skip(n):
            stream["j"] += n

        def chunk_products(j, groups, waits=(), steps=None):
            hi_in = at_chunk(hi_full[j % N_SPLIT], j, N_SPLIT, 1)
            lo_in = at_chunk(lo_full[j % N_SPLIT], j, N_SPLIT, 1)
            first = True
            last = len(groups) - 1
            for n, (o, a, b, start, lo, extra) in enumerate(groups):
                w = list(extra)
                if first:
                    w += [hi_in, *waits]
                if lo == 2:
                    w.append(lo_in)
                first = False
                pe(lambda e, o=o, a=a, b=b, start=start: e.matmul(o, a, b, start=start, stop=False,
                                                                  skip_group_check=True),
                   *w, inc=chunk_done if n == last else None)
            if j + N_SPLIT < len(SIZES):
                split(j + N_SPLIT)
            return Tok(chunk_done, j + 1, q.loop, 4 if q.loop else None)

        def products(hi, lo, wide, nk, outs, m_hi, m_lo, k0=0, ready=None, fresh=True, token_major=False):
            wh, wl = (w[:, 0:nk * wide].rearrange("p (k n) -> p k n", k=nk) for w in (hi, lo))
            first, second = [], []
            seen_banks = set()
            for n, (o, bank) in enumerate(outs):
                for k in range(nk):
                    start = fresh and k == 0 and (bank not in seen_banks)
                    if token_major:
                        t = slice(n * P, (n + 1) * P)
                        a, al, b, bl = m_hi[:, k0 + k, t], m_lo[:, k0 + k, t], wh[:, k, :], wl[:, k, :]
                        tri = [(a, b), (al, b), (a, bl)]
                    else:
                        c = slice(n * P, (n + 1) * P)
                        a, al, b, bl = wh[:, k, c], wl[:, k, c], m_hi[:, k0 + k, :], m_lo[:, k0 + k, :]
                        tri = [(a, b), (a, bl), (al, b)]
                    extra = ready[k] if ready is not None and n == 0 else ()
                    first.append((o, tri[0][0], tri[0][1], start, 0, extra))
                    first.append((o, tri[1][0], tri[1][1], False, 0, ()))
                    second.append((o, tri[2][0], tri[2][1], False, 2 if not second else 1, ()))
                    seen_banks.add(bank)
            return first + second

        def project(evac, act_k=KT, ready=None, wide=256, token_major=False, cols=None, m=None, nk=KT):
            j, hi, lo = next_chunk()
            w = stream["bank"]
            stream["bank"] += 1
            b = w % 2
            free = None
            if w >= 2:
                free = Tok(bank_free[b], w // 2, q.loop, 2 if q.loop else None)
                if q.loop and q.uses == 2:
                    free.step = 1
            hi_m, lo_m = m if m else (act_hi, act_lo)
            width = cols if token_major and cols else S
            n_out = ST if token_major else wide // P
            outs = [(work[b][:, n * S:n * S + width], b) for n in range(n_out)]
            done = chunk_products(j, products(hi, lo, wide, nk, outs, hi_m, lo_m, ready=ready,
                                              token_major=token_major), waits=[free])
            evac(work[b].rearrange("p (n t) -> p n t", n=2), done, bank_free[b])
            return done

        def accumulate(outs, m, nk=KT, wide=256, waits=(), ready=None):
            j, hi, lo = next_chunk()
            return chunk_products(j, products(hi, lo, wide, nk, outs, *m, ready=ready), waits=waits)

        def y_tiles(first, n):
            return [(y_acc[:, first + i, :], 2 + (first + i) // 2) for i in range(n)]

        ada_state = {"n": 0}

        def ada_chunk(extra=()):
            n = ada_state["n"]
            ada_state["n"] += 1
            r = n % N_ADA_RING
            k = n % KT
            g = n // KT % (ADA_COLS // CW)
            a = ada_acc[:, g * CW:(g + 1) * CW]
            before = ada_state.get("tok")
            landed = Tok(ada_full[r], (n // N_ADA_RING + 1) * 16)
            if k == 0:
                t = q.add("dve", lambda e: e.tensor_scalar(a, ada_raw[r][:, :], c_act[:, 0:1], None, ALU.mult),
                          [landed, ada_state["c"], *extra], ada_used)
            else:
                t = q.add("dve", lambda e: e.scalar_tensor_tensor(out=a, in0=ada_raw[r][:, :], scalar=c_act[:, k:k + 1],
                                                                  in1=a, op0=ALU.mult, op1=ALU.add),
                          [landed, before], ada_used)
            ada_state["tok"] = t
            load_ada(n + N_ADA_RING, t)
            return t

        def mods_of(layer, g, *waits):
            first = 16 * g
            m_ps = ps[:, 7, 0:16]
            t = None
            for n in range(16):
                t = pe(lambda e, n=n: e.matmul(ps[:, 7, n:n + P], ada_acc[:, (first + n) * P:(first + n + 1) * P],
                                               ones_sq[:, :], start=True, stop=True, skip_group_check=True),
                       *((ada_state["tok"], ada_state.get("mods"), consts, waits) if n == 0 else ()),
                       inc=True if n == 15 else None)
            b = VEC["b_ada"] + 48 * layer + first
            ada_state["mods"] = dve(lambda e: e.tensor_tensor(mods[layer][:, first:first + 16], m_ps,
                                                              vec[:, b:b + 16], ALU.add), t)
            ada_state["summed"] = t
            return ada_state["mods"]

        def mod(layer, which, n=None):
            if n is None:
                return mods[layer][:, which * KT:(which + 1) * KT]
            return mods[layer][:, which * KT + n:which * KT + n + 1]

        def load_ada(n, used=None):
            r = n % N_ADA_RING
            if n >= DEPTH * ADA_CHUNKS:
                return
            if q.loop:
                loop = q.loop
                q.add("pool", lambda e: e.dma_start(
                    ada_raw[r][:, :], ada[bass.ds(loop.i * N_ADA_RING + n, 1), :, :].squeeze(0)), [used],
                    ada_full[r], 16)
            else:
                q.add("pool", lambda e: e.dma_start(ada_raw[r][:, :], ada[n]), [used], ada_full[r], 16)

        t_vec = q.add("sp", lambda e: e.dma_start(vec[:, :], vecs), [], vec_in, 16)
        t_load = [t_vec, q.add("sp", lambda e: e.dma_start(res[:, :, :], x_in), [Tok(ada_used, 3)], x_arrived, 16)]
        for n in range(N_ADA_RING):
            load_ada(n)
        consts = [pool(lambda e: e.memset(ones_sq[:, :], 1.0)),
                  pool(lambda e: e.memset(ones_d[:, :], 1.0 / D)),
                  pool(lambda e: e.memset(minus_half[:, :], -0.5))]
        t = pool(lambda e: e.memset(ident[:, :], 0.0))
        consts.append(pool(lambda e: e.affine_select(out=ident[:, :], in_=ident[:, :], compare_op=ALU.not_equal,
                                                     fill=1.0, base=0, pattern=[[-1, P]], channel_multiplier=1), t))
        consts = consts[-1]

        ar = Arena("gla")
        g_q = ar("q", [P, GLA_H, S])
        g_k = ar("k", [P, GLA_H, S])
        g_v = ar("v", [P, ST, D])
        g_sg = ar("sg", [P, KT, S])
        g_la = ar("la", [P, GLA_H * S])
        g_e = ar("e", [P, GLA_H * S])
        g_en = ar("en", [P, GLA_H * S])
        g_scan = g_sg[:, 0:GLA_H, :].rearrange("p h t -> p (h t)")
        g_qn = ar("qn", [P, GLA_H, S])
        g_kn = g_en[:, :].rearrange("p (h t) -> p h t", h=GLA_H)
        g_kp = g_e[:, :].rearrange("p (h t) -> p h t", h=GLA_H)
        g_dec = ar("dec", [P, GLA_H * NCH])
        g_gk = ar("gk", [P, S])
        g_w2 = ar("w2", [GLA_RANK, GLA_H * P])
        g_fwd = ar("fwd", [P, ST * P])
        g_bwd = ar("bwd", [P, ST * P])
        a_at = [ar(f"a{i}", [P, ST, P]) for i in range(2)]
        g_ket = ar("ket", [P, ST, P])
        g_st = ar("st", [P, 3, GLA_DV])
        t_w2 = q.add("sp", lambda e: e.dma_start(g_w2[:, :], w_gk2), [], w2_in, 16)

        pool(lambda e: e.memset(g_scan, 1.0))
        t = pool(lambda e: e.memset(g_fwd[:, :], 1.0))
        pool(lambda e: e.memset(g_bwd[:, :], 1.0))
        for i in range(2):
            t = pool(lambda e, i=i: e.memset(a_at[i][:, :, :], 0.0))
        scan_v = g_scan.rearrange("p (c t) -> p c t", t=CHUNK)
        fwd_v, bwd_v = (m[:, :].rearrange("p (a t) -> p a t", a=ST) for m in (g_fwd, g_bwd))
        pool(lambda e: e.memset(scan_v[:, :, 0:1], 0.0), t)
        pool(lambda e: e.affine_select(out=fwd_v, in_=fwd_v, compare_op=ALU.is_ge, fill=0.0, base=0,
                                       pattern=[[0, ST], [1, P]], channel_multiplier=-1))
        t = pool(lambda e: e.affine_select(out=bwd_v, in_=bwd_v, compare_op=ALU.is_gt, fill=0.0, base=0,
                                           pattern=[[0, ST], [-1, P]], channel_multiplier=1))
        pool(lambda e: e.memset(fwd_v[0:CHUNK, :, CHUNK:P], 0.0), t)
        gla_consts = pool(lambda e: e.memset(bwd_v[CHUNK:P, :, 0:CHUNK], 0.0), t)

        def queue_weight_loads():
            j = 0
            while j < len(SIZES):
                run = 1
                pat = SIZES[j:j + 4]
                while SIZES[j + 4 * run:j + 4 * run + 4] == pat and j >= 4:
                    run += 1
                if run >= 2:
                    j0 = j

                    def body(loop):
                        for u in range(4):
                            jj = j0 + u
                            size = SIZES[jj]
                            freed = Tok(lo_full[jj % 2], (jj - 4) // 2 + 1, q.loop, 2)
                            q.add("sp", lambda e, jj=jj, size=size: e.dma_start(
                                weight_raw[jj % 4][:, 0:size],
                                weights[bass.ds(loop.i * 4 + jj, 1), :, 0:size].squeeze(0)),
                                [freed], raw_full[jj % 4], 16)

                    q.repeat(run, body)
                    j += 4 * run
                else:
                    size = SIZES[j]
                    freed = Tok(lo_full[j % 2], (j - 4) // 2 + 1) if j >= 4 else Tok(ada_used, 5 + j)
                    q.add("sp", lambda e, j=j, size=size: e.dma_start(weight_raw[j % 4][:, 0:size],
                                                                      weights[j, :, 0:size]),
                          [freed], raw_full[j % 4], 16)
                    j += 1

        queue_weight_loads()

        def split_activation(src, n, hi, lo, *waits, free=()):
            h = act(lambda e: e.activation(hi, src, ACT.Copy), *waits, *free)
            return [h, dve(lambda e: e.tensor_tensor(lo, src, hi.bitcast(F32), ALU.subtract), h, *waits, *free)]

        def modulate(src, a, b, tmp, ready):
            def first(k):
                scale, bias = a(k), b(k) if b else 0.0
                how = ACT.Identity if b else ACT.Copy
                h = act(lambda e: e.activation(act_hi[:, k, :], src(k), how, bias=bias, scale=scale), ready(k))
                if k % 2:
                    t = act(lambda e: e.activation(tmp(k), src(k), how, bias=bias, scale=scale), ready(k))
                elif b:
                    t = dve(lambda e: e.tensor_scalar(tmp(k), src(k), scale, bias, ALU.mult, ALU.add), ready(k))
                else:
                    t = dve(lambda e: e.tensor_scalar(tmp(k), src(k), scale, None, ALU.mult), ready(k))
                return [h, t]

            def second(k, ht):
                return dve(lambda e: e.tensor_tensor(act_lo[:, k, :], tmp(k), act_hi[:, k, :].bitcast(F32),
                                                     ALU.subtract), ht)
            return first, second

        def pipelined(n, first, second, before=None):
            out, f = [], {}
            for k in range(n + 1):
                if k < n:
                    if before:
                        before(k)
                    f[k] = first(k)
                if k:
                    out.append([f[k - 1], second(k - 1, f[k - 1])])
            return out

        def inverse_root(tiles, toks, count, eps_value, free, bank_free_toks=()):
            n = len(tiles)
            for t in range(ST):
                for k in range(n):
                    mm = pe(lambda e, k=k, t=t: e.matmul(ps[:, 7, t * P:(t + 1) * P], tiles[k][:, t * P:(t + 1) * P],
                                                         ones_sq[:, :], start=(k == 0 and t == 0), stop=(k == n - 1),
                                                         skip_group_check=True),
                            toks[k] if t == 0 else None, free if k == t == 0 else None,
                            inc=True if (t, k) == (ST - 1, n - 1) else None)
            m = dve(lambda e: e.tensor_scalar(root[:, 0:ST], ps[:, 7, 0:ST * P:P], 1.0 / count, eps_value, ALU.mult,
                                              ALU.add), mm, state.get("root"))
            p = pool(lambda e: e.tensor_tensor(root[:, 2:2 + ST], root[:, 0:ST], minus_half[:, :], ALU.pow), m, consts)
            dg = [dve(lambda e, t=t: e.tensor_scalar(diag[:, t, :], ident[:, :], root[:, 2 + t:3 + t], None, ALU.mult),
                      p, state.get("diag"), state.get("rstd_free")) for t in range(ST)]
            state["root"] = dg
            state["diag"] = pe(lambda e: e.matmul(rstd_ps, ones_sq[:, :], rstd[:, :],
                                                  start=True, stop=True, skip_group_check=True), dg, inc=True)
            return state["diag"]

        def norm(eps_value, z_toks, centre, x_of, u_of, free):
            t = None
            if centre:
                for k in range(KT):
                    t = pe(lambda e, k=k: e.matmul(mean_ps, ones_d[:, :], dev[:, k, :], start=(k == 0),
                                                   stop=(k == KT - 1), skip_group_check=True),
                           z_toks[k], *(free if k == 0 else ()), inc=True if k == KT - 1 else None)
                mean_t = t
                cent = []
                for h in range(4):
                    d = dev[:, 2 * h:2 * h + 2, :]
                    cent.append(dve(lambda e, d=d: e.tensor_tensor(
                        d, d, mean_ps.unsqueeze(1).broadcast_to([P, 2, S]), ALU.subtract), mean_t))
            else:
                cent = [z_toks[2 * h:2 * h + 2] for h in range(4)]
            sq_t = []
            for h in range(4):
                sq_t.append(act(lambda e, h=h: e.activation(square[:, 2 * h:2 * h + 2, :], dev[:, 2 * h:2 * h + 2, :],
                                                            ACT.Square), cent[h], *free))
            r = inverse_root([square[:, k, :] for k in range(KT)], [sq_t[k // 2] for k in range(KT)], D,
                             eps_value, free)
            used = {}

            def before(k):
                used[k] = dve(lambda e, k=k: e.tensor_tensor(dev[:, k, :], dev[:, k, :], rstd_ps, ALU.mult), r,
                              sq_t[k // 2], cent[k // 2])

            if u_of:
                first, second = u_of(lambda k: used[k])
                ready = pipelined(KT, first, second, before)
            else:
                ready = []
                for k in range(KT):
                    before(k)
            state["rstd_read"] = used[KT - 1]
            xs = [x_of(k, used[k]) for k in range(KT)] if x_of else []
            return ready, xs

        def residual(y_done, gate, x_toks, scale_x, free_dev):
            out_t = []
            for k in range(KT):
                if gate is None:
                    if k % 2 == 0:
                        t = dve(lambda e, k=k: e.tensor_tensor(dev[:, k:k + 2, :], y_acc[:, k:k + 2, :],
                                                               res[:, k:k + 2, :], ALU.add),
                                y_done, x_toks[k], x_toks[k + 1], *free_dev)
                    out_t.append(t)
                else:
                    out_t.append(dve(lambda e, k=k: e.scalar_tensor_tensor(
                        out=dev[:, k, :], in0=y_acc[:, k, :], scalar=gate[:, k:k + 1], in1=res[:, k, :],
                        op0=ALU.mult, op1=ALU.add), y_done, x_toks[k], *free_dev))
            return out_t

        state = {}

        def layer_norm_stage(idx, y_done, gate_t, sc, sh, next_vec_t):
            z = residual([y_done, gate_t], gate1, state["x"], ALPHA, state["dev_free"])
            g0, b0 = VEC["ln_g"] + KT * idx, VEC["ln_b"] + KT * idx
            lg, lb = vec[:, g0:g0 + KT], vec[:, b0:b0 + KT]
            w = state["norm_scale_free"]
            if sc is not None:
                t = dve(lambda e: e.scalar_tensor_tensor(out=norm_scale[:, 0, :], in0=sc, scalar=1.0, in1=lg,
                                                         op0=ALU.add, op1=ALU.mult), next_vec_t, *w)
                t1 = dve(lambda e: e.scalar_tensor_tensor(out=norm_scale[:, 1, :], in0=sc, scalar=1.0, in1=lb,
                                                          op0=ALU.add, op1=ALU.mult), next_vec_t, *w)
                t2 = dve(lambda e: e.tensor_tensor(norm_scale[:, 1, :], norm_scale[:, 1, :], sh, ALU.add), t1)
                t3 = dve(lambda e: e.tensor_scalar(alpha_ln[:, 0, :], lg, ALPHA, None, ALU.mult), *w)
                t4 = dve(lambda e: e.tensor_scalar(alpha_ln[:, 1, :], lb, ALPHA, None, ALU.mult), *w)
                vt = [t, t2, t3, t4]

                def u_of(used):
                    return modulate(lambda k: dev[:, k, :], lambda k: norm_scale[:, 0, k:k + 1],
                                    lambda k: norm_scale[:, 1, k:k + 1], lambda k: square[:, k, :],
                                    lambda k: [used(k), vt])

                def x_of(k, nt):
                    return act(lambda e: e.activation(res[:, k, :], dev[:, k, :], ACT.Identity,
                                                      bias=alpha_ln[:, 1, k:k + 1], scale=alpha_ln[:, 0, k:k + 1]),
                               nt, z[k], *vt)
                ready, xs = norm(LN_EPS, z, True, x_of, u_of, state["ps_free"])
            else:
                def x_only(k, nt):
                    return act(lambda e: e.activation(res[:, k, :], dev[:, k, :], ACT.Identity,
                                                      bias=vec[:, b0 + k:b0 + k + 1], scale=vec[:, g0 + k:g0 + k + 1]),
                               nt, z[k])
                ready, xs = norm(LN_EPS, z, True, x_only, None, state["ps_free"])
            state["x"] = xs
            state["z"] = z
            state["dev_free"] = [xs, ready, state["rstd_read"]]
            state["norm_scale_free"] = state["dev_free"]
            state["ps_free"] = state["dev_free"]
            return ready

        def rms_stage(vname, z, next_u=True):
            def u_of(used):
                return modulate(lambda k: dev[:, k, :], lambda k: v_of(vname, k), None, lambda k: square[:, k, :], used)

            def x_of(k, nt):
                return act(lambda e: e.activation(res[:, k, :], dev[:, k, :], ACT.Copy, scale=v_of(vname, k)), nt)
            ready, xs = norm(RMS_EPS, z, False, None if next_u else x_of, u_of if next_u else None, state["ps_free"])
            if next_u:
                state["dev_free"] = [ready, state["rstd_read"]]
                state["ps_free"] = state["dev_free"]
            return ready, xs

        e_c = act(lambda e: e.activation(c_act[:, :], vec[:, VEC["c"]:VEC["c"] + KT], ACT.Exp, scale=-1.0), t_vec)
        t = dve(lambda e: e.tensor_scalar(c_act[:, :], c_act[:, :], 1.0, None, ALU.add), e_c)
        t = dve(lambda e: e.reciprocal(c_act[:, :], c_act[:, :]), t)
        ada_state["c"] = dve(lambda e: e.tensor_tensor(c_act[:, :], c_act[:, :], vec[:, VEC["c"]:VEC["c"] + KT],
                                                       ALU.mult), t)
        for _ in range(KT):
            ada_chunk()
        for j in range(N_SPLIT):
            split(j)
        mt = mods_of(0, 0)
        t = dve(lambda e: e.tensor_scalar(norm_scale[:, 0, :], mod(0, 1), 1.0, None, ALU.add), mt)
        first, second = modulate(lambda k: res[:, k, :], lambda k: norm_scale[:, 0, k:k + 1], lambda k: mod(0, 0, k),
                                 lambda k: square[:, k, :], lambda k: [t, t_load])
        ready = pipelined(KT, first, second)
        state["x"] = [act(lambda e, k=k: e.activation(res[:, k, :], res[:, k, :], ACT.Copy, scale=ALPHA), ready[k])
                      for k in range(KT)]
        state["dev_free"], state["ps_free"] = [], []
        state["norm_scale_free"] = ready

        box = {}

        def evac_gk(b, done, s):
            box["gk"] = q.add("act", lambda e: e.activation(g_gk[:, :], b[:, 0, :], ACT.Copy), [done], s)

        project(evac_gk, wide=P, ready=ready)
        gate_ps = ps[:, 2:4, :].rearrange("p a (b n) -> p (a b) n", b=2)
        for h in range(GLA_H):
            t = pe(lambda e, h=h: e.matmul(gate_ps[:, h, :], g_w2[:, h * P:(h + 1) * P], g_gk[0:GLA_RANK, :],
                                           start=True, stop=True, skip_group_check=True),
                   box["gk"], t_w2, inc=True if h == GLA_H - 1 else None)
        la = g_la[:, :]
        zt = [dve(lambda e, h=h: e.tensor_scalar(g_la[:, h * S:(h + 1) * S], gate_ps[:, h, :], v_of("b_gk", h), None,
                                                 ALU.add), t) for h in range(GLA_H)]
        gate_read = zt[-1]
        a = act(lambda e: e.activation(g_e[:, :], la, ACT.Abs), zt)
        a = act(lambda e: e.activation(g_e[:, :], g_e[:, :], ACT.Exp, scale=-1.0), a)
        a = act(lambda e: e.activation(g_e[:, :], g_e[:, :], ACT.Ln, bias=1.0), a)
        t = dve(lambda e: e.scalar_tensor_tensor(out=g_en[:, :], in0=la, scalar=0.0, in1=g_e[:, :], op0=ALU.min,
                                                 op1=ALU.subtract), a)
        cum = dve(lambda e: e.tensor_tensor_scan(out=la, data0=g_scan, data1=g_en[:, :], initial=0.0,
                                                 op0=ALU.mult, op1=ALU.add), t, gla_consts, zt, a)
        TAU = 1.0 / 16.0
        e_pos = act(lambda e: e.activation(g_e[:, :], la, ACT.Exp, scale=TAU), cum, t)
        e_neg = act(lambda e: e.activation(g_en[:, :], la, ACT.Exp, scale=-TAU), cum)
        cum4 = la.rearrange("p (c t) -> p c t", t=CHUNK)
        end_t = dve(lambda e: e.tensor_tensor(g_qn[:, :, :].rearrange("p h (c t) -> p (h c) t", t=CHUNK),
                                              cum4[:, :, CHUNK - 1:CHUNK].broadcast_to([P, GLA_H * NCH, CHUNK]), cum4,
                                              ALU.subtract), cum)
        e_end = act(lambda e: e.activation(la, g_qn[:, :, :].rearrange("p h t -> p (h t)"), ACT.Exp, scale=TAU),
                    end_t, e_pos, e_neg)
        e3 = lambda m: m[:, :].rearrange("p (h t) -> p h t", h=GLA_H)
        dec_t = act(lambda e: e.activation(g_dec[:, :], g_e[:, CHUNK - 1::CHUNK], ACT.Copy), e_pos)

        def evac_to(dst, eng, scale=1.0, key=None):
            def evac(b, done, s):
                box.setdefault(key, []).append(
                    q.add("act", lambda e: e.activation(dst, b, ACT.Copy, scale=scale), [done], s) if eng == "act"
                    else q.add("dve", lambda e: e.tensor_scalar(dst, b, scale, None, ALU.mult), [done], s))
            return evac

        for n in range(2):
            project(evac_to(g_q[:, 2 * n:2 * n + 2, :], "act", GLA_DK ** -0.5, "q"))
            ada_chunk()
        for n in range(2):
            project(evac_to(g_k[:, 2 * n:2 * n + 2, :], "act", 1.0, "k"))
            ada_chunk()
        mul = lambda o, a, b: (lambda e: e.tensor_tensor(o, a, b, ALU.mult))
        qn_t = dve(mul(g_qn[:, :, :], g_q[:, :, :], e3(g_en)), box["q"], e_neg, e_end)
        qf_t = dve(mul(g_q[:, :, :], g_q[:, :, :], e3(g_e)), e_pos, qn_t)
        kn_t = dve(mul(g_kn, g_k[:, :, :], e3(g_en)), box["k"], e_neg, qn_t)
        kp_t = dve(mul(g_kp, g_k[:, :, :], e3(g_e)), e_pos, qf_t, dec_t)
        ke_t = dve(mul(g_k[:, :, :], g_k[:, :, :], e3(g_la)), e_end, kn_t, kp_t)
        for n in range(4):
            def evac_v(b, done, s, n=n):
                box.setdefault("v", []).append(
                    q.add("act", lambda e: e.activation(g_v[:, :, n * 256:(n + 1) * 256], b, ACT.Copy), [done], s))
            project(evac_v, token_major=True, cols=256)
            ada_chunk()

        a_ps = ps[:, 2, :].rearrange("p (a t) -> p a t", a=4)
        ket_ps = ps[:, 3, 0:2 * P].rearrange("p (a t) -> p a t", a=2)
        u_ps = ps[:, 4:6, :].rearrange("p a (b n) -> p (a b) n", b=2)
        o_ps = ps[:, 6, :].rearrange("p (v t) -> p v t", v=2)
        U_AT = (0, 2, 1)
        gh = {}

        def gla_scores(h):
            prev = gh.get(h - 1)
            for t in range(ST):
                c = slice(t * P, (t + 1) * P)
                pe(lambda e, t=t, c=c: e.matmul(a_ps[:, t, :], g_kn[:, h, c], g_q[:, h, c], start=True, stop=True,
                                                skip_group_check=True), kn_t, qf_t, gate_read, prev and prev["a"])
                pe(lambda e, t=t, c=c: e.matmul(a_ps[:, 2 + t, :], g_kp[:, h, c], g_qn[:, h, c], start=True,
                                                stop=True, skip_group_check=True), kp_t, qn_t)
            for t in range(ST):
                c = slice(t * P, (t + 1) * P)
                sc = pe(lambda e, t=t, c=c: e.matmul(ket_ps[:, t, :], g_k[:, h, c], ident[:, :], is_transpose=True,
                                                     start=True, stop=True, skip_group_check=True)
                        , ke_t, consts, prev and prev["ket"], inc=True if t else None)
            A = a_at[h % 2]
            w = gh[h - 2]["o_mm"] if h >= 2 else None
            t = dve(lambda e: e.copy_predicated(A[:, :, :], fwd_v.bitcast(I32), a_ps[:, 0:2, :]), sc, gla_consts, w)
            a2 = dve(lambda e: e.copy_predicated(A[:, :, :], bwd_v.bitcast(I32), a_ps[:, 2:4, :]), t)
            ket = act(lambda e: e.activation(g_ket[:, :, :], ket_ps, ACT.Copy), sc, prev and prev["u"])
            for c in range(NCH - 1):
                p0 = CHUNK * (c % 2)
                u = pe(lambda e, c=c, p0=p0: e.matmul(u_ps[:, U_AT[c], :], g_ket[p0:p0 + CHUNK, c // 2, :],
                                                      g_v[p0:p0 + CHUNK, c // 2, h * GLA_DV:(h + 1) * GLA_DV],
                                                      start=True, stop=True, skip_group_check=True),
                       ket, box["v"], prev and prev["st"], inc=True if c == NCH - 2 else None)
            st = act(lambda e: e.activation(g_st[:, 0, :], u_ps[:, 0, :], ACT.Copy), u, prev and prev["o_mm"])
            for c in (1, 2):
                st = dve(lambda e, c=c: e.scalar_tensor_tensor(
                    out=g_st[:, c, :], in0=g_st[:, c - 1, :], scalar=g_dec[:, h * NCH + c:h * NCH + c + 1],
                    in1=u_ps[:, U_AT[c], :], op0=ALU.mult, op1=ALU.add), st, dec_t, u, prev and prev["o_mm"])
            gh[h] = {"a": a2, "ket": ket, "u": u, "st": st}

        def gla_out(h):
            prev = gh.get(h - 1)
            first = True
            for v in range(2):
                for t in range(ST):
                    vs = slice(h * GLA_DV + v * P, h * GLA_DV + (v + 1) * P)
                    pe(lambda e, v=v, t=t, vs=vs, first=first: e.matmul(
                        o_ps[:, v, t * P:(t + 1) * P], g_v[:, t, vs], a_at[h % 2][:, t, :], start=first, stop=False,
                        skip_group_check=True), gh[h]["a"], prev and prev["og"])
                    first = False
            for v in range(2):
                for c in range(1, NCH):
                    o_mm = pe(lambda e, v=v, c=c: e.matmul(
                        o_ps[:, v, c * CHUNK:(c + 1) * CHUNK], g_st[:, c - 1, v * P:(v + 1) * P],
                        g_q[:, h, c * CHUNK:(c + 1) * CHUNK], start=False, stop=False, skip_group_check=True),
                        gh[h]["st"], inc=True if (v, c) == (1, NCH - 1) else None)
            sq = act(lambda e: e.activation(square[:, 0:2, :], o_ps, ACT.Square), o_mm, prev and prev["ms"],
                     ready)
            ms = inverse_root([square[:, v, :] for v in range(2)], [sq, sq], GLA_DV, RMS_EPS,
                              [prev and prev["r1"], ada_state["mods"], gate_read])
            r1 = act(lambda e: e.activation(rstd[:, :], rstd_ps, ACT.Copy), ms, prev and prev["og"])
            og = dve(lambda e: e.tensor_tensor(dev[:, 2 * h:2 * h + 2, :], o_ps,
                                               rstd[:, :].unsqueeze(1).broadcast_to([P, 2, S]), ALU.mult), r1)
            state["rstd_free"] = og
            gh[h].update(o_mm=o_mm, ms=ms, r1=r1, og=og)

        def evac_g(n):
            def evac(b, done, s):
                sg = g_sg[:, 2 * n:2 * n + 2, :]
                t = act(lambda e: e.activation(sg, b, ACT.Sigmoid), done)
                box.setdefault("sg", []).append(
                    q.add("dve", lambda e: e.tensor_tensor(sg, sg, b, ALU.mult), [t, done], s))
            return evac

        for h in range(GLA_H):
            gla_scores(h)
            project(evac_g(h))
            ada_chunk()
            gla_out(h)
        in_done = Tok(chunk_done, stream["j"])

        def gated(k):
            return dve(lambda e: e.scalar_tensor_tensor(out=dev[:, k, :], in0=dev[:, k, :], scalar=v_of("g_norm", k),
                                                        in1=g_sg[:, k, :], op0=ALU.mult, op1=ALU.mult),
                       gh[k // 2]["og"], box["sg"])

        def rounded(k):
            t = gated(k)
            return [t, act(lambda e: e.activation(act_hi[:, k, :], dev[:, k, :], ACT.Copy), t, in_done)]

        out_ready = pipelined(KT, rounded, lambda k, ht: dve(lambda e: e.tensor_tensor(
            act_lo[:, k, :], dev[:, k, :], act_hi[:, k, :].bitcast(F32), ALU.subtract), ht, in_done))
        y_free = [gh[GLA_H - 1]["st"], gh[GLA_H - 1]["a"], gh[GLA_H - 1]["ket"]]

        def out_projection(ready, ada_n=0, m=None, nk=KT, wide=256, waits=()):
            tiles = wide // P
            for n in range(KT // tiles):
                done = accumulate(y_tiles(n * tiles, tiles), m or (act_hi, act_lo), nk=nk, wide=wide,
                                  waits=waits if n == 0 else (), ready=ready if n == 0 else None)
                if ada_n:
                    ada_chunk()
            return done

        y_done = out_projection(out_ready, ada_n=1, waits=y_free)
        mods_of(0, 1, gh[GLA_H - 1]["r1"])
        mods_of(0, 2)
        state["dev_free"] = out_ready
        state["ps_free"] = [gh[GLA_H - 1]["og"], gh[GLA_H - 1]["r1"], ada_state["mods"], state["dev_free"]]


        def everything():
            return [Tok(q.done[k], q.count[q.done[k]]) for k in ("act", "dve", "pe", "pool")
                    if q.count.get(q.done[k])] + [Tok(chunk_done, stream["j"])]

        def up_down(tag, ready, y_read, n_blocks, n_tiles, evac_up, buffers, in_loop=None, after_first=None, after_loop=None):
            hid_hi, hid_lo = buffers
            buf = {("y", 0): None, ("y", 1): None, ("split", 0): None, ("split", 1): None}
            base_j = stream["j"]

            def up(i, block, ready=None):
                p = i % 2

                def evac(b, done, s):
                    buf[("split", p)] = evac_up(block, p, b, done, s, buf[("y", p)], buf[("split", p)])

                project(evac, ready=ready)

            def down(i, fresh=False):
                p = i % 2
                j, hi, lo = next_chunk()
                buf[("y", p)] = chunk_products(
                    j, products(hi, lo, D, n_tiles, y_tiles(0, KT), hid_hi[p], hid_lo[p], fresh=fresh),
                    waits=[buf[("split", p)], y_read if fresh else None])
                return buf[("y", p)]

            up(0, 0, ready)
            if after_first:
                after_first()
            up(1, 1)
            down(0, fresh=True)
            n_loop = (n_blocks - 2) // 2 - 1

            def body(loop):
                lags = {}
                for key in buf:
                    lags[key] = Lag()
                    buf[key] = [lags[key], buf[key]]
                up(0, lambda: loop.i * 2 + 2)
                down(1)
                up(1, lambda: loop.i * 2 + 3)
                down(0)
                if in_loop:
                    in_loop(loop)
                for key, lag in lags.items():
                    lag.bind(buf[key][-1] if isinstance(buf[key], list) else buf[key])

            q.uses = 2
            q.repeat(n_loop, body)
            q.uses = 4
            skip(4 * (n_loop - 1))
            stream["bank"] += 2 * (n_loop - 1)
            last = 2 * n_loop + 2
            up(0, last)
            down(1)
            up(1, last + 1)
            down(0)
            done = down(1)
            if after_loop:
                after_loop()
            assert stream["j"] == base_j + 2 * n_blocks and n_blocks % 2 == 0
            return done

        def mlp(tag, ready, y_read, in_loop=None, after_first=None, after_loop=None):
            ar = Arena(tag)
            relu_buf = [ar(f"relu{i}", [P, 2, S]) for i in range(2)]
            sq_buf = [ar(f"sq{i}", [P, 2, S]) for i in range(2)]
            hid_hi = [ar(f"hi{i}", [P, 2, S], F32R) for i in range(2)]
            hid_lo = [ar(f"lo{i}", [P, 2, S], F32R) for i in range(2)]
            free = state["arena_free"]

            def evac_up(block, p, b, done, s, y_tok, split_tok):
                r = q.add("dve", lambda e: e.tensor_scalar(relu_buf[p][:, :, :], b, 0.0, None, ALU.max),
                          [done, split_tok, free], s)
                h = act(lambda e: e.activation(hid_hi[p][:, :, :], relu_buf[p][:, :, :], ACT.Square), r, y_tok)
                t = dve(lambda e: e.tensor_tensor(sq_buf[p][:, :, :], relu_buf[p][:, :, :], relu_buf[p][:, :, :],
                                                  ALU.mult), r)
                lo = dve(lambda e: e.tensor_tensor(hid_lo[p][:, :, :], sq_buf[p][:, :, :],
                                                   hid_hi[p][:, :, :].bitcast(F32), ALU.subtract), h, t, y_tok)
                return lo

            done = up_down(tag, ready, y_read, D_FF // 256, 2, evac_up, (hid_hi, hid_lo), in_loop, after_first,
                           after_loop)
            state["arena_free"] = everything()
            return done

        def ada_step(k, k_col, g, extra):
            n = ada_state["n"]
            a = ada_acc[:, g * CW:(g + 1) * CW]
            landed = Tok(ada_full[n % N_ADA_RING], (n // N_ADA_RING + 1) * 16, q.loop, 16 if q.loop else None)
            ada_state["n"] += 1
            r = n % N_ADA_RING
            if k == 0:
                t = q.add("dve", lambda e: e.tensor_scalar(a, ada_raw[r][:, :], c_act[:, 0:1], None, ALU.mult),
                          [landed, extra], ada_used)
            else:
                t = q.add("dve", lambda e: e.scalar_tensor_tensor(out=a, in0=ada_raw[r][:, :], scalar=k_col(), in1=a,
                                                                  op0=ALU.mult, op1=ALU.add), [landed, extra],
                          ada_used)
            load_ada(n + N_ADA_RING, t)
            return t

        def gate_plus_one(layer, which):
            return dve(lambda e: e.tensor_scalar(gate1[:, :], mod(layer, which), 1.0, None, ALU.add),
                       ada_state["mods"], state.get("z"))

        state["arena_free"] = everything()
        gt = gate_plus_one(0, 2)
        ready = layer_norm_stage(0, y_done, gt, mod(0, 4), mod(0, 3), ada_state["mods"])
        n_groups = ADA_COLS // CW

        def ada_first():
            ada_state["g"] = [ada_step(0, None, g, ada_state["summed"]) for g in range(n_groups)]

        def ada_loop(loop):
            ada_state["after"] = ada_state["n"] + n_groups * loop.n
            for g in range(n_groups):
                lag = Lag()
                t = ada_step(1, lambda: c_act[:, bass.ds(loop.i + 1, 1)], g, [lag, ada_state["g"][g]])
                lag.bind(t)
                ada_state["g"][g] = t

        def ada_last():
            ada_state["n"] = ada_state["after"]
            for g in range(n_groups):
                ada_state["tok"] = ada_step(KT - 1, lambda: c_act[:, KT - 1:KT], g, ada_state["g"][g])

        y_done = mlp("mlp0", ready, state["z"], ada_loop, ada_first, ada_last)
        ada_state["n"] = DEPTH * ADA_CHUNKS
        gt = gate_plus_one(0, 5)
        for g in range(n_groups):
            mods_of(1, g)
        state["ps_free"] = [state["ps_free"], ada_state["mods"]]
        ready = layer_norm_stage(1, y_done, gt, mod(1, 1), mod(1, 0), ada_state["mods"])

        def attention(tag, qs, ks, vs, n_heads, bias_of, out_tile, s_sb, pt_sb, stats, free):
            h_of = {}
            s_ps = [ps[:, 2 + i, 0:3 * P] for i in range(2)]
            pt_ps = [ps[:, 4 + i, 0:3 * P].rearrange("p (a n) -> p a n", a=3) for i in range(2)]
            o_ps = [ps[:, 6 + i, 0:S] for i in range(2)]
            n_pt = len(pt_sb)

            def part(h):
                p0 = HD * (h % 2)
                return slice(p0, p0 + HD), h // 2

            def scores(h, q_tok):
                rows, n = part(h)
                sp, s = s_ps[h % 2], s_sb[h % 2]
                old = h_of.get(h - 2, {})
                pe(lambda e: e.matmul(sp[:, 0:P], qs[rows, n, 0:P], ks[rows, n, 0:P], start=True, stop=True,
                                      skip_group_check=True), q_tok, old.get("biased"), free)
                mm = pe(lambda e: e.matmul(sp[:, P:3 * P], qs[rows, n, P:S], ks[rows, n, :], start=True, stop=True,
                                           skip_group_check=True), inc=True)
                b0, b1, b_tok = bias_of(h)
                t0 = dve(lambda e: e.scalar_tensor_tensor(out=s[:, 0:P], in0=sp[:, 0:P], scalar=HD ** -0.5, in1=b0,
                                                          op0=ALU.mult, op1=ALU.add), mm, b_tok, old.get("turned"), free)
                t1 = dve(lambda e: e.scalar_tensor_tensor(out=s[:, P:3 * P], in0=sp[:, P:3 * P], scalar=HD ** -0.5,
                                                          in1=b1, op0=ALU.mult, op1=ALU.add), mm, b_tok)
                st = stats[h % 2]
                m0 = dve(lambda e: e.tensor_reduce(st[:, 0:1], s[:, 0:P], AX.X, ALU.max, negate=True), t0,
                         old.get("scaled"))
                m1 = dve(lambda e: e.tensor_reduce(st[:, 1:2], s[:, P:3 * P], AX.X, ALU.max, negate=True), t1)
                e0 = act(lambda e: e.activation(s[:, 0:P], s[:, 0:P], ACT.Exp, bias=st[:, 0:1],
                                                accum_out=st[:, 2:3]), m0)
                e1 = act(lambda e: e.activation(s[:, P:3 * P], s[:, P:3 * P], ACT.Exp, bias=st[:, 1:2],
                                                accum_out=st[:, 3:4]), m1)
                r = dve(lambda e: e.reciprocal(st[:, 4:6], st[:, 2:4]), e0, e1)
                p0 = dve(lambda e: e.tensor_scalar(s[:, 0:P], s[:, 0:P], st[:, 4:5], None, ALU.mult), r)
                p1 = dve(lambda e: e.tensor_scalar(s[:, P:3 * P], s[:, P:3 * P], st[:, 5:6], None, ALU.mult), r)
                h_of[h] = {"biased": [t0, t1], "scaled": [p0, p1]}

            def turn(h):
                s, pp = s_sb[h % 2], pt_ps[h % 2]
                old = h_of.get(h - 2, {})
                for a in range(3):
                    t = pe(lambda e, a=a: e.matmul(pp[:, a, :], s[:, a * P:(a + 1) * P], ident[:, :], is_transpose=True,
                                                   start=True, stop=True, skip_group_check=True),
                           h_of[h]["scaled"], old.get("pt"), free, inc=True if a == 2 else None)
                h_of[h]["turned"] = t
                h_of[h]["pt"] = act(lambda e: e.activation(pt_sb[h % n_pt], pp, ACT.Copy), t,
                                    h_of.get(h - n_pt, {}).get("pv"), free)

            def values(h, v_tok):
                rows, n = part(h)
                o, pt = o_ps[n % 2][rows, :], pt_sb[h % n_pt]
                vh = slice(h * HD, (h + 1) * HD)
                old = h_of.get(("out", n - 2))
                pe(lambda e: e.matmul(o[:, 0:P], vs[:, 0, vh], pt[:, 0, :], start=True, stop=False,
                                      skip_group_check=True), v_tok, h_of[h]["pt"], old, free)
                pe(lambda e: e.matmul(o[:, P:S], vs[:, 0, vh], pt[:, 1, :], start=False, stop=False,
                                      skip_group_check=True))
                h_of[h]["pv"] = t = pe(lambda e: e.matmul(o[:, P:S], vs[:, 1, vh], pt[:, 2, :], start=False, stop=True,
                                                          skip_group_check=True), inc=True)
                if h % 2:
                    h_of[("out", n)] = out_tile(n, o_ps[n % 2], [t, h_of[h - 1]["pv"]])
                    return h_of[("out", n)]

            return scores, turn, values

        ar = Arena("att")
        at_q, at_k = ar("q", [P, KT, S]), ar("k", [P, KT, S])
        at_v = ar("v", [P, ST, D])
        at_s = [ar(f"s{i}", [P, 3 * P]) for i in range(2)]
        N_PT = 8
        at_pt = [ar(f"pt{i}", [P, 3, P]) for i in range(N_PT)]
        N_BIAS = 4
        at_bias = [ar(f"bias{i}", [P, S]) for i in range(N_BIAS)]
        at_st = [ar(f"st{i}", [P, 8]) for i in range(2)]
        arena_free = state["arena_free"]
        masked = []
        box = {}

        def load_bias(h, free):
            r = h % N_BIAS
            t = q.add("pool", lambda e: e.dma_start(at_bias[r][:, :], rel_bias[h]), free, bias_full[r], 16)
            masked.append(pool(lambda e: e.memset(at_bias[r][0:CHUNK, S - CHUNK:S], NEG), t))

        for h in range(N_BIAS):
            load_bias(h, [arena_free])

        def evac_bias(dst, first):
            def evac(b, done, s):
                t = act(lambda e: e.activation(dst[:, first % KT, :], b[:, 0, :], ACT.Identity,
                                               bias=v_of("att_b", first)), done, arena_free)
                t2 = q.add("act", lambda e: e.activation(dst[:, first % KT + 1, :], b[:, 1, :], ACT.Identity,
                                                         bias=v_of("att_b", first + 1)), [done, arena_free], s)
                box.setdefault("qk", []).extend([t, t2])
            return evac

        for n in range(8):
            project(evac_bias(at_q if n < 4 else at_k, 2 * n), ready=ready if n == 0 else None)

        def out_tile1(n, o, toks):
            in_done = Tok(chunk_done, box["in_done"])
            h = act(lambda e: e.activation(act_hi[:, n, :], o, ACT.Identity, bias=v_of("att_b", 16 + n)), toks, in_done)
            t = dve(lambda e: e.tensor_scalar(square[:, n, :], o, v_of("att_b", 16 + n), None, ALU.add), toks, h,
                    state["dev_free"])
            return [h, dve(lambda e: e.tensor_tensor(act_lo[:, n, :], square[:, n, :],
                                                     act_hi[:, n, :].bitcast(F32), ALU.subtract), h, t, in_done), t]

        def bias1(h):
            b = at_bias[h % N_BIAS]
            return b[:, P:S], b[:, :], masked[h]

        scores, turn, values = attention("att", at_q, at_k, at_v, ATT_H, bias1, out_tile1, at_s,
                                         [x[:, :, :] for x in at_pt], at_st, [arena_free, state["ps_free"]])

        def scores1(h):
            scores(h, box["qk"])
            if h + N_BIAS < ATT_H:
                load_bias(h + N_BIAS, [Tok(q.done["dve"], q.count[q.done["dve"]])])

        for n in range(4):
            scores1(2 * n)
            scores1(2 * n + 1)

            def evac_v1(b, done, s, n=n):
                box.setdefault("v", []).append(q.add("act", lambda e: e.activation(
                    at_v[:, :, n * 256:(n + 1) * 256], b, ACT.Copy), [done, arena_free], s))
            project(evac_v1, token_major=True, cols=256)
            turn(2 * n)
            turn(2 * n + 1)
        box["in_done"] = stream["j"]
        att_ready = []
        scores1(8)
        for h in range(8, ATT_H):
            if h + 1 < ATT_H:
                scores1(h + 1)
            t = values(h - 8, box["v"])
            att_ready += [t] if t else []
            turn(h)
        for h in range(8, ATT_H):
            t = values(h, box["v"])
            att_ready += [t] if t else []
        fr = everything()
        y_done = out_projection(att_ready, waits=[fr])
        state["arena_free"] = fr
        gt = gate_plus_one(1, 2)
        state["dev_free"] = [state["dev_free"], att_ready]
        state["ps_free"] = [state["ps_free"], fr]
        ready = layer_norm_stage(2, y_done, gt, mod(1, 4), mod(1, 3), ada_state["mods"])
        y_done = mlp("mlp1", ready, state["z"])
        gt = gate_plus_one(1, 5)
        layer_norm_stage(3, y_done, gt, None, None, None)

        z = [dve(lambda e, k=k: e.tensor_copy(dev[:, k, :], res[:, k, :]), state["x"][k]) for k in range(KT)]
        state["ps_free"] = [state["ps_free"], state["x"]]
        ready, _ = rms_stage("norm_mix", z)

        ar = Arena("mix")
        arena_free = state["arena_free"]
        m_tab = ar("rope", [P, 2 * S + P])
        m_cnt = ar("cnt", [P, 4, 16])
        m_pw = ar("pw", [P, 4, P])
        iq_at = ar.at
        m_iq = ar("iq", [P, 4, S])
        up_at = ar.at
        m_up = ar("up", [P, 4, S])
        m_ik = ar("ik", [P, S])
        m_iw = ar("iw", [P, ST, IDX_H])
        m_q, m_k = ar("q", [P, 4, S]), ar("k", [P, 4, S])
        m_v = ar("v", [P, ST, 512])
        m_mix_hi, m_mix_lo = ar("mix_hi", [P, 4, S], F32R), ar("mix_lo", [P, 4, S], F32R)
        m_score, m_mask = ar("score", [P, 3 * P]), ar("mask", [P, 3 * P])
        m_top = ar("top", [P, 2, 8])
        m_s = [ar(f"s{i}", [P, 3 * P]) for i in range(2)]
        m_st = [ar(f"st{i}", [P, 8]) for i in range(2)]
        m_ptb = ar("ptb", [P, 6 * 3 * P])
        m_pt = [m_ptb[:, i * 3 * P:(i + 1) * 3 * P].rearrange("p (a n) -> p a n", a=3) for i in range(6)]
        rope_tmp = [m_ptb[:, i * 512:(i + 1) * 512].rearrange("p (a n) -> p a n", a=2) for i in range(2)]
        relu_tmp = [m_ptb[:, 1024 + i * 384:1024 + (i + 1) * 384] for i in range(2)]
        m_o_hi = nc.alloc_sbuf_tensor_at("mix_o_hi", [P, 4, S], F32R, offset=iq_at)
        m_o_lo = nc.alloc_sbuf_tensor_at("mix_o_lo", [P, 4, S], F32R, offset=up_at)
        t_tab = [q.add("pool", lambda e, a=a, b=b: e.dma_start(a, b), [arena_free], s, 16)
                 for a, b, s in ((m_tab[:, :], rope, tables_in[0]), (m_cnt[:, :, :], pool_count, tables_in[1]),
                                 (m_pw[:, :, :], pool_w, tables_in[2]))]
        cos_t, sin_t, rot_t = m_tab[:, 0:S], m_tab[:, S:2 * S], m_tab[:, 2 * S:2 * S + P]
        m_ps_free = state["ps_free"]
        box = {}

        j, hi, lo = next_chunk()
        wide = 2 * HD + IDX_H
        wh, wl = (w[:, 0:KT * wide].rearrange("p (k n) -> p k n", k=KT) for w in (hi, lo))
        w = stream["bank"]
        stream["bank"] += 1
        b = w % 2
        groups = []
        for k in range(KT):
            groups.append((work[b][:, 0:S], wh[:, k, 0:P], act_hi[:, k, :], k == 0, 0, ready[k]))
            groups.append((work[b][:, 0:S], wh[:, k, 0:P], act_lo[:, k, :], False, 0, ()))
        for t in range(ST):
            c = slice(t * P, (t + 1) * P)
            o = work[b][:, S + 8 * t:S + 8 * t + 8]
            for k in range(KT):
                groups.append((o, act_hi[:, k, c], wh[:, k, P:P + 8], False, 0, ()))
                groups.append((o, act_lo[:, k, c], wh[:, k, P:P + 8], False, 0, ()))
        for k in range(KT):
            groups.append((work[b][:, 0:S], wl[:, k, 0:P], act_hi[:, k, :], False, 2 if k == 0 else 1, ()))
        for t in range(ST):
            for k in range(KT):
                groups.append((work[b][:, S + 8 * t:S + 8 * t + 8], act_hi[:, k, t * P:(t + 1) * P],
                               wl[:, k, P:P + 8], False, 1, ()))
        done = chunk_products(j, groups, waits=[Tok(bank_free[b], w // 2)])
        ik_t = act(lambda e: e.activation(m_ik[:, :], work[b][:, 0:S], ACT.Copy), done, arena_free)
        iw_t = q.add("act", lambda e: e.activation(m_iw[:, :, :], work[b][:, S:S + 16].rearrange("p (t h) -> p t h", t=2),
                                                   ACT.Copy, scale=IDX_H ** -0.5), [done, arena_free], bank_free[b])

        rope_state = {"free": [m_ps_free, arena_free]}

        def rope_tiles(x, n, tok):
            rp = ps[:, 7, 0:n * S].rearrange("p (a t) -> p a t", a=n)
            mm = pe(lambda e: e.matmul(rp, rot_t, x, start=True, stop=True, skip_group_check=True), tok, t_tab,
                    rope_state["free"], inc=True)
            a, b = rope_tmp[0][:, 0:n, :], rope_tmp[1][:, 0:n, :]
            cb, sbb = (v.unsqueeze(1).broadcast_to([P, n, S]) for v in (cos_t, sin_t))
            t1 = dve(lambda e: e.tensor_tensor(a, x, cb, ALU.mult), tok, t_tab, rope_state["free"])
            t2 = dve(lambda e: e.tensor_tensor(b, rp, sbb, ALU.mult), mm)
            t3 = dve(lambda e: e.tensor_tensor(x, a, b, ALU.add), t1, t2)
            rope_state["free"] = [t3]
            return t3

        def evac_plain(dst, first, key, n=2):
            def evac(b, done, s):
                box.setdefault(key, []).append(q.add("act", lambda e: e.activation(
                    dst[:, first:first + n, :], b[:, 0:n, :], ACT.Copy), [done, arena_free], s))
            return evac

        background = []

        def drip(n):
            for _ in range(min(n, len(background))):
                background.pop(0)()

        project(evac_plain(m_iq, 0, "iq"))
        ik_t = rope_tiles(m_ik[:, :].unsqueeze(1), 1, ik_t)
        project(evac_plain(m_iq, 2, "iq"))
        iq_t = [rope_tiles(m_iq[:, 0:2, :], 2, box["iq"][0])]
        project(evac_plain(m_q, 0, "q"))
        iq_t.append(rope_tiles(m_iq[:, 2:4, :], 2, box["iq"][1]))

        idx = {}

        def index_scores(h):
            rows = slice(HD * (h % 2), HD * (h % 2) + HD)
            sp = ps[:, 2 + h % 2, 0:3 * P]
            rel = relu_tmp[h % 2]
            n = h // 2
            old = idx.get(h - 2, {})
            pe(lambda e: e.matmul(sp[:, 0:P], m_iq[rows, n, 0:P], m_ik[rows, 0:P], start=True, stop=True,
                                  skip_group_check=True), iq_t[n // 2], ik_t, old.get("relu"), m_ps_free)
            mm = pe(lambda e: e.matmul(sp[:, P:3 * P], m_iq[rows, n, P:S], m_ik[rows, :], start=True, stop=True,
                                       skip_group_check=True), inc=True)
            r = act(lambda e: e.activation(rel, sp, ACT.Relu, scale=HD ** -0.5), mm, old.get("sum"), arena_free)
            t = []
            for a, cols in ((0, slice(0, P)), (1, slice(P, 3 * P))):
                w = m_iw[:, a, h:h + 1]
                if h == 0:
                    t.append(dve(lambda e, w=w, cols=cols: e.tensor_scalar(m_score[:, cols], rel[:, cols], w, None,
                                                                           ALU.mult), r, iw_t, arena_free))
                else:
                    t.append(dve(lambda e, w=w, cols=cols: e.scalar_tensor_tensor(
                        out=m_score[:, cols], in0=rel[:, cols], scalar=w, in1=m_score[:, cols], op0=ALU.mult,
                        op1=ALU.add), r, idx[h - 1]["sum"]))
            idx[h] = {"relu": r, "sum": t, "mm": mm}

        for h in range(4):
            index_scores(h)
        project(evac_plain(m_q, 2, "q"))
        for h in range(4, IDX_H):
            index_scores(h)

        causal = []
        for a, cols, n in ((0, slice(0, P), P), (1, slice(P, 3 * P), S)):
            causal.append(pool(lambda e, cols=cols, n=n, a=a: e.affine_select(
                out=m_score[:, cols], in_=m_score[:, cols], compare_op=ALU.is_ge, fill=NEG, base=a * P,
                pattern=[[-1, n]], channel_multiplier=1), idx[IDX_H - 1]["sum"][a]))
        top_state = {"t": list(causal)}

        def top_max(a, cols):
            def f():
                top_state["t"][a] = dve(lambda e: e.max(m_top[:, a, :], m_score[:, cols]), top_state["t"][a])
            return f

        def top_mark(a, cols):
            def f():
                top_state["t"][a] = dve(lambda e: e.match_replace(m_score[:, cols], m_top[:, a, :], m_score[:, cols],
                                                                  TAKEN), top_state["t"][a])
            return f

        halves = ((0, slice(0, P)), (1, slice(P, 3 * P)))
        for _ in range(TOPK // 8):
            background += [top_max(*x) for x in halves] + [top_mark(*x) for x in halves]
        project(evac_plain(m_k, 0, "k"))
        q_t = [rope_tiles(m_q[:, 0:2, :], 2, box["q"][0])]
        drip(6)
        project(evac_plain(m_k, 2, "k"))
        q_t.append(rope_tiles(m_q[:, 2:4, :], 2, box["q"][1]))
        drip(5)
        gates_t = []
        gate_free = state["dev_free"]

        def evac_gate(n):
            def evac(b, done, s):
                g = (dev if n < 4 else square)[:, (2 * n) % KT:(2 * n) % KT + 2, :]
                gates_t.append(q.add("act", lambda e: e.activation(g, b, ACT.Sigmoid), [done, gate_free], s))
            return evac

        for n in range(8):
            project(evac_gate(n))
            if n < 2:
                q_t.append(rope_tiles(m_k[:, 2 * n:2 * n + 2, :], 2, box["k"][n]))
            drip(4)
        drip(99)
        t = dve(lambda e: e.tensor_scalar(m_mask[:, :], m_score[:, :], TAKEN / 2, NEG, ALU.is_gt, ALU.mult),
                top_state["t"], arena_free)
        mask_t = [pool(lambda e, cols=cols, n=n, a=a: e.affine_select(
            out=m_mask[:, cols], in_=m_mask[:, cols], compare_op=ALU.is_ge, fill=NEG, base=a * P,
            pattern=[[-1, n]], channel_multiplier=1), t) for a, cols, n in ((0, slice(0, P), P), (1, slice(P, 3 * P), S))]

        def out_tile2(n, o, toks):
            h = act(lambda e: e.activation(m_o_hi[:, n, :], o, ACT.Copy), toks, iq_done, up_done)
            return [h, dve(lambda e: e.tensor_tensor(m_o_lo[:, n, :], o, m_o_hi[:, n, :].bitcast(F32), ALU.subtract),
                           h)]

        scores, turn, values = attention(
            "att2", m_q, m_k, m_v, ATT2_H, lambda h: (m_mask[:, 0:P], m_mask[:, P:3 * P], mask_t), out_tile2, m_s,
            m_pt, m_st, [rope_state["free"], idx[IDX_H - 1]["sum"], idx[IDX_H - 2]["relu"], idx[IDX_H - 1]["relu"]])
        iq_done = [idx[IDX_H - 1]["mm"]]

        def pool_group(g, first_tok):
            u = m_up[:, g, :]
            a, t = u, first_tok
            bufs = [rstd[:, :], pool_tmp[:, :]]
            for i in range(g + 1):
                sh = 1 << i
                o = bufs[i % 2]
                t1 = dve(lambda e, o=o, a=a, sh=sh: e.tensor_tensor(o[:, sh:S], a[:, sh:S], a[:, 0:S - sh], ALU.add), t)
                t2 = dve(lambda e, o=o, a=a, sh=sh: e.tensor_copy(o[:, 0:sh], a[:, 0:sh]), t)
                a, t = o, [t1, t2]
            o = bufs[(g + 1) % 2]
            t1 = dve(lambda e: e.tensor_tensor(o[:, 0:16], a[:, 0:16], m_cnt[:, g, :], ALU.mult), t, t_tab)
            t2 = dve(lambda e: e.tensor_tensor(u[:, 0:16], o[:, 0:16], u[:, 0:16], ALU.subtract), t1)
            t3 = dve(lambda e: e.scalar_tensor_tensor(out=u[:, 16:S], in0=a[:, 16:S], scalar=1.0 / POOL_WINDOWS[g],
                                                      in1=u[:, 16:S], op0=ALU.mult, op1=ALU.subtract), t)
            return [t2, t3]

        for n in range(2):
            project(evac_plain(m_up, 2 * n, "up"))
        pool_tmp = ar("pool_tmp", [P, S])
        pooled, prev_t = [], [box["up"], arena_free, state["diag"]]
        for g in range(4):
            prev_t = pool_group(g, prev_t)
            pooled.append(prev_t)
        mix_ready, pool_mm = [], []
        for half in range(2):
            mp = ps[:, 6 + half, :].rearrange("p (a t) -> p a t", a=2)
            for i in range(2):
                g = 2 * half + i
                t = pe(lambda e, g=g, i=i, mp=mp: e.matmul(mp[:, i, :], m_pw[:, g, :], m_up[:, g, :], start=True,
                                                           stop=True, skip_group_check=True),
                       pooled[g], t_tab, rope_state["free"], m_ps_free, inc=True if i else None)
            pool_mm.append(t)
            rounded = [act(lambda e, g=g, i=i, mp=mp: e.activation(m_mix_hi[:, g, :], mp[:, i, :], ACT.Copy,
                                                                scale=v_of("pool_scale", g)), t, arena_free)
                       for i, g in enumerate((2 * half, 2 * half + 1))]
            for i in range(2):
                g = 2 * half + i
                h = rounded[i]
                t1 = dve(lambda e, g=g, i=i, mp=mp: e.tensor_scalar(rstd[:, :], mp[:, i, :], v_of("pool_scale", g), None,
                                                                    ALU.mult), rounded, prev_t)
                prev_t = dve(lambda e, g=g: e.tensor_tensor(m_mix_lo[:, g, :], rstd[:, :],
                                                            m_mix_hi[:, g, :].bitcast(F32), ALU.subtract), h, t1, arena_free)
                mix_ready.append([h, prev_t])
        state["rstd_free"] = prev_t
        up_done = [pool_mm, [x for r in mix_ready for x in r]]

        att2_ready = []

        def keep_tile(t):
            if t:
                att2_ready.append(t)

        for n in range(2):
            def evac_v2(b, done, s, n=n):
                box.setdefault("v", []).append(q.add("act", lambda e: e.activation(
                    m_v[:, :, n * 256:(n + 1) * 256], b, ACT.Copy), [done, arena_free], s))
            if n == 0:
                scores(0, q_t)
            scores(2 * n + 1, q_t)
            project(evac_v2, token_major=True, cols=256)
            turn(2 * n)
            scores(2 * n + 2, q_t)
            turn(2 * n + 1)
        for h in range(4, ATT2_H):
            if h + 1 < ATT2_H:
                scores(h + 1, q_t)
            keep_tile(values(h - 4, [box["v"], up_done]))
            turn(h)
        for h in range(4, ATT2_H):
            keep_tile(values(h, box["v"]))
        y_free = everything()

        def accumulate_all(m, ready, waits):
            for n in range(2):
                done = accumulate(y_tiles(4 * n, 4), m, nk=4, wide=512, waits=waits if n == 0 else (),
                                  ready=ready if n == 0 else None)
            return done

        y1 = accumulate_all((m_mix_hi, m_mix_lo), mix_ready, [y_free])
        prod = [dve(lambda e, h=h: e.tensor_tensor(dev[:, 4 * h:4 * h + 4, :], dev[:, 4 * h:4 * h + 4, :],
                                                   y_acc[:, 4 * h:4 * h + 4, :], ALU.mult), y1, gates_t)
                for h in range(2)]
        y2 = accumulate_all((m_o_hi, m_o_lo), att2_ready, [prod])
        in_done = Tok(chunk_done, stream["j"] - 4)
        merged_ready, prod2 = [], []
        for h in range(4):
            c = slice(2 * h, 2 * h + 2)
            t = dve(lambda e, c=c: e.tensor_tensor(square[:, c, :], square[:, c, :], y_acc[:, c, :], ALU.mult), y2,
                    gates_t)
            prod2.append(t)
            t = dve(lambda e, c=c: e.tensor_tensor(dev[:, c, :], dev[:, c, :], square[:, c, :], ALU.add), t, prod)
            r = split_activation(dev[:, c, :], 0, act_hi[:, c, :], act_lo[:, c, :], t, free=[in_done])
            merged_ready += [r, r]
        y_done = out_projection(merged_ready, waits=[prod2])
        state["arena_free"] = everything()

        z = residual([y_done], None, [[] for _ in range(KT)], 1.0, [x for r in merged_ready for x in r])
        keep = [act(lambda e, k=k: e.activation(res[:, k, :], dev[:, k, :], ACT.Copy), z[k]) for k in range(KT)]
        state["ps_free"] = [state["ps_free"], state["arena_free"]]
        ready, _ = rms_stage("norm_ffn", [[z[k], keep[k]] for k in range(KT)])

        ar = Arena("conv")
        cv = [ar(f"cv{i}", [P, 2, S]) for i in range(2)]
        sig = [ar(f"sig{i}", [P, S]) for i in range(2)]
        hid_hi = [ar(f"hi{i}", [P, 1, S], F32R) for i in range(2)]
        hid_lo = [ar(f"lo{i}", [P, 1, S], F32R) for i in range(2)]
        arena_free = state["arena_free"]

        def evac_conv(block, p, b, done, s, y_tok, split_tok):
            def col(name, half, tap=0):
                first = VEC[name] + 2 * FT2 * tap + FT2 * half
                if isinstance(block, int):
                    return vec[:, first + block:first + block + 1]
                return vec[:, bass.ds(block() + first, 1)]

            t = [act(lambda e, x=x: e.activation(cv[p][:, x, :], b[:, x, :], ACT.Identity, bias=col("conv_b", x),
                                                 scale=col("conv_w", x, 2)), done, split_tok, arena_free)
                 for x in range(2)]
            t1 = [dve(lambda e, x=x: e.scalar_tensor_tensor(
                out=cv[p][:, x, 1:S], in0=b[:, x, 0:S - 1], scalar=col("conv_w", x, 1), in1=cv[p][:, x, 1:S],
                op0=ALU.mult, op1=ALU.add), t) for x in range(2)]
            a = dve(lambda e: e.scalar_tensor_tensor(
                out=cv[p][:, 0, 2:S], in0=b[:, 0, 0:S - 2], scalar=col("conv_w", 0, 0), in1=cv[p][:, 0, 2:S],
                op0=ALU.mult, op1=ALU.add), t1[0])
            bb = q.add("dve", lambda e: e.scalar_tensor_tensor(
                out=cv[p][:, 1, 2:S], in0=b[:, 1, 0:S - 2], scalar=col("conv_w", 1, 0), in1=cv[p][:, 1, 2:S],
                op0=ALU.mult, op1=ALU.add), [t1[1]], s)
            t = act(lambda e: e.activation(sig[p][:, :], cv[p][:, 0, :], ACT.Sigmoid), a, split_tok)
            t = dve(lambda e: e.tensor_tensor(cv[p][:, 0, :], cv[p][:, 0, :], sig[p][:, :], ALU.mult), t, a)
            t = dve(lambda e: e.tensor_tensor(cv[p][:, 0, :], cv[p][:, 0, :], cv[p][:, 1, :], ALU.mult), t, bb)
            h = act(lambda e: e.activation(hid_hi[p][:, 0, :], cv[p][:, 0, :], ACT.Copy), t, y_tok)
            return dve(lambda e: e.tensor_tensor(hid_lo[p][:, 0, :], cv[p][:, 0, :], hid_hi[p][:, 0, :].bitcast(F32),
                                                 ALU.subtract), h, t, y_tok)

        y_done = up_down("conv", ready, z, FT2, 1, evac_conv, (hid_hi, hid_lo))

        z = residual([y_done], None, [[k] for k in keep], 1.0, state["dev_free"])
        _, xs = rms_stage("norm_final", z, next_u=False)
        for h in range(4):
            t = q.add("sp", lambda e, h=h: e.dma_start(out[:, 2 * h:2 * h + 2, :], res[:, 2 * h:2 * h + 2, :]),
                      [xs[2 * h], xs[2 * h + 1]], stored, 16)
        assert stream["j"] == len(SIZES), (stream["j"], len(SIZES))
        q.items["sp"].append((lambda e: None, [t], None, 0, None))

        block = ctx.enter_context(nc.Block())

        @block.sync
        def _(e):
            q.emit("sp", e)

        @block.tensor
        def _(e):
            q.emit("pe", e)

        @block.scalar
        def _(e):
            q.emit("act", e)

        @block.vector
        def _(e):
            q.emit("dve", e)

        @block.gpsimd
        def _(e):
            q.emit("pool", e)


def _tiles(w, c0, n, k0=0, nk=KT):
    return w[k0 * P:(k0 + nk) * P, c0:c0 + n].reshape(nk, P, n).transpose(1, 0, 2).reshape(P, nk * n)


def _weights(a):
    parts = []
    w = a["gla_w_in"][0]
    qk, v0 = 2 * GLA_H * GLA_DK, 2 * GLA_H * GLA_DK + D
    gk = np.concatenate([w[:, v0 + D:], np.zeros((D, P - GLA_RANK), np.float32)], 1)
    parts.append(_tiles(gk, 0, P))
    parts += [_tiles(w, c, 256) for c in range(0, qk + 2 * D, 256)]
    parts += [_tiles(a["gla_w_out"][0], c, 256) for c in range(0, D, 256)]

    def mlp(w1, w2):
        n = D_FF // 256
        up = [_tiles(w1, 256 * i, 256) for i in range(n)]
        down = [_tiles(w2, 0, D, 2 * i, 2) for i in range(n)]
        out = [up[0]]
        for i in range(1, n):
            out += [up[i], down[i - 1]]
        return out + [down[-1]]

    parts += mlp(a["ff_w1"][0], a["ff_w2"][0])
    parts += [_tiles(a["att_w_in"][0], c, 256) for c in range(0, 3 * D, 256)]
    parts += [_tiles(a["att_w_out"][0], c, 256) for c in range(0, D, 256)]
    parts += mlp(a["ff_w1"][1], a["ff_w2"][1])
    w = a["w_in_2"][0]
    o_pool, o_q, o_k, o_v, o_iq, o_ik, o_iw, o_g = 0, 512, 1024, 1536, 2048, 2560, 2624, 2632
    ik = w[:, o_ik:o_ik + HD]
    parts.append(_tiles(np.concatenate([ik, ik, w[:, o_iw:o_iw + IDX_H]], 1), 0, 2 * HD + IDX_H))
    for o in (o_iq, o_q, o_k):
        parts += [_tiles(w, o + c, 256) for c in (0, 256)]
    parts += [_tiles(w, o_g + c, 256) for c in range(0, 2 * D, 256)]
    for o in (o_pool, o_v):
        parts += [_tiles(w, o + c, 256) for c in (0, 256)]
    for name in ("w_pool_proj_2", "w_attn_proj_2"):
        parts += [_tiles(a[name][0], c, 512, 0, 4) for c in (0, 512)]
    parts += [_tiles(a["w_out_2"][0], c, 256) for c in range(0, D, 256)]
    w = a["w_up_2"][0]
    up = [_tiles(np.concatenate([w[:, f * P:(f + 1) * P], w[:, D_FF2 + f * P:D_FF2 + (f + 1) * P]], 1), 0, 256)
          for f in range(FT2)]
    down = [_tiles(a["w_down_2"][0], 0, D, f, 1) for f in range(FT2)]
    parts.append(up[0])
    for f in range(1, FT2):
        parts += [up[f], down[f - 1]]
    parts.append(down[-1])
    out = np.zeros((len(parts), P, CW), np.float32)
    for j, x in enumerate(parts):
        assert x.shape[1] == SIZES[j], (j, x.shape, SIZES[j])
        out[j, :, :x.shape[1]] = x
    return out


def _ada(w):
    t = w.reshape(DEPTH, KT, P, ADA_COLS // CW, CW)
    return np.ascontiguousarray(np.concatenate(
        [t[0].transpose(2, 0, 1, 3).reshape(ADA_CHUNKS, P, CW), t[1].transpose(0, 2, 1, 3).reshape(ADA_CHUNKS, P, CW)]))


def _cols(v):
    return np.ascontiguousarray(v).reshape(-1, P).T


def _rope_tables():
    half = ROT // 2
    inv = np.float32(1.0) / (np.float32(ROPE_THETA) ** (np.arange(half, dtype=np.float32) * np.float32(2.0)
                                                         / np.float32(ROT)))
    ang = (np.arange(S, dtype=np.float32)[:, None] * inv.astype(np.float32)[None, :]).astype(np.float32)
    cos, sin = np.cos(ang.astype(np.float64)).T, np.sin(ang.astype(np.float64)).T
    t = np.zeros((P, 2 * S + P), np.float32)
    t[:, 0:S] = 1.0
    for h in range(2):
        for x in range(2):
            r = slice(HD * h + half * x, HD * h + half * (x + 1))
            t[r, 0:S] = cos
            t[r, S:2 * S] = sin
        for i in range(half):
            t[HD * h + half + i, 2 * S + HD * h + i] = -1.0
            t[HD * h + i, 2 * S + HD * h + half + i] = 1.0
    return t


def kernel(**inputs):
    import concourse.bacc as bacc
    from concourse.bass_utils import run_bass_kernel_spmd

    a = {k: np.asarray(v) for k, v in inputs.items()}
    vec = np.concatenate([
        _cols(a["c"][0]), _cols(a["b_ada"]), _cols(a["ln_g"]), _cols(a["ln_b"]), _cols(a["gla_b_gk"][0]),
        _cols(a["gla_g_norm"][0]), _cols(a["att_b_in"][0]), _cols(a["pool_scale_2"][0]), _cols(a["norm_mix_g_2"][0]),
        _cols(a["norm_ffn_g_2"][0]), _cols(a["conv_b_2"][0]), _cols(a["conv_w_2"][0]), _cols(a["norm_final_g_2"])], 1)
    key, query = np.arange(S)[None, :], P + np.arange(P)[:, None]
    rel = np.clip(query - key, -MAX_REL, MAX_REL) + MAX_REL
    count = np.zeros((P, 4, 16), np.float32)
    for g, w in enumerate(POOL_WINDOWS):
        count[:, g, :] = 1.0 / np.minimum(np.arange(16) + 1, w)
    arrays = {
        "weights": _weights(a), "ada": _ada(a["w_ada"]), "vecs": np.ascontiguousarray(vec),
        "x_in": np.ascontiguousarray(a["x"][0].T.reshape(KT, P, S).transpose(1, 0, 2)),
        "w_gk2": np.ascontiguousarray(a["gla_w_gk2"][0]),
        "rel_bias": np.ascontiguousarray(a["att_rel_bias"][0][:, rel]),
        "pool_w": np.ascontiguousarray(a["pool_w_2"][0].transpose(1, 0, 2)), "rope": _rope_tables(),
        "pool_count": count,
    }
    nc = bacc.Bacc("TRN2", target_bir_lowering=False, num_devices=1)
    args = [nc.dram_tensor(k, v.shape, mybir.dt.from_np(v.dtype), kind="ExternalInput").ap() for k, v in arrays.items()]
    out = nc.dram_tensor("out", (P, KT, S), F32, kind="ExternalOutput").ap()
    build(nc, *args, out)
    r = run_bass_kernel_spmd(nc, [arrays], core_ids=[0])
    return r.results[0]["out"].transpose(1, 0, 2).reshape(D, S).T.reshape(1, S, D)
```

```python
from contextlib import ExitStack

import numpy as np
import concourse.bass as bass
from concourse import mybir

F32 = mybir.dt.float32
F32R = mybir.dt.float32r
I32 = mybir.dt.int32
ACT = mybir.ActivationFunctionType
ALU = mybir.AluOpType
AX = mybir.AxisListType

P = 128
D = 1024
KT = D // P
S = 256
ST = S // P
DEPTH = 2
CHUNK = 64
NCH = S // CHUNK
GLA_H, GLA_DK, GLA_DV, GLA_RANK = 4, 128, 256, 16
ATT_H, HD = 16, 64
MAX_REL = 128
D_FF = 4096
ALPHA = (2.0 * DEPTH) ** 0.25
LN_EPS, RMS_EPS = 1e-5, 1e-6
NEG = -1e30
TAKEN = -3e38
POOL_WINDOWS = (2, 4, 8, 16)
ATT2_H = 8
IDX_H = 8
ROT = 16
ROPE_THETA = 500000.0
TOPK = min(256, S // 4)
D_FF2 = 2816
FT2 = D_FF2 // P

CW = 2048
N_RAW, N_SPLIT, N_ADA_RING = 4, 2, 3
ADA_COLS = 6 * D
ADA_CHUNKS = KT * ADA_COLS // CW


def chunk_sizes():
    full, out = CW, []
    out += [KT * P] + [full] * 16
    out += [full] * (2 * (D_FF // 256))
    out += [full] * 16
    out += [full] * (2 * (D_FF // 256))
    out += [KT * (2 * HD + IDX_H)] + [full] * (10 + 8)
    out += [full] * 8
    out += [full] + [full, D] * (FT2 - 1) + [D]
    return out


SIZES = chunk_sizes()

VEC_PARTS = [("c", KT), ("b_ada", DEPTH * 48), ("ln_g", 4 * KT), ("ln_b", 4 * KT), ("b_gk", 4),
             ("g_norm", 8), ("att_b", 24), ("pool_scale", 4), ("norm_mix", 8), ("norm_ffn", 8),
             ("conv_b", 2 * FT2), ("conv_w", 3 * 2 * FT2), ("norm_final", 8)]
VEC = {}
_at = 0
for _name, _n in VEC_PARTS:
    VEC[_name] = _at
    _at += _n
N_VEC = _at


class Tok:

    def __init__(self, sem, base, loop=None, step=None):
        self.sem, self.base, self.loop, self.step = sem, base, loop, step

    def value(self, loop, i):
        if self.loop is None:
            return self.base
        step = self.step if self.step is not None else self.loop.per.get(self.sem, 0)
        if self.loop is loop:
            return self.base + step * i
        return self.base + step * (self.loop.n - 1)


class Lag:

    def __init__(self, tok=None, back=1):
        self.tok, self.back = tok, back

    def bind(self, tok):
        self.tok = tok

    @property
    def sem(self):
        return self.tok.sem

    def value(self, loop, i):
        step = self.tok.step if self.tok.step is not None else self.tok.loop.per[self.tok.sem]
        return self.tok.base - step * self.back + step * i


class Loop:
    def __init__(self, n):
        self.n, self.per, self.base, self.i = n, {}, {}, None


class Queues:

    def __init__(self, nc, sem):
        self.nc, self.sem = nc, sem
        self.items = {k: [] for k in ("pe", "act", "dve", "pool", "sp")}
        self.done = {k: sem(f"{k}_done") for k in self.items}
        self.count = {}
        self.loop = None

    def token(self, s, by):
        if self.loop is not None:
            self.loop.base.setdefault(s, self.count.get(s, 0))
            self.loop.per[s] = self.loop.per.get(s, 0) + by
        self.count[s] = self.count.get(s, 0) + by
        return Tok(s, self.count[s], self.loop)

    def add(self, engine, make, waits, inc=None, by=1):
        flat = []

        def spread(ws):
            for w in ws:
                if isinstance(w, (list, tuple)):
                    spread(w)
                elif w is not None:
                    flat.append(w)

        spread(waits)
        s = self.done[engine] if inc is True else inc
        tok = self.token(s, by) if s is not None else None
        self.items[engine].append((make, flat, s, by, self.loop))
        return tok

    def pe(self, make, *waits, inc=None):
        return self.add("pe", make, waits, inc)

    def act(self, make, *waits, inc=True):
        return self.add("act", make, waits, inc)

    def dve(self, make, *waits, inc=True):
        return self.add("dve", make, waits, inc)

    def pool(self, make, *waits, inc=True):
        return self.add("pool", make, waits, inc)

    def repeat(self, n, body):
        loop = Loop(n)
        marks = {k: len(v) for k, v in self.items.items()}
        self.loop = loop
        body(loop)
        self.loop = None
        for s, per in loop.per.items():
            self.count[s] += per * (n - 1)
        for k, v in self.items.items():
            inside = v[marks[k]:]
            if inside:
                v[marks[k]:] = [(loop, inside)]

    def emit(self, name, e):
        seen = {}

        def wait(w, loop):
            inside = loop is not None and w.loop is loop if isinstance(w, Tok) else True
            if inside:
                assert w.value(loop, 0) > 0
                e.wait_ge(w.sem, w.value(loop, loop.i))
                return
            v = w.value(None, None)
            if seen.get(id(w.sem), 0) < v:
                e.wait_ge(w.sem, v)
                if loop is None:
                    seen[id(w.sem)] = v

        def one(item):
            make, waits, s, by, loop = item
            for w in waits:
                wait(w, loop)
            ins = make(e)
            if s is not None:
                ins.then_inc(s, by)

        for item in self.items[name]:
            if isinstance(item[0], Loop):
                loop, inside = item
                with e.Fori(0, loop.n) as i:
                    loop.i = i
                    for x in inside:
                        one(x)
                loop.i = None
            else:
                one(item)


def build(nc, weights, ada, vecs, x_in, w_gk2, rel_bias, pool_w, rope, pool_count, out):
    with ExitStack() as ctx:
        def sb(name, shape, dt=F32):
            return ctx.enter_context(nc.sbuf_tensor(name, shape, dt))

        def sem(name):
            return ctx.enter_context(nc.semaphore(name))

        weight_raw = [sb(f"weight_raw{i}", [P, CW]) for i in range(N_RAW)]
        weight_hi = [sb(f"weight_hi{i}", [P, CW], F32R) for i in range(N_SPLIT)]
        weight_lo = [sb(f"weight_lo{i}", [P, CW], F32R) for i in range(N_SPLIT)]
        ada_raw = [sb(f"ada_raw{i}", [P, CW]) for i in range(N_ADA_RING)]
        raw_full = [sem(f"raw_full{i}") for i in range(N_RAW)]
        hi_full = [sem(f"hi_full{i}") for i in range(N_SPLIT)]
        lo_full = [sem(f"lo_full{i}") for i in range(N_SPLIT)]
        chunk_done = sem("chunk_done")
        ada_full = [sem(f"ada_full{i}") for i in range(N_ADA_RING)]
        ada_used = sem("ada_used")
        bank_free = [sem(f"bank_free{i}") for i in range(2)]
        vec_in, x_arrived, w2_in = sem("vec_in"), sem("x_arrived"), sem("w2_in")
        tables_in = [sem(f"tables_in{i}") for i in range(3)]
        stored = sem("stored")
        bias_full = [sem(f"bias_full{i}") for i in range(4)]

        ada_acc = sb("ada_acc", [P, ADA_COLS])
        res = sb("res", [P, KT, S])
        dev = sb("dev", [P, KT, S])
        act_hi = sb("act_hi", [P, KT, S], F32R)
        act_lo = sb("act_lo", [P, KT, S], F32R)
        vec = sb("vec", [P, N_VEC])
        mods = [sb(f"mods{i}", [P, 48]) for i in range(DEPTH)]
        norm_scale = sb("norm_scale", [P, 2, KT])
        gate1 = sb("gate1", [P, KT])
        c_act = sb("c_act", [P, KT])
        ident = sb("ident", [P, P])
        ones_d = sb("ones_d", [P, P])
        minus_half = sb("minus_half", [P, ST])
        root = sb("root", [P, 2 * ST])
        rstd = sb("rstd", [P, S])
        diag = rstd[:, :].rearrange("p (t n) -> p t n", t=ST)
        ones_sq = sb("ones_sq", [P, P])
        square = sb("square", [P, KT, S])
        alpha_ln = sb("alpha_ln", [P, 2, KT])
        arena_at = nc.sbuf_base
        arena_end = nc.sbuf_usable_end

        class Arena:

            def __init__(self, tag):
                self.tag, self.at = tag, arena_at

            def __call__(self, name, shape, dt=F32):
                n = 4 * int(np.prod(shape[1:]))
                t = nc.alloc_sbuf_tensor_at(f"{self.tag}_{name}", shape, dt, offset=self.at)
                self.at += (n + 31) // 32 * 32
                assert self.at <= arena_end, (self.tag, name, self.at, arena_end)
                return t

        ps = ctx.enter_context(nc.psum_tensor("ps", [P, 8, 512], F32))
        work = [ps[:, b, :] for b in range(2)]
        y_acc = ps[:, 2:6, :].rearrange("p a (b n) -> p (a b) n", b=2)
        mean_ps = ps[:, 6, 0:S]
        rstd_ps = ps[:, 6, S:2 * S]

        q = Queues(nc, sem)
        pe, act, dve, pool = q.pe, q.act, q.dve, q.pool

        def v_of(name, n=0):
            return vec[:, VEC[name] + n:VEC[name] + n + 1]

        stream = {"j": 0, "bank": 0}

        def at_chunk(s, j, slots, unit):
            step = 4 // slots * unit if q.loop else None
            return Tok(s, (j // slots + 1) * unit, q.loop, step)

        def split(j):
            split_hi(j)
            split_lo(j)

        def split_hi(j):
            r, h, size = j % N_RAW, j % N_SPLIT, SIZES[j]
            q.add("act", lambda e: e.activation(weight_hi[h][:, 0:size], weight_raw[r][:, 0:size], ACT.Copy),
                  [at_chunk(raw_full[r], j, N_RAW, 16), slot_free(j)], hi_full[h])

        def slot_free(j):
            return Tok(chunk_done, j - N_SPLIT + 1, q.loop, 4 if q.loop else None) if j >= N_SPLIT else None

        def split_lo(j, part=0, parts=1, engine="dve"):
            r, h, n = j % N_RAW, j % N_SPLIT, SIZES[j] // parts
            c = slice(part * n, (part + 1) * n)
            q.add(engine, lambda e: e.tensor_tensor(weight_lo[h][:, c], weight_raw[r][:, c],
                                                   weight_hi[h][:, c].bitcast(F32), ALU.subtract),
                  [at_chunk(hi_full[h], j, N_SPLIT, 1), slot_free(j)], lo_full[h] if part == parts - 1 else None)

        def next_chunk():
            j = stream["j"]
            stream["j"] += 1
            return j, weight_hi[j % N_SPLIT], weight_lo[j % N_SPLIT]

        def skip(n):
            stream["j"] += n

        def finished(j, on_done=None, hold=False, no_split=False, hi_only=False):
            done = Tok(chunk_done, j + 1, q.loop, 4 if q.loop else None)
            if on_done:
                on_done(done)
            if j + N_SPLIT < len(SIZES) and not no_split:
                if hold:
                    stream["held"] = j + N_SPLIT
                elif hi_only:
                    split_hi(j + N_SPLIT)
                else:
                    split(j + N_SPLIT)
            return done

        def chunk_products(j, groups, waits=(), on_done=None, hold=False, no_split=False, hi_only=False):
            hi_in = at_chunk(hi_full[j % N_SPLIT], j, N_SPLIT, 1)
            lo_in = at_chunk(lo_full[j % N_SPLIT], j, N_SPLIT, 1)
            first = True
            last = len(groups) - 1
            for n, (o, a, b, start, lo, extra) in enumerate(groups):
                w = list(extra)
                if first:
                    w += [hi_in, *waits]
                if lo == 2:
                    w.append(lo_in)
                first = False
                pe(lambda e, o=o, a=a, b=b, start=start: e.matmul(o, a, b, start=start, stop=False,
                                                                  skip_group_check=True),
                   *w, inc=chunk_done if n == last else None)
            return finished(j, on_done, hold, no_split, hi_only)

        def products_by_bank(j, groups, waits, on_bank):
            n_bank = len(groups) // KT // 3 * 2
            hi_part, lo_part = groups[:2 * len(groups) // 3], groups[2 * len(groups) // 3:]
            for b in range(KT // 2):
                part = hi_part[2 * b * n_bank:2 * (b + 1) * n_bank] + lo_part[b * n_bank:(b + 1) * n_bank]
                for n, (o, a, m, start, kind, _) in enumerate(part):
                    w = []
                    if b == n == 0:
                        w += [at_chunk(hi_full[j % N_SPLIT], j, N_SPLIT, 1), *waits]
                    if b == 0 and kind == 2:
                        w.append(at_chunk(lo_full[j % N_SPLIT], j, N_SPLIT, 1))
                    end = n == len(part) - 1
                    t = pe(lambda e, o=o, a=a, m=m, start=start: e.matmul(o, a, m, start=start, stop=False,
                                                                          skip_group_check=True),
                           *w, inc=(True if b < KT // 2 - 1 else chunk_done) if end else None)
                on_bank(b, t)
            return finished(j, hold=True)

        def products(hi, lo, wide, nk, outs, m_hi, m_lo, k0=0, ready=None, fresh=True, token_major=False):
            wh, wl = (w[:, 0:nk * wide].rearrange("p (k n) -> p k n", k=nk) for w in (hi, lo))
            first, second = [], []
            seen_banks = set()
            for n, (o, bank) in enumerate(outs):
                for k in range(nk):
                    start = fresh and k == 0 and (bank not in seen_banks)
                    if token_major:
                        t = slice(n * P, (n + 1) * P)
                        a, al, b, bl = m_hi[:, k0 + k, t], m_lo[:, k0 + k, t], wh[:, k, :], wl[:, k, :]
                        tri = [(a, b), (al, b), (a, bl)]
                    else:
                        c = slice(n * P, (n + 1) * P)
                        a, al, b, bl = wh[:, k, c], wl[:, k, c], m_hi[:, k0 + k, :], m_lo[:, k0 + k, :]
                        tri = [(a, b), (a, bl), (al, b)]
                    extra = ready[k] if ready is not None and n == 0 else ()
                    first.append((o, tri[0][0], tri[0][1], start, 0, extra))
                    first.append((o, tri[1][0], tri[1][1], False, 0, ()))
                    second.append((o, tri[2][0], tri[2][1], False, 2 if not second else 1, ()))
                    seen_banks.add(bank)
            return first + second

        def project(evac, wide=256, token_major=False, first=False, ahead=None, hi_only=False):
            j, hi, lo = next_chunk()
            w = stream["bank"]
            stream["bank"] += 1
            b = w % 2
            free = None
            if w >= 2:
                free = Tok(bank_free[b], w // 2, q.loop, 1 if q.loop else None)
            n_out = ST if token_major else wide // P
            outs = [(work[b][:, n * S:(n + 1) * S], b) for n in range(n_out)]
            take = lambda done: evac(work[b].rearrange("p (n t) -> p n t", n=2), done, bank_free[b])
            done = chunk_products(j, products(hi, lo, wide, KT, outs, act_hi, act_lo, token_major=token_major),
                                  waits=[free], on_done=take if first else ahead, hi_only=hi_only)
            if not first:
                take(done)
            return done

        def accumulate(outs, m, nk=KT, wide=256, waits=(), ready=None, on_done=None, hold=False, no_split=False):
            j, hi, lo = next_chunk()
            return chunk_products(j, products(hi, lo, wide, nk, outs, *m, ready=ready), waits, on_done, hold, no_split)

        def by_k(groups, nk):
            n = len(groups) // (3 * nk)
            hi_part, lo_part = groups[:2 * n * nk], groups[2 * n * nk:]
            out = []
            for k in range(nk):
                out.append([g for o in range(n) for g in hi_part[2 * (o * nk + k):2 * (o * nk + k) + 2]] +
                           [lo_part[o * nk + k] for o in range(n)])
            return out

        def job(outs, m, nk=KT, wide=256, waits=(), evac=None, on_done=None, no_split=False):
            j, hi, lo = next_chunk()
            return {"j": j, "on_done": on_done, "no_split": no_split, "waits": waits, "evac": evac,
                    "k": by_k(products(hi, lo, wide, nk, outs, *m), nk)}

        def project_job(evac, wide=256, no_split=False):
            w = stream["bank"]
            stream["bank"] += 1
            b = w % 2
            view = work[b].rearrange("p (n t) -> p n t", n=2)
            return job([(work[b][:, n * S:(n + 1) * S], b) for n in range(wide // P)], (act_hi, act_lo), wide=wide,
                       waits=[Tok(bank_free[b], w // 2)] if w >= 2 else [],
                       evac=lambda done: evac(view, done, bank_free[b]), no_split=no_split)

        def run_pair(one, two, ready, share=3, hook=None, fill=()):
            share = share if isinstance(share, tuple) else (share,) * KT
            seen = set()

            def emit(c, group, extra=(), last=False):
                o, a, b, start, kind, _ = group
                w = list(extra)
                if c["j"] not in seen:
                    w += [at_chunk(hi_full[c["j"] % N_SPLIT], c["j"], N_SPLIT, 1), *c["waits"]]
                    seen.add(c["j"])
                if kind and (c["j"], "lo") not in seen:
                    w.append(at_chunk(lo_full[c["j"] % N_SPLIT], c["j"], N_SPLIT, 1))
                    seen.add((c["j"], "lo"))
                pe(lambda e: e.matmul(o, a, b, start=start, stop=False, skip_group_check=True), *w,
                   inc=chunk_done if last else None)

            rest = [g for k in two["k"] for g in k]
            nk = len(one["k"])
            for k, groups in enumerate(one["k"]):
                if hook and k == hook[0]:
                    hook[1]()
                for n, g in enumerate(groups):
                    emit(one, g, [ready[k]] if n == 0 else (), last=(k, n) == (nk - 1, len(groups) - 1))
                if k < nk - 1:
                    for g in rest[:share[k]]:
                        emit(two, g)
                    rest = rest[share[k]:]
            for n, g in enumerate(rest):
                emit(two, g, last=n == len(rest) - 1)
            for f in fill:
                f()
            for c in (one, two):
                done = finished(c["j"], c["on_done"], no_split=c["no_split"])
                if c["evac"]:
                    c["evac"](done)

        def y_tiles(first, n):
            return [(y_acc[:, first + i, :], 2 + (first + i) // 2) for i in range(n)]

        GROUPS = ADA_COLS // CW
        IN_LOOP = [ADA_CHUNKS + KT * g for g in range(2)]
        ada_state = {"here": [], "to_load": [
            *range(ADA_CHUNKS), *IN_LOOP, *[n + 1 for n in IN_LOOP], *range(ADA_CHUNKS + 2 * KT, DEPTH * ADA_CHUNKS)]}

        def load_ada(slot, used=None):
            if ada_state["to_load"]:
                n = ada_state["to_load"].pop(0)
                t = q.add("pool", lambda e: e.dma_start(ada_raw[slot][:, :], ada[n]), [used], ada_full[slot], 16)
                ada_state["here"].append((n, slot, t))

        def ada_of(n):
            g = n // KT % GROUPS
            return ada_acc[:, g * CW:(g + 1) * CW]

        def ada_chunk():
            n, slot, landed = ada_state["here"].pop(0)
            k, a = n % KT, ada_of(n)
            if k == 0:
                t = q.add("dve", lambda e: e.tensor_scalar(a, ada_raw[slot][:, :], c_act[:, 0:1], None, ALU.mult),
                          [landed, ada_state["c"]], ada_used)
            else:
                t = q.add("dve", lambda e: e.scalar_tensor_tensor(
                    out=a, in0=ada_raw[slot][:, :], scalar=c_act[:, k:k + 1], in1=a, op0=ALU.mult, op1=ALU.add),
                    [landed, ada_state["tok"]], ada_used)
            ada_state["tok"] = ada_state["group", n // KT] = t
            load_ada(slot, t)

        def ada_chunks_in_loop(loop):
            assert loop.n == KT - 2
            after = []
            for first in IN_LOOP:
                n, slot, landed = ada_state["here"].pop(0)
                assert n == first + 1
                a, lag = ada_of(n), Lag()
                t = q.add("dve", lambda e, a=a, slot=slot: e.scalar_tensor_tensor(
                    out=a, in0=ada_raw[slot][:, :], scalar=c_act[:, bass.ds(loop.i + 1, 1)], in1=a, op0=ALU.mult,
                    op1=ALU.add), [Tok(landed.sem, landed.base, loop, 16), lag, ada_state["group", n // KT]], ada_used)
                lag.bind(t)
                ada_state["tok"] = ada_state["group", n // KT] = t
                t = q.add("pool", lambda e, n=n, slot=slot: e.dma_start(
                    ada_raw[slot][:, :], ada[bass.ds(loop.i + n + 1, 1), :, :].squeeze(0)), [t], ada_full[slot], 16)
                after.append((n + KT - 2, slot, t))
            ada_state["here"][:0] = after

        def mods_of(layer, g):
            first = 16 * g
            w = stream["bank"]
            stream["bank"] += 1
            bank = work[w % 2]
            free = Tok(bank_free[w % 2], w // 2) if w >= 2 else None
            for n in range(16):
                t = pe(lambda e, n=n: e.matmul(bank[:, n:n + P], ada_acc[:, (first + n) * P:(first + n + 1) * P],
                                               ones_sq[:, :], start=True, stop=True, skip_group_check=True),
                       *((ada_state["group", GROUPS * layer + g], consts, free) if n == 0 else ()),
                       inc=True if n == 15 else None)
            b = VEC["b_ada"] + 48 * layer + first
            ada_state["mods"] = q.add("dve", lambda e: e.tensor_tensor(
                mods[layer][:, first:first + 16], bank[:, 0:16], vec[:, b:b + 16], ALU.add), [t], bank_free[w % 2])
            return ada_state["mods"]

        def mod(layer, which, n=None):
            if n is None:
                return mods[layer][:, which * KT:(which + 1) * KT]
            return mods[layer][:, which * KT + n:which * KT + n + 1]

        t_vec = q.add("sp", lambda e: e.dma_start(vec[:, :], vecs), [], vec_in, 16)
        t_load = [t_vec, q.add("sp", lambda e: e.dma_start(res[:, :, :], x_in), [Tok(ada_used, 3)], x_arrived, 16)]
        for slot in range(N_ADA_RING):
            load_ada(slot)
        consts = [pool(lambda e: e.memset(ones_sq[:, :], 1.0)),
                  pool(lambda e: e.memset(ones_d[:, :], 1.0 / D)),
                  pool(lambda e: e.memset(minus_half[:, :], -0.5))]
        t = pool(lambda e: e.memset(ident[:, :], 0.0))
        consts.append(pool(lambda e: e.affine_select(out=ident[:, :], in_=ident[:, :], compare_op=ALU.not_equal,
                                                     fill=1.0, base=0, pattern=[[-1, P]], channel_multiplier=1), t))
        consts = consts[-1]

        ar = Arena("gla")
        g_q = ar("q", [P, GLA_H, S])
        g_k = ar("k", [P, GLA_H, S])
        g_v = ar("v", [P, ST, D])
        g_sg = ar("sg", [P, KT, S])
        g_la = ar("la", [P, GLA_H * S])
        g_e = ar("e", [P, GLA_H * S])
        g_en = ar("en", [P, GLA_H * S])
        g_scan = g_sg[:, 0:GLA_H, :].rearrange("p h t -> p (h t)")
        g_qn = ar("qn", [P, GLA_H, S])
        g_kn = g_en[:, :].rearrange("p (h t) -> p h t", h=GLA_H)
        g_kp = g_e[:, :].rearrange("p (h t) -> p h t", h=GLA_H)
        g_dec = ar("dec", [P, GLA_H * NCH])
        g_gk = ar("gk", [P, S])
        g_w2 = ar("w2", [GLA_RANK, GLA_H * P])
        g_fwd = ar("fwd", [P, ST * P])
        g_bwd = ar("bwd", [P, ST * P])
        a_at = [ar(f"a{i}", [P, ST, P]) for i in range(2)]
        g_st = ar("st", [P, 3, GLA_DV])
        t_w2 = q.add("sp", lambda e: e.dma_start(g_w2[:, :], w_gk2), [], w2_in, 16)

        pool(lambda e: e.memset(g_scan, 1.0))
        t = pool(lambda e: e.memset(g_fwd[:, :], 1.0))
        pool(lambda e: e.memset(g_bwd[:, :], 1.0))
        for i in range(2):
            t = pool(lambda e, i=i: e.memset(a_at[i][:, :, :], 0.0))
        scan_v = g_scan.rearrange("p (c t) -> p c t", t=CHUNK)
        fwd_v, bwd_v = (m[:, :].rearrange("p (a t) -> p a t", a=ST) for m in (g_fwd, g_bwd))
        pool(lambda e: e.memset(scan_v[:, :, 0:1], 0.0), t)
        pool(lambda e: e.affine_select(out=fwd_v, in_=fwd_v, compare_op=ALU.is_ge, fill=0.0, base=0,
                                       pattern=[[0, ST], [1, P]], channel_multiplier=-1))
        t = pool(lambda e: e.affine_select(out=bwd_v, in_=bwd_v, compare_op=ALU.is_gt, fill=0.0, base=0,
                                           pattern=[[0, ST], [-1, P]], channel_multiplier=1))
        pool(lambda e: e.memset(fwd_v[0:CHUNK, :, CHUNK:P], 0.0), t)
        gla_consts = pool(lambda e: e.memset(bwd_v[CHUNK:P, :, 0:CHUNK], 0.0), t)

        def queue_weight_loads():
            j = 0
            while j < len(SIZES):
                run = 1
                pat = SIZES[j:j + 4]
                while SIZES[j + 4 * run:j + 4 * run + 4] == pat and j >= 4:
                    run += 1
                if run >= 2:
                    j0 = j

                    def body(loop):
                        for u in range(4):
                            jj = j0 + u
                            size = SIZES[jj]
                            freed = Tok(lo_full[jj % 2], (jj - 4) // 2 + 1, q.loop, 2)
                            q.add("sp", lambda e, jj=jj, size=size: e.dma_start(
                                weight_raw[jj % 4][:, 0:size],
                                weights[bass.ds(loop.i * 4 + jj, 1), :, 0:size].squeeze(0)),
                                [freed], raw_full[jj % 4], 16)

                    q.repeat(run, body)
                    j += 4 * run
                else:
                    size = SIZES[j]
                    freed = Tok(lo_full[j % 2], (j - 4) // 2 + 1) if j >= 4 else Tok(ada_used, 5 + j)
                    q.add("sp", lambda e, j=j, size=size: e.dma_start(weight_raw[j % 4][:, 0:size],
                                                                      weights[j, :, 0:size]),
                          [freed], raw_full[j % 4], 16)
                    j += 1

        queue_weight_loads()

        def modulate(src, a, b, tmp, ready):
            def first(k):
                scale, bias = a(k), b(k) if b else 0.0
                how = ACT.Identity if b else ACT.Copy
                h = act(lambda e: e.activation(act_hi[:, k, :], src(k), how, bias=bias, scale=scale), ready(k))
                if k % 2:
                    t = act(lambda e: e.activation(tmp(k), src(k), how, bias=bias, scale=scale), ready(k))
                elif b:
                    t = dve(lambda e: e.tensor_scalar(tmp(k), src(k), scale, bias, ALU.mult, ALU.add), ready(k))
                else:
                    t = dve(lambda e: e.tensor_scalar(tmp(k), src(k), scale, None, ALU.mult), ready(k))
                return [h, t]

            def second(k, ht):
                return dve(lambda e: e.tensor_tensor(act_lo[:, k, :], tmp(k), act_hi[:, k, :].bitcast(F32),
                                                     ALU.subtract), ht)
            return first, second

        def pipelined(n, first, second, before=None):
            out, f = [], {}
            for k in range(n + 1):
                if k < n:
                    if before:
                        before(k)
                    f[k] = first(k)
                if k:
                    out.append([f[k - 1], second(k - 1, f[k - 1])])
            return out

        def root_sum(k, n, tile, tok, free=()):
            for t in range(ST):
                mm = pe(lambda e, t=t: e.matmul(ps[:, 7, t * P:(t + 1) * P], tile[:, t * P:(t + 1) * P], ones_sq[:, :],
                                                start=(k == 0 and t == 0), stop=(k == n - 1), skip_group_check=True),
                        tok if t == 0 else None, (free, state.get("mean_sq")) if k == t == 0 else None,
                        inc=True if (t, k) == (ST - 1, n - 1) else None)
            return mm

        def root_of(mm, count, eps_value, held_from=0):
            m = dve(lambda e: e.tensor_scalar(root[:, 0:ST], ps[:, 7, 0:ST * P:P], 1.0 / count, eps_value, ALU.mult,
                                              ALU.add), mm, state.get("root"))
            p = pool(lambda e: e.tensor_tensor(root[:, 2:2 + ST], root[:, 0:ST], minus_half[:, :], ALU.pow), m, consts)
            if "held" in stream:
                for part in range(held_from, 2):
                    split_lo(stream["held"], part, 2, "pool")
                stream.pop("held")
            dg = [dve(lambda e, t=t: e.tensor_scalar(diag[:, t, :], ident[:, :], root[:, 2 + t:3 + t], None, ALU.mult),
                      p, state.get("diag"), state.get("rstd_free")) for t in range(ST)]
            state["root"], state["mean_sq"] = dg, m
            return dg

        def root_spread(dst, dg, free=None):
            state["diag"] = pe(lambda e: e.matmul(dst, ones_sq[:, :], rstd[:, :], start=True, stop=True,
                                                  skip_group_check=True), dg, free, inc=True)
            return state["diag"]

        def ln_begin(gate_t, y_view=None, release=None):
            z = []
            y_view = y_view or [y_acc[:, k, :] for k in range(KT)]
            release = release or {}

            def mean(b):
                for k in (2 * b, 2 * b + 1):
                    t = pe(lambda e, k=k: e.matmul(mean_ps, ones_d[:, :], dev[:, k, :], start=(k == 0),
                                                   stop=(k == KT - 1), skip_group_check=True),
                           z[k], state["ps_free"] if k == 0 else None, inc=True if k == KT - 1 else None)
                return t

            def on_bank(b, tok):
                if b:
                    mean(b - 1)
                for k in (2 * b, 2 * b + 1):
                    z.append(q.add("dve", lambda e, k=k: e.scalar_tensor_tensor(
                        out=dev[:, k, :], in0=y_view[k], scalar=gate1[:, k:k + 1], in1=res[:, k, :],
                        op0=ALU.mult, op1=ALU.add), [tok, gate_t, state["x"][k], state["dev_free"]],
                        release.get(k, True)))
            return on_bank, z, lambda: mean(KT // 2 - 1)

        def ln_root(mean_t):
            free = state["ps_free"]
            if "held" in stream:
                split_hi(stream["held"])
                split_lo(stream["held"], 0, 2, "pool")
            cent, sq = [], []
            for h in range(KT // 2):
                c = slice(2 * h, 2 * h + 2)
                cent.append(dve(lambda e, c=c: e.tensor_tensor(
                    dev[:, c, :], dev[:, c, :], mean_ps.unsqueeze(1).broadcast_to([P, 2, S]), ALU.subtract), mean_t))
                sq.append(act(lambda e, c=c: e.activation(square[:, c, :], dev[:, c, :], ACT.Square), cent[h], free))
                for k in (2 * h, 2 * h + 1):
                    mm = root_sum(k, KT, square[:, k, :], sq[h], free)
            return (root_spread(rstd_ps, root_of(mm, D, LN_EPS, 1)),
                    [[c, s] for c, s in zip(cent, sq) for _ in range(2)])

        def layer_norm_stage(idx, closing, sc, sh, next_vec_t):
            _, z, last_mean = closing
            g0, b0 = VEC["ln_g"] + KT * idx, VEC["ln_b"] + KT * idx
            lg, lb = vec[:, g0:g0 + KT], vec[:, b0:b0 + KT]
            mean_t = last_mean()
            w = state["norm_scale_free"]
            t = dve(lambda e: e.scalar_tensor_tensor(out=norm_scale[:, 0, :], in0=sc, scalar=1.0, in1=lg,
                                                     op0=ALU.add, op1=ALU.mult), next_vec_t, *w)
            t1 = dve(lambda e: e.scalar_tensor_tensor(out=norm_scale[:, 1, :], in0=sc, scalar=1.0, in1=lb,
                                                      op0=ALU.add, op1=ALU.mult), next_vec_t, *w)
            t3 = dve(lambda e: e.tensor_scalar(alpha_ln[:, 0, :], lg, ALPHA, None, ALU.mult), *w)
            t4 = dve(lambda e: e.tensor_scalar(alpha_ln[:, 1, :], lb, ALPHA, None, ALU.mult), *w)
            t2 = dve(lambda e: e.tensor_tensor(norm_scale[:, 1, :], norm_scale[:, 1, :], sh, ALU.add), t1)
            vt = [t, t2, t3, t4]
            r, before = ln_root(mean_t)
            used = {}

            def normalise(k):
                used[k] = dve(lambda e, k=k: e.tensor_tensor(dev[:, k, :], dev[:, k, :], rstd_ps, ALU.mult), r,
                              before[k])

            first, second = modulate(lambda k: dev[:, k, :], lambda k: norm_scale[:, 0, k:k + 1],
                                     lambda k: norm_scale[:, 1, k:k + 1], lambda k: square[:, k, :],
                                     lambda k: [used[k], vt])
            ready = pipelined(KT, first, second, normalise)
            state["z"] = z
            state["norm_scale_free"] = state["dev_free"] = state["ps_free"] = [ready, used[KT - 1]]

            def late():
                state["x"] = [act(lambda e, k=k: e.activation(
                    res[:, k, :], dev[:, k, :], ACT.Identity, bias=alpha_ln[:, 1, k:k + 1],
                    scale=alpha_ln[:, 0, k:k + 1]), used[k], z[k], vt) for k in range(KT)]
                state["dev_free"] = [state["dev_free"], state["x"]]
                state["norm_scale_free"] = [state["norm_scale_free"], state["x"]]
                state["ps_free"] = [state["ps_free"], state["x"]]
            return ready, late

        def last_layer_norm(idx, closing):
            g0, b0 = VEC["ln_g"] + KT * idx, VEC["ln_b"] + KT * idx
            _, z, last_mean = closing
            r, before = ln_root(last_mean())
            x, used, sums = [], [], []
            for k in range(KT):
                g, b = vec[:, g0 + k:g0 + k + 1], vec[:, b0 + k:b0 + k + 1]
                used.append(dve(lambda e, k=k, g=g: e.scalar_tensor_tensor(
                    out=dev[:, k, :], in0=dev[:, k, :], scalar=g, in1=rstd_ps, op0=ALU.mult, op1=ALU.mult), r,
                    before[k]))
                sq = act(lambda e, k=k, b=b: e.activation(square[:, k, :], dev[:, k, :], ACT.Square, bias=b), used[k])
                x.append(dve(lambda e, k=k, b=b: e.tensor_scalar(res[:, k, :], dev[:, k, :], b, None, ALU.add),
                             used[k], z[k]))
                sums.append(sq)
                mm = root_sum(k, KT, square[:, k, :], sq)
            state["x"], state["z"], state["ps_free"], state["dev_free"] = x, z, [x, sums], [x, sums]
            return mm

        def rms_begin(x_toks):
            x, end = [], []

            def on_bank(b, tok):
                c = slice(2 * b, 2 * b + 2)
                x.append(dve(lambda e: e.tensor_tensor(res[:, c, :], y_acc[:, c, :], res[:, c, :], ALU.add),
                             tok, x_toks[2 * b], x_toks[2 * b + 1]))
                sq = act(lambda e: e.activation(square[:, c, :], res[:, c, :], ACT.Square), x[-1],
                         state["dev_free"] if b == 0 else None)
                end.append((b, sq))
                if b:
                    sums(*end[b - 1])

            def sums(b, sq):
                for k in (2 * b, 2 * b + 1):
                    mm = root_sum(k, KT, square[:, k, :], sq, state["ps_free"])
                return mm

            return on_bank, x, lambda: sums(*end[-1])

        def rms_stage(vname, x_toks, mm):
            if "held" in stream:
                split_hi(stream["held"])
            r = root_spread(rstd_ps, root_of(mm, D, RMS_EPS))

            def first(k):
                u = dve(lambda e: e.scalar_tensor_tensor(out=dev[:, k, :], in0=res[:, k, :], scalar=v_of(vname, k),
                                                         in1=rstd_ps, op0=ALU.mult, op1=ALU.mult), r, x_toks[k],
                        state["dev_free"])
                return [u, act(lambda e: e.activation(act_hi[:, k, :], dev[:, k, :], ACT.Copy), u)]

            ready = pipelined(KT, first, lambda k, ht: dve(lambda e: e.tensor_tensor(
                act_lo[:, k, :], dev[:, k, :], act_hi[:, k, :].bitcast(F32), ALU.subtract), ht))
            state["dev_free"] = state["ps_free"] = [ready]
            return ready

        state = {}

        e_c = act(lambda e: e.activation(c_act[:, :], vec[:, VEC["c"]:VEC["c"] + KT], ACT.Exp, scale=-1.0), t_vec)
        t = dve(lambda e: e.tensor_scalar(c_act[:, :], c_act[:, :], 1.0, None, ALU.add), e_c)
        t = dve(lambda e: e.reciprocal(c_act[:, :], c_act[:, :]), t)
        ada_state["c"] = dve(lambda e: e.tensor_tensor(c_act[:, :], c_act[:, :], vec[:, VEC["c"]:VEC["c"] + KT],
                                                       ALU.mult), t)
        for _ in range(KT):
            ada_chunk()
        for j in range(N_SPLIT):
            split(j)
        mt = mods_of(0, 0)
        t = dve(lambda e: e.tensor_scalar(norm_scale[:, 0, :], mod(0, 1), 1.0, None, ALU.add), mt)
        first, second = modulate(lambda k: res[:, k, :], lambda k: norm_scale[:, 0, k:k + 1], lambda k: mod(0, 0, k),
                                 lambda k: square[:, k, :], lambda k: [t, t_load])
        ready = pipelined(KT, first, second)
        state["x"] = [act(lambda e, k=k: e.activation(res[:, k, :], res[:, k, :], ACT.Copy, scale=ALPHA), ready[k])
                      for k in range(KT)]
        state["dev_free"], state["ps_free"] = [], []
        state["norm_scale_free"] = ready

        box = {}

        def evac_gk(b, done, s):
            box["gk"] = q.add("act", lambda e: e.activation(g_gk[:, :], b[:, 0, :], ACT.Copy), [done], s)

        def evac_to(dst, key, scale=1.0):
            def evac(b, done, s):
                box.setdefault(key, []).append(
                    q.add("act", lambda e: e.activation(dst, b, ACT.Copy, scale=scale), [done], s))
            return evac

        run_pair(project_job(evac_gk, wide=P), project_job(evac_to(g_q[:, 0:2, :], "q", GLA_DK ** -0.5)), ready,
                 share=6)
        gate_ps = ps[:, 2:4, :].rearrange("p a (b n) -> p (a b) n", b=2)
        for h in range(GLA_H):
            t = pe(lambda e, h=h: e.matmul(gate_ps[:, h, :], g_w2[:, h * P:(h + 1) * P], g_gk[0:GLA_RANK, :],
                                           start=True, stop=True, skip_group_check=True),
                   box["gk"], t_w2, inc=True if h == GLA_H - 1 else None)
        la = g_la[:, :]
        zt = [dve(lambda e, h=h: e.tensor_scalar(g_la[:, h * S:(h + 1) * S], gate_ps[:, h, :], v_of("b_gk", h), None,
                                                 ALU.add), t) for h in range(GLA_H)]
        gate_read = zt[-1]
        a = act(lambda e: e.activation(g_e[:, :], la, ACT.Abs), zt)
        a = act(lambda e: e.activation(g_e[:, :], g_e[:, :], ACT.Exp, scale=-1.0), a)
        a = act(lambda e: e.activation(g_e[:, :], g_e[:, :], ACT.Ln, bias=1.0), a)
        t = dve(lambda e: e.scalar_tensor_tensor(out=g_en[:, :], in0=la, scalar=0.0, in1=g_e[:, :], op0=ALU.min,
                                                 op1=ALU.subtract), a)
        cum = dve(lambda e: e.tensor_tensor_scan(out=la, data0=g_scan, data1=g_en[:, :], initial=0.0,
                                                 op0=ALU.mult, op1=ALU.add), t, gla_consts, zt, a)
        TAU = 1.0 / 16.0
        e_pos = act(lambda e: e.activation(g_e[:, :], la, ACT.Exp, scale=TAU), cum, t)
        e_neg = act(lambda e: e.activation(g_en[:, :], la, ACT.Exp, scale=-TAU), cum)
        cum4 = la.rearrange("p (c t) -> p c t", t=CHUNK)
        end_t = dve(lambda e: e.tensor_tensor(g_qn[:, :, :].rearrange("p h (c t) -> p (h c) t", t=CHUNK),
                                              cum4[:, :, CHUNK - 1:CHUNK].broadcast_to([P, GLA_H * NCH, CHUNK]), cum4,
                                              ALU.subtract), cum)
        e_end = act(lambda e: e.activation(la, g_qn[:, :, :].rearrange("p h t -> p (h t)"), ACT.Exp, scale=TAU),
                    end_t, e_pos, e_neg)
        dec_t = act(lambda e: e.activation(g_dec[:, :], g_e[:, CHUNK - 1::CHUNK], ACT.Copy), e_pos)

        e3 = lambda m: m[:, :].rearrange("p (h t) -> p h t", h=GLA_H)
        mul = lambda o, a, b: (lambda e: e.tensor_tensor(o, a, b, ALU.mult))
        qn_t, qf_t, kn_t, kp_t, ke_t = {}, {}, {}, {}, {}

        def decayed_q(n):
            c = slice(2 * n, 2 * n + 2)
            qn_t[n] = dve(mul(g_qn[:, c, :], g_q[:, c, :], e3(g_en)[:, c, :]), box["q"][n], e_neg, e_end)
            qf_t[n] = dve(mul(g_q[:, c, :], g_q[:, c, :], e3(g_e)[:, c, :]), e_pos, qn_t[n])

        def decayed_k(n):
            c = slice(2 * n, 2 * n + 2)
            kn_t[n] = dve(mul(g_kn[:, c, :], g_k[:, c, :], e3(g_en)[:, c, :]), box["k"][n], e_neg, qn_t[n])
            kp_t[n] = dve(mul(g_kp[:, c, :], g_k[:, c, :], e3(g_e)[:, c, :]), e_pos, qf_t[n], dec_t)
            ke_t[n] = dve(mul(g_k[:, c, :], g_k[:, c, :], e3(g_la)[:, c, :]), e_end, kn_t[n], kp_t[n])

        project(evac_to(g_q[:, 2:4, :], "q", GLA_DK ** -0.5))
        ada_chunk()
        project(evac_to(g_k[:, 0:2, :], "k"))
        decayed_q(0)
        decayed_k(0)
        project(evac_to(g_k[:, 2:4, :], "k"))
        decayed_q(1)
        decayed_k(1)
        a_ps = ps[:, 2, :].rearrange("p (a t) -> p a t", a=4)
        ket_ps = ps[:, 3, 0:2 * P].rearrange("p (a t) -> p a t", a=2)
        head_root_ps = ps[:, 3, 2 * P:4 * P]
        u_ps = ps[:, 4:6, :].rearrange("p a (b n) -> p (a b) n", b=2)
        o_ps = ps[:, 6, :].rearrange("p (v t) -> p v t", v=2)
        U_AT = (0, 2, 1)
        as_pair = lambda m: m.rearrange("p (a t) -> p a t", a=ST)
        a_of = [a_at[0][:, :, :], a_at[1][:, :, :], as_pair(square[:, 6, :]), as_pair(square[:, 7, :])]
        ket_of = [as_pair(square[:, 2 + h, :]) for h in range(GLA_H)]
        a_zero = [None, None] + [pool(lambda e, h=h: e.memset(square[:, 4 + h, :], 0.0), ready) for h in (2, 3)]
        gh = {}

        def gla_scores(h):
            prev = gh.get(h - 1)
            for t in range(ST):
                c = slice(t * P, (t + 1) * P)
                pe(lambda e, t=t, c=c: e.matmul(a_ps[:, t, :], g_kn[:, h, c], g_q[:, h, c], start=True, stop=True,
                                                skip_group_check=True),
                   kn_t[h // 2], qf_t[h // 2], gate_read, prev and prev["a"])
                pe(lambda e, t=t, c=c: e.matmul(a_ps[:, 2 + t, :], g_kp[:, h, c], g_qn[:, h, c], start=True,
                                                stop=True, skip_group_check=True), kp_t[h // 2], qn_t[h // 2])
            for t in range(ST):
                c = slice(t * P, (t + 1) * P)
                sc = pe(lambda e, t=t, c=c: e.matmul(ket_ps[:, t, :], g_k[:, h, c], ident[:, :], is_transpose=True,
                                                     start=True, stop=True, skip_group_check=True),
                        ke_t[h // 2], consts, prev and prev["ket"], inc=True if t else None)
            A = a_of[h]
            t = dve(lambda e: e.copy_predicated(A, fwd_v.bitcast(I32), a_ps[:, 0:2, :]), sc, gla_consts, a_zero[h])
            a2 = dve(lambda e: e.copy_predicated(A, bwd_v.bitcast(I32), a_ps[:, 2:4, :]), t)
            ket = act(lambda e: e.activation(ket_of[h], ket_ps, ACT.Copy), sc, ready)
            gh[h] = {"a": a2, "ket": ket}

        def gla_states(h):
            prev = gh.get(h - 1)
            for c in (0, 2, 1):
                p0 = CHUNK * (c % 2)
                u = pe(lambda e, c=c, p0=p0: e.matmul(u_ps[:, U_AT[c], :], ket_of[h][p0:p0 + CHUNK, c // 2, :],
                                                      g_v[p0:p0 + CHUNK, c // 2, h * GLA_DV:(h + 1) * GLA_DV],
                                                      start=True, stop=True, skip_group_check=True),
                       gh[h]["ket"], box["v"][h], prev and prev["st"], gate_read, inc=True if c == 1 else None)
            st = act(lambda e: e.activation(g_st[:, 0, :], u_ps[:, 0, :], ACT.Copy), u, prev and prev["o_mm"])
            for c in (1, 2):
                st = dve(lambda e, c=c: e.scalar_tensor_tensor(
                    out=g_st[:, c, :], in0=g_st[:, c - 1, :], scalar=g_dec[:, h * NCH + c:h * NCH + c + 1],
                    in1=u_ps[:, U_AT[c], :], op0=ALU.mult, op1=ALU.add), st, dec_t, u, prev and prev["o_mm"])
            gh[h]["st"] = st

        def gla_out(h):
            prev = gh.get(h - 1)
            first = True
            for v in range(2):
                for t in range(ST):
                    vs = slice(h * GLA_DV + v * P, h * GLA_DV + (v + 1) * P)
                    pe(lambda e, v=v, t=t, vs=vs, first=first: e.matmul(
                        o_ps[:, v, t * P:(t + 1) * P], g_v[:, t, vs], a_of[h][:, t, :], start=first, stop=False,
                        skip_group_check=True), gh[h]["a"], prev and prev["o"])
                    first = False
            for v in range(2):
                for c in range(1, NCH):
                    o_mm = pe(lambda e, v=v, c=c: e.matmul(
                        o_ps[:, v, c * CHUNK:(c + 1) * CHUNK], g_st[:, c - 1, v * P:(v + 1) * P],
                        g_q[:, h, c * CHUNK:(c + 1) * CHUNK], start=False, stop=False, skip_group_check=True),
                        gh[h]["st"], inc=True if (v, c) == (1, NCH - 1) else None)
            o = act(lambda e: e.activation(dev[:, 2 * h:2 * h + 2, :], o_ps, ACT.Copy), o_mm)
            sq = act(lambda e: e.activation(square[:, 0:2, :], dev[:, 2 * h:2 * h + 2, :], ACT.Square), o,
                     prev and prev["ms"], ready)
            gh[h].update(o_mm=o_mm, o=o, sq=sq)

        def gla_sums(h):
            for v in range(2):
                mm = root_sum(v, 2, square[:, v, :], gh[h]["sq"])
            gh[h]["ms"], gh[h]["dg"] = mm, root_of(mm, GLA_DV, RMS_EPS)

        def gla_norm(h):
            prev = gh.get(h - 1)
            r = root_spread(head_root_ps, gh[h]["dg"], [prev and prev["og"], gh[GLA_H - 1]["ket"]])
            gh[h]["og"] = dve(lambda e: e.tensor_tensor(
                dev[:, 2 * h:2 * h + 2, :], dev[:, 2 * h:2 * h + 2, :],
                head_root_ps.unsqueeze(1).broadcast_to([P, 2, S]), ALU.mult), r, gh[h]["sq"])

        def gla_step(n):
            for first, step in ((4, gla_norm), (3, gla_sums), (2, gla_out), (1, gla_states)):
                if 0 <= n - first < GLA_H:
                    step(n - first)

        for n in range(4):
            def evac_v(b, done, s, n=n):
                box.setdefault("v", []).append(
                    q.add("act", lambda e: e.activation(g_v[:, :, n * 256:(n + 1) * 256], b, ACT.Copy), [done], s))
            project(evac_v, token_major=True)
            gla_scores(n)
            gla_step(n)
            for _ in range((1, 2, 2, 1)[n]):
                ada_chunk()

        def evac_g(n):
            def evac(b, done, s):
                sg = g_sg[:, 2 * n:2 * n + 2, :]
                t = act(lambda e: e.activation(sg, b, ACT.Sigmoid), done)
                box.setdefault("sg", []).append(
                    q.add("dve", lambda e: e.tensor_tensor(sg, sg, b, ALU.mult), [t, done], s))
            return evac

        gated = {}

        def gated_head(h):
            for k in (2 * h, 2 * h + 1):
                gated[k] = dve(lambda e, k=k: e.scalar_tensor_tensor(
                    out=dev[:, k, :], in0=dev[:, k, :], scalar=v_of("g_norm", k), in1=g_sg[:, k, :], op0=ALU.mult,
                    op1=ALU.mult), gh[h]["og"], box["sg"][h])

        out_ready = []

        def out_parts(first, end):
            out_ready.extend(pipelined(
                end - first, lambda i: [gated[first + i], act(lambda e: e.activation(
                    act_hi[:, first + i, :], dev[:, first + i, :], ACT.Copy), gated[first + i], in_done[0])],
                lambda i, ht: dve(lambda e: e.tensor_tensor(
                    act_lo[:, first + i, :], dev[:, first + i, :], act_hi[:, first + i, :].bitcast(F32), ALU.subtract),
                    ht, in_done)))

        in_done = []
        for n in range(4):
            if n < 3:
                project(evac_g(n))
            else:
                project(evac_g(n), ahead=lambda done: (in_done.append(done), out_parts(0, 6)))
            gla_step(GLA_H + n)
            gated_head(n)
            for _ in range((2, 2, 2, 0)[n]):
                ada_chunk()
            if n == 2:
                mods_of(0, 1)
        out_parts(6, 8)
        last = gh[GLA_H - 1]
        y_free = [[last["a"]], [last["ket"], last["og"]], [last["st"]], [last["st"]]]

        def out_projection(ready, on_bank, ada_n=0, waits=None, where=None, hook=None, between=None, share=3):
            m = (act_hi, act_lo)
            where = where or y_tiles(0, KT)
            after = lambda n: (lambda tok: on_bank(n, tok))
            run_pair(*[job(where[2 * n:2 * n + 2], m, waits=[waits(n)], on_done=after(n)) for n in range(2)], ready,
                     hook=hook, share=share, fill=[ada_chunk] * ada_n)
            if between:
                between()
            for n in range(2, 4):
                accumulate(where[2 * n:2 * n + 2], m, waits=[waits(n)], on_done=after(n), hold=n == 3)
                if n == 2 and ada_n:
                    mods_of(0, 2)

        def everything():
            return [Tok(q.done[k], q.count[q.done[k]]) for k in ("act", "dve", "pe", "pool")
                    if q.count.get(q.done[k])] + [Tok(chunk_done, stream["j"])]

        def up_down(ready, y_read, n_blocks, n_tiles, evac_up, buffers, closing, late=None, fill=None,
                    early=False):
            hid_hi, hid_lo = buffers
            buf = {("y", 0): None, ("y", 1): None, ("split", 0): None, ("split", 1): None}
            base_j = stream["j"]

            def evac_of(i, block, mid=()):
                p = i % 2

                def evac(b, done, s):
                    buf[("split", p)] = evac_up(block, p, b, done, s, buf[("y", p)], buf[("split", p)], *mid)
                return evac

            def up(i, block, first=False):
                j = stream["j"] + 3
                mid = [lambda: split_lo(j - 1, 0, 2), lambda: split_hi(j), lambda: split_lo(j - 1, 1, 2),
                       lambda: split_lo(j)] if early and not first else ()
                project(evac_of(i, block, mid), first=first, hi_only=bool(mid))

            def down(i, fresh=False, on_bank=None, last=False):
                p = i % 2
                j, hi, lo = next_chunk()
                if on_bank:
                    return products_by_bank(j, products(hi, lo, D, n_tiles, y_tiles(0, KT), hid_hi[p], hid_lo[p],
                                                        fresh=False), [buf[("split", p)]], on_bank)
                buf[("y", p)] = chunk_products(
                    j, products(hi, lo, D, n_tiles, y_tiles(0, KT), hid_hi[p], hid_lo[p], fresh=fresh),
                    waits=[buf[("split", p)], y_read if fresh else None], no_split=early and not fresh and not last)
                return buf[("y", p)]

            after = [lambda: None, lambda: split_hi(base_j + 2), lambda: None, lambda: split_lo(base_j + 2)]
            run_pair(project_job(evac_of(0, 0, after), no_split=True), project_job(evac_of(1, 1)), ready)
            if late:
                late()
            down(0, fresh=True)
            for _ in range(2 if fill else 0):
                fill()
            n_loop = (n_blocks - 2) // 2 - 1

            def body(loop):
                lags = {}
                for key in buf:
                    lags[key] = Lag()
                    buf[key] = [lags[key], buf[key]]
                up(0, lambda: loop.i * 2 + 2)
                down(1)
                up(1, lambda: loop.i * 2 + 3)
                down(0)
                if fill:
                    ada_chunks_in_loop(loop)
                for key, lag in lags.items():
                    lag.bind(buf[key][-1] if isinstance(buf[key], list) else buf[key])

            q.repeat(n_loop, body)
            skip(4 * (n_loop - 1))
            stream["bank"] += 2 * (n_loop - 1)
            last = 2 * n_loop + 2
            up(0, last)
            if fill:
                fill()
            down(1)
            if fill:
                fill()
            up(1, last + 1, first=True)
            if fill:
                mods_of(1, 0)
            down(0, last=True)
            down(1, on_bank=closing[0])
            assert stream["j"] == base_j + 2 * n_blocks and n_blocks % 2 == 0

        def mlp(tag, ready, y_read, closing, late, fill=None):
            ar = Arena(tag)
            relu_buf = [ar(f"relu{i}", [P, 2, S]) for i in range(2)]
            sq_buf = [ar(f"sq{i}", [P, 2, S]) for i in range(2)]
            hid_hi = [ar(f"hi{i}", [P, 2, S], F32R) for i in range(2)]
            hid_lo = [ar(f"lo{i}", [P, 2, S], F32R) for i in range(2)]
            free = state["arena_free"]

            def evac_up(block, p, b, done, s, y_tok, split_tok, *mid):
                r = q.add("dve", lambda e: e.tensor_scalar(relu_buf[p][:, :, :], b, 0.0, None, ALU.max),
                          [done, split_tok, free], s)
                h = act(lambda e: e.activation(hid_hi[p][:, :, :], relu_buf[p][:, :, :], ACT.Square), r, y_tok)
                if mid:
                    mid[1]()
                t = dve(lambda e: e.tensor_tensor(sq_buf[p][:, :, :], relu_buf[p][:, :, :], relu_buf[p][:, :, :],
                                                  ALU.mult), r)
                lo = dve(lambda e: e.tensor_tensor(hid_lo[p][:, :, :], sq_buf[p][:, :, :],
                                                   hid_hi[p][:, :, :].bitcast(F32), ALU.subtract), h, t, y_tok)
                if mid:
                    mid[3]()
                return lo

            up_down(ready, y_read, D_FF // 256, 2, evac_up, (hid_hi, hid_lo), closing, late, fill)
            state["arena_free"] = everything()

        def gate_plus_one(layer, which):
            return dve(lambda e: e.tensor_scalar(gate1[:, :], mod(layer, which), 1.0, None, ALU.add),
                       ada_state["mods"], state.get("z"))

        state["dev_free"] = out_ready
        state["ps_free"] = [gh[GLA_H - 1]["og"], gh[GLA_H - 1]["o"], out_ready]
        closing = ln_begin(gate_plus_one(0, 2))
        out_projection(out_ready, closing[0], ada_n=3, waits=lambda n: y_free[n], share=(0, 0, 0, 0, 3, 6, 6))
        state["arena_free"] = everything()
        ready, late = layer_norm_stage(0, closing, mod(0, 4), mod(0, 3), ada_state["mods"])

        closing = ln_begin(gate_plus_one(0, 5))
        mlp("mlp0", ready, state["z"], closing, late, fill=ada_chunk)
        ready, late = layer_norm_stage(1, closing, mod(1, 1), mod(1, 0), ada_state["mods"])

        def attention(qs, ks, vs, n_heads, bias_of, out_tile, s_sb, pt_sb, stats, free):
            h_of = {}
            s_ps = [ps[:, 2 + i, 0:3 * P] for i in range(2)]
            pt_ps = [ps[:, 4 + i, 0:3 * P].rearrange("p (a n) -> p a n", a=3) for i in range(2)]
            o_ps = [ps[:, 6 + i, 0:S] for i in range(2)]
            n_pt = len(pt_sb)

            def part(h):
                p0 = HD * (h % 2)
                return slice(p0, p0 + HD), h // 2

            def scores(h, q_tok):
                rows, n = part(h)
                sp, s = s_ps[h % 2], s_sb[h % 2]
                old = h_of.get(h - 2, {})
                pe(lambda e: e.matmul(sp[:, 0:P], qs[rows, n, 0:P], ks[rows, n, 0:P], start=True, stop=True,
                                      skip_group_check=True), q_tok, old.get("biased"), free)
                mm = pe(lambda e: e.matmul(sp[:, P:3 * P], qs[rows, n, P:S], ks[rows, n, :], start=True, stop=True,
                                           skip_group_check=True), inc=True)
                b0, b1, b_tok = bias_of(h)
                t0 = dve(lambda e: e.scalar_tensor_tensor(out=s[:, 0:P], in0=sp[:, 0:P], scalar=HD ** -0.5, in1=b0,
                                                          op0=ALU.mult, op1=ALU.add),
                         mm, b_tok, old.get("turned"), free)
                t1 = dve(lambda e: e.scalar_tensor_tensor(out=s[:, P:3 * P], in0=sp[:, P:3 * P], scalar=HD ** -0.5,
                                                          in1=b1, op0=ALU.mult, op1=ALU.add), mm, b_tok)
                st = stats[h % 2]
                m0 = dve(lambda e: e.tensor_reduce(st[:, 0:1], s[:, 0:P], AX.X, ALU.max, negate=True), t0,
                         old.get("scaled"))
                m1 = dve(lambda e: e.tensor_reduce(st[:, 1:2], s[:, P:3 * P], AX.X, ALU.max, negate=True), t1)
                e0 = act(lambda e: e.activation(s[:, 0:P], s[:, 0:P], ACT.Exp, bias=st[:, 0:1],
                                                accum_out=st[:, 2:3]), m0)
                e1 = act(lambda e: e.activation(s[:, P:3 * P], s[:, P:3 * P], ACT.Exp, bias=st[:, 1:2],
                                                accum_out=st[:, 3:4]), m1)
                r = dve(lambda e: e.reciprocal(st[:, 4:6], st[:, 2:4]), e0, e1)
                p0 = dve(lambda e: e.tensor_scalar(s[:, 0:P], s[:, 0:P], st[:, 4:5], None, ALU.mult), r)
                p1 = dve(lambda e: e.tensor_scalar(s[:, P:3 * P], s[:, P:3 * P], st[:, 5:6], None, ALU.mult), r)
                h_of[h] = {"biased": [t0, t1], "scaled": [p0, p1]}

            def turn(h):
                s, pp = s_sb[h % 2], pt_ps[h % 2]
                old = h_of.get(h - 2, {})
                for a in range(3):
                    t = pe(lambda e, a=a: e.matmul(pp[:, a, :], s[:, a * P:(a + 1) * P], ident[:, :], is_transpose=True,
                                                   start=True, stop=True, skip_group_check=True),
                           h_of[h]["scaled"], old.get("pt"), free, inc=True if a == 2 else None)
                h_of[h]["turned"] = t
                h_of[h]["pt"] = act(lambda e: e.activation(pt_sb[h % n_pt], pp, ACT.Copy), t,
                                    h_of.get(h - n_pt, {}).get("pv"), free)

            def values(h, v_tok):
                rows, n = part(h)
                o, pt = o_ps[n % 2][rows, :], pt_sb[h % n_pt]
                vh = slice(h * HD, (h + 1) * HD)
                old = h_of.get(("out", n - 2))
                pe(lambda e: e.matmul(o[:, 0:P], vs[:, 0, vh], pt[:, 0, :], start=True, stop=False,
                                      skip_group_check=True), v_tok, h_of[h]["pt"], old, free)
                pe(lambda e: e.matmul(o[:, P:S], vs[:, 0, vh], pt[:, 1, :], start=False, stop=False,
                                      skip_group_check=True))
                h_of[h]["pv"] = t = pe(lambda e: e.matmul(o[:, P:S], vs[:, 1, vh], pt[:, 2, :], start=False, stop=True,
                                                          skip_group_check=True), inc=True)
                if h % 2:
                    h_of[("out", n)] = out_tile(n, o_ps[n % 2], [t, h_of[h - 1]["pv"]])
                    return h_of[("out", n)]

            return scores, turn, values

        ar = Arena("att")
        at_q, at_k = ar("q", [P, KT, S]), ar("k", [P, KT, S])
        at_v = ar("v", [P, ST, D])
        at_s = [ar(f"s{i}", [P, 3 * P]) for i in range(2)]
        N_PT = 8
        at_pt = [ar(f"pt{i}", [P, 3, P]) for i in range(N_PT)]
        N_BIAS = 4
        at_bias = [ar(f"bias{i}", [P, S]) for i in range(N_BIAS)]
        at_st = [ar(f"st{i}", [P, 8]) for i in range(2)]
        arena_free = state["arena_free"]
        masked = []
        box = {}

        def load_bias(h, free):
            r = h % N_BIAS
            t = q.add("pool", lambda e: e.dma_start(at_bias[r][:, :], rel_bias[h]), free, bias_full[r], 16)
            masked.append(pool(lambda e: e.memset(at_bias[r][0:CHUNK, S - CHUNK:S], NEG), t))

        for h in range(N_BIAS):
            load_bias(h, [arena_free])

        def evac_bias(dst, first):
            def evac(b, done, s):
                t = act(lambda e: e.activation(dst[:, first % KT, :], b[:, 0, :], ACT.Identity,
                                               bias=v_of("att_b", first)), done, arena_free)
                t2 = q.add("act", lambda e: e.activation(dst[:, first % KT + 1, :], b[:, 1, :], ACT.Identity,
                                                         bias=v_of("att_b", first + 1)), [done, arena_free], s)
                qk_toks.append([t, t2])
            return evac

        qk_toks, v_toks = [], []
        ATT_ADA = (2, 0, 0, 1, 1, 1, 1, 1, 1, 0, 0)

        def qk_job(n):
            return evac_bias((at_q, at_k)[n % 2], n // 2 * 2 + (n % 2) * KT)

        run_pair(project_job(qk_job(0)), project_job(qk_job(1)), ready, fill=[ada_chunk] * ATT_ADA[0])
        late()
        for n in (2, 3):
            project(qk_job(n))
            for _ in range(ATT_ADA[n - 1]):
                ada_chunk()

        def out_tile1(n, o, toks):
            return dve(lambda e: e.tensor_scalar(square[:, n, :], o, v_of("att_b", 16 + n), None, ALU.add), toks,
                       state["dev_free"])

        def bias1(h):
            b = at_bias[h % N_BIAS]
            return b[:, P:S], b[:, :], masked[h]

        scores, turn, values = attention(at_q, at_k, at_v, ATT_H, bias1, out_tile1, at_s,
                                         [x[:, :, :] for x in at_pt], at_st, [arena_free, state["ps_free"]])

        def scores1(h):
            scores(h, qk_toks[0:2 * (h // 4 + 1)])
            if h + N_BIAS < ATT_H:
                load_bias(h + N_BIAS, [Tok(q.done["dve"], q.count[q.done["dve"]])])

        out_tiles = []

        def values1(h):
            t = values(h, v_toks[h // 4])
            if t:
                out_tiles.append(t)

        def evac_v1(n):
            def evac(b, done, s):
                v_toks.append(q.add("act", lambda e: e.activation(
                    at_v[:, :, n * 256:(n + 1) * 256], b, ACT.Copy), [done, arena_free], s))
            return evac

        before = []
        for slot, heads in enumerate([(0, 1), (2,), (3,), (4,), (5,), (6, 7), (8, 9), (10, 11)]):
            for h in heads:
                scores1(h)
            if slot < 4:
                project(evac_v1(slot), token_major=True)
            else:
                project(qk_job(slot))
            for _ in range(ATT_ADA[3 + slot]):
                ada_chunk()
            for h in before:
                values1(h)
            for h in heads:
                turn(h)
            before = heads
        in_done = Tok(chunk_done, stream["j"])
        scores1(12)
        scores1(13)
        for h in before:
            values1(h)
        mods_of(1, 1)
        turn(12)
        turn(13)
        scores1(14)
        scores1(15)
        values1(12)
        values1(13)
        mods_of(1, 2)
        turn(14)
        turn(15)

        def hi_part(n):
            return act(lambda e: e.activation(act_hi[:, n, :], square[:, n, :], ACT.Copy), out_tiles[n], in_done)

        def lo_part(n, hi):
            return dve(lambda e: e.tensor_tensor(act_lo[:, n, :], square[:, n, :], act_hi[:, n, :].bitcast(F32),
                                                 ALU.subtract), hi, in_done)

        his = [hi_part(n) for n in range(7)]
        att_ready = [[h, lo_part(n, h)] for n, h in enumerate(his)]

        def last_heads():
            values1(14)
            values1(15)
            h = hi_part(7)
            att_ready.append([h, lo_part(7, h)])

        state["dev_free"] = [state["dev_free"], att_ready]
        first_bank = [stream["bank"] % 2, (stream["bank"] + 1) % 2]
        uses = [Tok(bank_free[b], (stream["bank"] + i) // 2) for i, b in enumerate(first_bank)]
        stream["bank"] += 2
        y_view = [work[first_bank[k // 2]][:, (k % 2) * S:(k % 2 + 1) * S] if k < 4 else y_acc[:, k, :]
                  for k in range(KT)]
        y_where = [(y_view[k], first_bank[k // 2] if k < 4 else 2 + k // 2) for k in range(KT)]
        closing = ln_begin(gate_plus_one(1, 2), y_view, {k: bank_free[first_bank[k // 2]] for k in (1, 3)})
        fr = []
        out_projection(att_ready, closing[0], waits=lambda n: uses[n] if n < 2 else fr, where=y_where,
                       hook=(6, last_heads), between=lambda: fr.append(everything()))
        state["arena_free"] = fr
        ready, late = layer_norm_stage(2, closing, mod(1, 4), mod(1, 3), ada_state["mods"])
        closing = ln_begin(gate_plus_one(1, 5))
        mlp("mlp1", ready, state["z"], closing, late)
        sums = last_layer_norm(3, closing)

        ready = rms_stage("norm_mix", state["x"], sums)

        ar = Arena("mix")
        arena_free = state["arena_free"]
        m_tab = ar("rope", [P, 2 * S + P])
        m_cnt = ar("cnt", [P, 4, 16])
        m_pw = ar("pw", [P, 4, P])
        iq_at = ar.at
        m_iq = ar("iq", [P, 4, S])
        m_up = ar("up", [P, 4, S])
        m_ik = ar("ik", [P, S])
        m_iw = ar("iw", [P, ST, IDX_H])
        m_iw_rows = ar("iw_rows", [P, S])
        m_q, m_k = ar("q", [P, 4, S]), ar("k", [P, 4, S])
        m_v = ar("v", [P, ST, 512])
        mix_at = ar.at
        m_mix_hi, m_mix_lo = ar("mix_hi", [P, 4, S], F32R), ar("mix_lo", [P, 4, S], F32R)
        m_score, m_mask = ar("score", [P, 3 * P]), ar("mask", [P, 3 * P])
        m_top = ar("top", [P, 2, 8])
        m_s = [ar(f"s{i}", [P, 3 * P]) for i in range(2)]
        m_st = [ar(f"st{i}", [P, 8]) for i in range(2)]
        m_pt = [ar(f"pt{i}", [P, 3, P]) for i in range(3)]
        pool_tmp = m_iw_rows
        m_o_lo = ar("o_lo", [P, 4, S], F32R)
        m_o_hi = nc.alloc_sbuf_tensor_at("mix_o_hi", [P, 4, S], F32R, offset=iq_at)
        relu_tmp = [nc.alloc_sbuf_tensor_at(f"mix_relu{i}", [P, 3 * P], F32, offset=mix_at + 4 * 3 * P * i)
                    for i in range(2)]
        relu_tmp = [x[:, :] for x in relu_tmp]
        rope_tmp = [nc.alloc_sbuf_tensor_at(f"mix_rope{i}", [P, 2, S], F32, offset=mix_at + 4 * (4 + 2 * i) * S)
                    for i in range(2)]
        t_tab = [q.add("pool", lambda e, a=a, b=b: e.dma_start(a, b), [arena_free], s, 16)
                 for a, b, s in ((m_tab[:, :], rope, tables_in[0]), (m_cnt[:, :, :], pool_count, tables_in[1]),
                                 (m_pw[:, :, :], pool_w, tables_in[2]))]
        cos_t, sin_t, rot_t = m_tab[:, 0:S], m_tab[:, S:2 * S], m_tab[:, 2 * S:2 * S + P]
        m_ps_free = state["ps_free"]
        box = {}

        wide = 2 * HD + IDX_H

        def index_job():
            j, hi, lo = next_chunk()
            wh, wl = (w[:, 0:KT * wide].rearrange("p (k n) -> p k n", k=KT) for w in (hi, lo))
            w = stream["bank"]
            stream["bank"] += 1
            bank = work[w % 2]
            by_tile = []
            for k in range(KT):
                g = []
                for o, c in ((bank[:, 0:S], slice(0, P)), (bank[0:IDX_H, S:2 * S], slice(P, P + IDX_H))):
                    g += [(o, wh[:, k, c], act_hi[:, k, :], k == 0 and c.start == 0, 0, ()),
                          (o, wh[:, k, c], act_lo[:, k, :], False, 0, ()),
                          (o, wl[:, k, c], act_hi[:, k, :], False, 1, ())]
                by_tile.append(g)

            def evac(done):
                box["ik"] = act(lambda e: e.activation(m_ik[:, :], bank[:, 0:S], ACT.Copy), done, arena_free)
                box["iw"] = q.add("act", lambda e: e.activation(
                    m_iw_rows[0:IDX_H, :], bank[0:IDX_H, S:2 * S], ACT.Copy, scale=IDX_H ** -0.5), [done, arena_free],
                    bank_free[w % 2])
            return {"j": j, "waits": [Tok(bank_free[w % 2], w // 2)], "on_done": None, "no_split": False,
                    "evac": evac, "k": by_tile}

        rope_state = {"free": [m_ps_free, arena_free]}

        def rope_tiles(x, n, tok):
            rp = ps[:, 7, 0:n * S].rearrange("p (a t) -> p a t", a=n)
            mm = pe(lambda e: e.matmul(rp, rot_t, x, start=True, stop=True, skip_group_check=True), tok, t_tab,
                    rope_state["free"], inc=True)
            a, b = rope_tmp[0][:, 0:n, :], rope_tmp[1][:, 0:n, :]
            cb, sbb = (v.unsqueeze(1).broadcast_to([P, n, S]) for v in (cos_t, sin_t))
            t1 = dve(lambda e: e.tensor_tensor(a, x, cb, ALU.mult), tok, t_tab, rope_state["free"])
            t2 = dve(lambda e: e.tensor_tensor(b, rp, sbb, ALU.mult), mm)
            t3 = dve(lambda e: e.tensor_tensor(x, a, b, ALU.add), t1, t2)
            rope_state["free"] = [t3]
            return t3

        def evac_plain(dst, first, key, n=2):
            def evac(b, done, s):
                box.setdefault(key, []).append(q.add("act", lambda e: e.activation(
                    dst[:, first:first + n, :], b[:, 0:n, :], ACT.Copy), [done, arena_free], s))
            return evac

        background = []

        def drip(n):
            for _ in range(min(n, len(background))):
                background.pop(0)()

        run_pair(index_job(), project_job(evac_plain(m_iq, 0, "iq")), ready)
        iw_ps = ps[:, 6, 0:ST * IDX_H].rearrange("p (t h) -> p t h", t=ST)
        for t in range(ST):
            mm = pe(lambda e, t=t: e.matmul(iw_ps[:, t, :], m_iw_rows[0:IDX_H, t * P:(t + 1) * P],
                                            ident[0:IDX_H, 0:IDX_H], is_transpose=True, start=True, stop=True,
                                            skip_group_check=True), box["iw"], m_ps_free, inc=True if t else None)
        iw_t = act(lambda e: e.activation(m_iw[:, :, :], iw_ps, ACT.Copy), mm, arena_free)
        ik_t = rope_tiles(m_ik[:, :].unsqueeze(1), 1, box["ik"])
        project(evac_plain(m_iq, 2, "iq"))
        iq_t = [rope_tiles(m_iq[:, 0:2, :], 2, box["iq"][0])]
        project(evac_plain(m_q, 0, "q"))
        iq_t.append(rope_tiles(m_iq[:, 2:4, :], 2, box["iq"][1]))

        idx = {}

        def index_scores(h):
            rows = slice(HD * (h % 2), HD * (h % 2) + HD)
            sp = ps[:, 2 + h % 2, 0:3 * P]
            rel = relu_tmp[h % 2]
            n = h // 2
            old = idx.get(h - 2, {})
            pe(lambda e: e.matmul(sp[:, 0:P], m_iq[rows, n, 0:P], m_ik[rows, 0:P], start=True, stop=True,
                                  skip_group_check=True), iq_t[n // 2], ik_t, old.get("relu"), m_ps_free)
            mm = pe(lambda e: e.matmul(sp[:, P:3 * P], m_iq[rows, n, P:S], m_ik[rows, :], start=True, stop=True,
                                       skip_group_check=True), inc=True)
            r = act(lambda e: e.activation(rel, sp, ACT.Relu, scale=HD ** -0.5), mm, old.get("sum"), arena_free)
            t = []
            for a, cols in ((0, slice(0, P)), (1, slice(P, 3 * P))):
                w = m_iw[:, a, h:h + 1]
                if h == 0:
                    t.append(dve(lambda e, w=w, cols=cols: e.tensor_scalar(m_score[:, cols], rel[:, cols], w, None,
                                                                           ALU.mult), r, iw_t, arena_free))
                else:
                    t.append(dve(lambda e, w=w, cols=cols: e.scalar_tensor_tensor(
                        out=m_score[:, cols], in0=rel[:, cols], scalar=w, in1=m_score[:, cols], op0=ALU.mult,
                        op1=ALU.add), r, idx[h - 1]["sum"]))
            idx[h] = {"relu": r, "sum": t, "mm": mm}

        for h in range(4):
            index_scores(h)
        project(evac_plain(m_q, 2, "q"))
        for h in range(4, IDX_H):
            index_scores(h)

        causal = []
        for a, cols, n in ((0, slice(0, P), P), (1, slice(P, 3 * P), S)):
            causal.append(pool(lambda e, cols=cols, n=n, a=a: e.affine_select(
                out=m_score[:, cols], in_=m_score[:, cols], compare_op=ALU.is_ge, fill=NEG, base=a * P,
                pattern=[[-1, n]], channel_multiplier=1), idx[IDX_H - 1]["sum"][a]))
        top_state = {"t": list(causal)}

        def top_max(a, cols):
            def f():
                top_state["t"][a] = dve(lambda e: e.max(m_top[:, a, :], m_score[:, cols]), top_state["t"][a])
            return f

        def top_mark(a, cols):
            def f():
                top_state["t"][a] = dve(lambda e: e.match_replace(m_score[:, cols], m_top[:, a, :], m_score[:, cols],
                                                                  TAKEN), top_state["t"][a])
            return f

        halves = ((0, slice(0, P)), (1, slice(P, 3 * P)))
        for _ in range(TOPK // 8):
            background += [top_max(*x) for x in halves] + [top_mark(*x) for x in halves]
        project(evac_plain(m_k, 0, "k"))
        q_t = [rope_tiles(m_q[:, 0:2, :], 2, box["q"][0])]
        drip(4)
        project(evac_plain(m_k, 2, "k"))
        q_t.append(rope_tiles(m_q[:, 2:4, :], 2, box["q"][1]))
        drip(4)
        for n in range(2):
            project(evac_plain(m_up, 2 * n, "up"))
            q_t.append(rope_tiles(m_k[:, 2 * n:2 * n + 2, :], 2, box["k"][n]))
            drip(6)

        def evac_v2(n):
            def evac(b, done, s):
                box.setdefault("v", []).append(q.add("act", lambda e: e.activation(
                    m_v[:, :, n * 256:(n + 1) * 256], b, ACT.Copy), [done, arena_free], s))
            return evac

        for n in range(2):
            project(evac_v2(n), token_major=True)
            drip(6)
        drip(99)
        t = dve(lambda e: e.tensor_scalar(m_mask[:, :], m_score[:, :], TAKEN / 2, NEG, ALU.is_gt, ALU.mult),
                top_state["t"], arena_free)
        mask_t = [pool(lambda e, cols=cols, n=n, a=a: e.affine_select(
            out=m_mask[:, cols], in_=m_mask[:, cols], compare_op=ALU.is_ge, fill=NEG, base=a * P,
            pattern=[[-1, n]], channel_multiplier=1), t)
            for a, cols, n in ((0, slice(0, P), P), (1, slice(P, 3 * P), S))]

        def out_tile2(n, o, toks):
            h = act(lambda e: e.activation(m_o_hi[:, n, :], o, ACT.Copy), toks, iq_done)
            return [h, dve(lambda e: e.tensor_tensor(m_o_lo[:, n, :], o, m_o_hi[:, n, :].bitcast(F32), ALU.subtract),
                           h)]

        scores, turn, values = attention(
            m_q, m_k, m_v, ATT2_H, lambda h: (m_mask[:, 0:P], m_mask[:, P:3 * P], mask_t), out_tile2, m_s,
            [x[:, :, :] for x in m_pt], m_st,
            [rope_state["free"], idx[IDX_H - 1]["sum"], idx[IDX_H - 2]["relu"], idx[IDX_H - 1]["relu"]])
        iq_done = [idx[IDX_H - 1]["mm"]]

        def pool_group(g, first_tok):
            u = m_up[:, g, :]
            a, t = u, first_tok
            bufs = [rstd[:, :], pool_tmp[:, :]]
            for i in range(g + 1):
                sh = 1 << i
                o = bufs[i % 2]
                t1 = dve(lambda e, o=o, a=a, sh=sh: e.tensor_tensor(o[:, sh:S], a[:, sh:S], a[:, 0:S - sh], ALU.add), t)
                t2 = dve(lambda e, o=o, a=a, sh=sh: e.tensor_copy(o[:, 0:sh], a[:, 0:sh]), t)
                a, t = o, [t1, t2]
            o = bufs[(g + 1) % 2]
            t1 = dve(lambda e: e.tensor_tensor(o[:, 0:16], a[:, 0:16], m_cnt[:, g, :], ALU.mult), t, t_tab)
            t2 = dve(lambda e: e.tensor_tensor(u[:, 0:16], o[:, 0:16], u[:, 0:16], ALU.subtract), t1)
            t3 = dve(lambda e: e.scalar_tensor_tensor(out=u[:, 16:S], in0=a[:, 16:S], scalar=1.0 / POOL_WINDOWS[g],
                                                      in1=u[:, 16:S], op0=ALU.mult, op1=ALU.subtract), t)
            return [t2, t3]

        pool_state = {"t": [box["up"], arena_free, state["diag"]], "ready": []}
        mix_free = [rope_state["free"], idx[IDX_H - 1]["sum"], idx[IDX_H - 2]["sum"]]

        def pool_half(half):
            w = stream["bank"]
            stream["bank"] += 1
            mp = work[w % 2].rearrange("p (a t) -> p a t", a=2)
            for i in range(2):
                g = 2 * half + i
                t = pe(lambda e, g=g, i=i: e.matmul(mp[:, i, :], m_pw[:, g, :], m_up[:, g, :], start=True,
                                                    stop=True, skip_group_check=True),
                       pooled[g], t_tab, Tok(bank_free[w % 2], w // 2), inc=True if i else None)
            rounded = [act(lambda e, g=g, i=i: e.activation(m_mix_hi[:, g, :], mp[:, i, :], ACT.Copy,
                                                            scale=v_of("pool_scale", g)), t, arena_free, mix_free)
                       for i, g in enumerate((2 * half, 2 * half + 1))]
            for i in range(2):
                g, h = 2 * half + i, rounded[i]
                t1 = q.add("dve", lambda e, g=g, i=i: e.tensor_scalar(rstd[:, :], mp[:, i, :], v_of("pool_scale", g),
                                                                      None, ALU.mult),
                           [rounded, pool_state["t"]], bank_free[w % 2] if i else True)
                t2 = dve(lambda e, g=g: e.tensor_tensor(m_mix_lo[:, g, :], rstd[:, :], m_mix_hi[:, g, :].bitcast(F32),
                                                        ALU.subtract), h, t1, arena_free, mix_free)
                pool_state["t"] = t2
                pool_state["ready"].append([h, t2])

        pooled = {}

        def pool_means(g):
            pooled[g] = pool_state["t"] = pool_group(g, pool_state["t"])

        gates_raw = []
        gate_free = state["dev_free"]

        def evac_gate(n):
            def evac(b, done, s):
                g = (dev if n < 4 else square)[:, (2 * n) % KT:(2 * n) % KT + 2, :]
                gates_raw.append(q.add("act", lambda e: e.activation(g, b, ACT.Copy), [done, gate_free], s))
            return evac

        att2_ready = []
        for h in range(ATT2_H):
            scores(h, q_t)
            project(evac_gate(h))
            if h < 4:
                pool_means(h)
            if h in (4, 5):
                pool_half(h - 4)
            if h:
                if h == 1:
                    turn(0)
                t = values(h - 1, box["v"])
                att2_ready += [t] if t else []
                turn(h)
        att2_ready.append(values(ATT2_H - 1, box["v"]))
        y_free = everything()
        sig = [act(lambda e, m=m, h=h: e.activation(m[:, 4 * h:4 * h + 4, :], m[:, 4 * h:4 * h + 4, :], ACT.Sigmoid),
                   gates_raw) for m in (dev, square) for h in range(2)]
        state["rstd_free"] = pool_state["t"]

        prod, merged_ready, prod2 = [], [], []

        def gate_pool(h):
            c = slice(4 * h, 4 * h + 4)
            return lambda tok: prod.append(dve(lambda e: e.tensor_tensor(dev[:, c, :], dev[:, c, :], y_acc[:, 0:4, :],
                                                                         ALU.mult), tok, sig[h]))

        in_done = Tok(chunk_done, stream["j"])

        def merge(h):
            def f(tok):
                after = stream["j"] - 1 + N_SPLIT
                split_hi(after)
                cs = [slice(4 * h + 2 * i, 4 * h + 2 * i + 2) for i in range(2)]
                a = [dve(lambda e, i=i, c=c: e.tensor_tensor(
                    square[:, c, :], square[:, c, :], y_acc[:, 4 + 2 * i:6 + 2 * i, :], ALU.mult), tok, sig[2 + h])
                    for i, c in enumerate(cs)]
                prod2.append(a)
                b = [dve(lambda e, c=c: e.tensor_tensor(dev[:, c, :], dev[:, c, :], square[:, c, :], ALU.add), t,
                         prod[h]) for c, t in zip(cs, a)]
                hi = [act(lambda e, c=c: e.activation(act_hi[:, c, :], dev[:, c, :], ACT.Copy), t, in_done)
                      for c, t in zip(cs, b)]
                for c, t in zip(cs, hi):
                    r = [t, dve(lambda e, c=c: e.tensor_tensor(act_lo[:, c, :], dev[:, c, :],
                                                               act_hi[:, c, :].bitcast(F32), ALU.subtract), t)]
                    merged_ready.extend([r, r])
                split_lo(after)
            return f

        for h in range(2):
            accumulate(y_tiles(0, 4), (m_mix_hi, m_mix_lo), nk=4, wide=512, waits=[y_free, prod[-1:]],
                       ready=pool_state["ready"] if h == 0 else None, on_done=gate_pool(h))
            accumulate(y_tiles(4, 4), (m_o_hi, m_o_lo), nk=4, wide=512, waits=[prod2[-1:]],
                       ready=att2_ready if h == 0 else None, on_done=merge(h), no_split=True)
        on_bank, x_tiles, last_sums = rms_begin(state["x"])
        state["dev_free"] = merged_ready
        state["ps_free"] = [state["ps_free"], y_free]
        out_projection(merged_ready, on_bank, waits=lambda n: prod[1] if n < 2 else prod2[1],
                       share=0)
        state["arena_free"] = everything()
        state["x"] = [x for x in x_tiles for _ in range(2)]
        ready = rms_stage("norm_ffn", state["x"], last_sums())

        ar = Arena("conv")
        cv = [ar(f"cv{i}", [P, 2, S]) for i in range(2)]
        sig = [ar(f"sig{i}", [P, S]) for i in range(2)]
        hid_hi = [ar(f"hi{i}", [P, 1, S], F32R) for i in range(2)]
        hid_lo = [ar(f"lo{i}", [P, 1, S], F32R) for i in range(2)]
        arena_free = state["arena_free"]

        def evac_conv(block, p, b, done, s, y_tok, split_tok, *mid):
            def col(name, half, tap=0):
                first = VEC[name] + 2 * FT2 * tap + FT2 * half
                if isinstance(block, int):
                    return vec[:, first + block:first + block + 1]
                return vec[:, bass.ds(block() + first, 1)]

            t = [act(lambda e, x=x: e.activation(cv[p][:, x, :], b[:, x, :], ACT.Identity, bias=col("conv_b", x),
                                                 scale=col("conv_w", x, 2)), done, split_tok, arena_free)
                 for x in range(2)]
            if mid:
                mid[0]()
                mid[1]()
            t1 = [dve(lambda e, x=x: e.scalar_tensor_tensor(
                out=cv[p][:, x, 1:S], in0=b[:, x, 0:S - 1], scalar=col("conv_w", x, 1), in1=cv[p][:, x, 1:S],
                op0=ALU.mult, op1=ALU.add), t) for x in range(2)]
            a = dve(lambda e: e.scalar_tensor_tensor(
                out=cv[p][:, 0, 2:S], in0=b[:, 0, 0:S - 2], scalar=col("conv_w", 0, 0), in1=cv[p][:, 0, 2:S],
                op0=ALU.mult, op1=ALU.add), t1[0])
            bb = q.add("dve", lambda e: e.scalar_tensor_tensor(
                out=cv[p][:, 1, 2:S], in0=b[:, 1, 0:S - 2], scalar=col("conv_w", 1, 0), in1=cv[p][:, 1, 2:S],
                op0=ALU.mult, op1=ALU.add), [t1[1]], s)
            t = act(lambda e: e.activation(sig[p][:, :], cv[p][:, 0, :], ACT.Sigmoid), a, split_tok)
            if mid:
                mid[2]()
            t = dve(lambda e: e.tensor_tensor(cv[p][:, 0, :], cv[p][:, 0, :], sig[p][:, :], ALU.mult), t, a)
            t = dve(lambda e: e.tensor_tensor(cv[p][:, 0, :], cv[p][:, 0, :], cv[p][:, 1, :], ALU.mult), t, bb)
            h = act(lambda e: e.activation(hid_hi[p][:, 0, :], cv[p][:, 0, :], ACT.Copy), t, y_tok)
            lo = dve(lambda e: e.tensor_tensor(hid_lo[p][:, 0, :], cv[p][:, 0, :], hid_hi[p][:, 0, :].bitcast(F32),
                                               ALU.subtract), h, t, y_tok)
            if mid:
                mid[3]()
            return lo

        on_bank, x_tiles, last_sums = rms_begin(state["x"])
        up_down(ready, state["x"], FT2, 1, evac_conv, (hid_hi, hid_lo), [on_bank], early=True)

        stream.pop("held", None)
        r = root_spread(rstd_ps, root_of(last_sums(), D, RMS_EPS))
        t = [None] * KT
        for k in range(KT):
            t[k] = dve(lambda e, k=k: e.scalar_tensor_tensor(
                out=res[:, k, :], in0=res[:, k, :], scalar=v_of("norm_final", k), in1=rstd_ps, op0=ALU.mult,
                op1=ALU.mult), r, x_tiles[k // 2])
        for h in range(4):
            t_out = q.add("sp", lambda e, h=h: e.dma_start(out[:, 2 * h:2 * h + 2, :], res[:, 2 * h:2 * h + 2, :]),
                          [t[2 * h + 1]], stored, 16)
        assert stream["j"] == len(SIZES) and not ada_state["here"] and not ada_state["to_load"]
        q.items["sp"].append((lambda e: None, [t_out], None, 0, None))

        block = ctx.enter_context(nc.Block())

        @block.sync
        def _(e):
            q.emit("sp", e)

        @block.tensor
        def _(e):
            q.emit("pe", e)

        @block.scalar
        def _(e):
            q.emit("act", e)

        @block.vector
        def _(e):
            q.emit("dve", e)

        @block.gpsimd
        def _(e):
            q.emit("pool", e)


def _tiles(w, c0, n, k0=0, nk=KT):
    return w[k0 * P:(k0 + nk) * P, c0:c0 + n].reshape(nk, P, n).transpose(1, 0, 2).reshape(P, nk * n)


def _weights(a):
    parts = []
    w = a["gla_w_in"][0]
    qk, v0 = 2 * GLA_H * GLA_DK, 2 * GLA_H * GLA_DK + D
    gk = np.concatenate([w[:, v0 + D:], np.zeros((D, P - GLA_RANK), np.float32)], 1)
    parts.append(_tiles(gk, 0, P))
    parts += [_tiles(w, c, 256) for c in range(0, qk + 2 * D, 256)]
    parts += [_tiles(a["gla_w_out"][0], c, 256) for c in range(0, D, 256)]

    def mlp(w1, w2):
        n = D_FF // 256
        up = [_tiles(w1, 256 * i, 256) for i in range(n)]
        down = [_tiles(w2, 0, D, 2 * i, 2) for i in range(n)]
        out = [up[0]]
        for i in range(1, n):
            out += [up[i], down[i - 1]]
        return out + [down[-1]]

    parts += mlp(a["ff_w1"][0], a["ff_w2"][0])
    qk, v = [[c + D * x for c in range(0, D, 256) for x in (0, 1)], range(2 * D, 3 * D, 256)]
    parts += [_tiles(a["att_w_in"][0], c, 256) for c in [*qk[:4], *v, *qk[4:]]]
    parts += [_tiles(a["att_w_out"][0], c, 256) for c in range(0, D, 256)]
    parts += mlp(a["ff_w1"][1], a["ff_w2"][1])
    w = a["w_in_2"][0]
    o_pool, o_q, o_k, o_v, o_iq, o_ik, o_iw, o_g = 0, 512, 1024, 1536, 2048, 2560, 2624, 2632
    ik = w[:, o_ik:o_ik + HD]
    parts.append(_tiles(np.concatenate([ik, ik, w[:, o_iw:o_iw + IDX_H]], 1), 0, 2 * HD + IDX_H))
    for o in (o_iq, o_q, o_k, o_pool, o_v):
        parts += [_tiles(w, o + c, 256) for c in (0, 256)]
    parts += [_tiles(w, o_g + c, 256) for c in range(0, 2 * D, 256)]
    parts += [_tiles(a[name][0], c, 512, 0, 4) for c in (0, 512) for name in ("w_pool_proj_2", "w_attn_proj_2")]
    parts += [_tiles(a["w_out_2"][0], c, 256) for c in range(0, D, 256)]
    w = a["w_up_2"][0]
    up = [_tiles(np.concatenate([w[:, f * P:(f + 1) * P], w[:, D_FF2 + f * P:D_FF2 + (f + 1) * P]], 1), 0, 256)
          for f in range(FT2)]
    down = [_tiles(a["w_down_2"][0], 0, D, f, 1) for f in range(FT2)]
    parts.append(up[0])
    for f in range(1, FT2):
        parts += [up[f], down[f - 1]]
    parts.append(down[-1])
    out = np.zeros((len(parts), P, CW), np.float32)
    for j, x in enumerate(parts):
        assert x.shape[1] == SIZES[j], (j, x.shape, SIZES[j])
        out[j, :, :x.shape[1]] = x
    return out


def _ada(w):
    return np.ascontiguousarray(w.reshape(DEPTH, KT, P, ADA_COLS // CW, CW).transpose(0, 3, 1, 2, 4)).reshape(-1, P, CW)


def _cols(v):
    return np.ascontiguousarray(v).reshape(-1, P).T


def _rope_tables():
    half = ROT // 2
    inv = np.float32(1.0) / (np.float32(ROPE_THETA) ** (np.arange(half, dtype=np.float32) * np.float32(2.0)
                                                         / np.float32(ROT)))
    ang = (np.arange(S, dtype=np.float32)[:, None] * inv.astype(np.float32)[None, :]).astype(np.float32)
    cos, sin = np.cos(ang.astype(np.float64)).T, np.sin(ang.astype(np.float64)).T
    t = np.zeros((P, 2 * S + P), np.float32)
    t[:, 0:S] = 1.0
    for h in range(2):
        for x in range(2):
            r = slice(HD * h + half * x, HD * h + half * (x + 1))
            t[r, 0:S] = cos
            t[r, S:2 * S] = sin
        for i in range(half):
            t[HD * h + half + i, 2 * S + HD * h + i] = -1.0
            t[HD * h + i, 2 * S + HD * h + half + i] = 1.0
    return t


def kernel(**inputs):
    import concourse.bacc as bacc
    from concourse.bass_utils import run_bass_kernel_spmd

    a = {k: np.asarray(v) for k, v in inputs.items()}
    vec = np.concatenate([
        _cols(a["c"][0]), _cols(a["b_ada"]), _cols(a["ln_g"]), _cols(a["ln_b"]), _cols(a["gla_b_gk"][0]),
        _cols(a["gla_g_norm"][0]), _cols(a["att_b_in"][0]), _cols(a["pool_scale_2"][0]), _cols(a["norm_mix_g_2"][0]),
        _cols(a["norm_ffn_g_2"][0]), _cols(a["conv_b_2"][0]), _cols(a["conv_w_2"][0]), _cols(a["norm_final_g_2"])], 1)
    key, query = np.arange(S)[None, :], P + np.arange(P)[:, None]
    rel = np.clip(query - key, -MAX_REL, MAX_REL) + MAX_REL
    count = np.zeros((P, 4, 16), np.float32)
    for g, w in enumerate(POOL_WINDOWS):
        count[:, g, :] = 1.0 / np.minimum(np.arange(16) + 1, w)
    arrays = {
        "weights": _weights(a), "ada": _ada(a["w_ada"]), "vecs": np.ascontiguousarray(vec),
        "x_in": np.ascontiguousarray(a["x"][0].T.reshape(KT, P, S).transpose(1, 0, 2)),
        "w_gk2": np.ascontiguousarray(a["gla_w_gk2"][0]),
        "rel_bias": np.ascontiguousarray(a["att_rel_bias"][0][:, rel]),
        "pool_w": np.ascontiguousarray(a["pool_w_2"][0].transpose(1, 0, 2)), "rope": _rope_tables(),
        "pool_count": count,
    }
    nc = bacc.Bacc("TRN2", target_bir_lowering=False, num_devices=1)
    args = [nc.dram_tensor(k, v.shape, mybir.dt.from_np(v.dtype), kind="ExternalInput").ap() for k, v in arrays.items()]
    out = nc.dram_tensor("out", (P, KT, S), F32, kind="ExternalOutput").ap()
    build(nc, *args, out)
    r = run_bass_kernel_spmd(nc, [arrays], core_ids=[0])
    return r.results[0]["out"].transpose(1, 0, 2).reshape(D, S).T.reshape(1, S, D)
```
